# Optimizing a Trainium2 kernel written in Bass

```python
import math
import jax, jax.numpy as jnp
from jax import lax
import numpy as np

D_MODEL = 1024
BATCH = 1
SEQ = 512
DEPTH = 1

HEAD_DIM = 64
N_HEADS = D_MODEL // HEAD_DIM
H_A = N_HEADS // 2
H_B = N_HEADS - H_A
G_B = 2
R_B = H_B // G_B
BLK_A = 256
TOPK_A = 3
QC_A = 32
CMP_LEN = 32
CMP_STRIDE = 16
CMP_HIDDEN = 256
SEL_BLK = 64
SEL_TOPK = 16
WINDOW = 512
QC_B = 64
N_BUCKETS = 32
MAX_DIST = 128
FFN_HIDDEN = ((8 * D_MODEL // 3 + 255) // 256) * 256
ADA_CHUNKS = 6
PAD_MULT = 256
W_IN_COLS = 3 * H_A * HEAD_DIM + H_B * HEAD_DIM + 6 * G_B * HEAD_DIM + 3 * H_B
NEG = -1e30
BIG = 1e9
EPS = 1e-6

kernel_name = 'hymba_moba_nsa_t5bias_adaln_swiglu'

def rmsnorm(x, g):
    xf = x.astype(jnp.float32)
    y = xf * lax.rsqrt(jnp.mean(xf * xf, axis=-1, keepdims=True) + EPS)
    return (y * g.astype(jnp.float32)).astype(x.dtype)

def t5_bucket(dist):
    max_exact = N_BUCKETS // 2
    d = jnp.maximum(dist, 0)
    df = jnp.maximum(d, 1).astype(jnp.float32)
    large = max_exact + (jnp.log(df / max_exact) / math.log(MAX_DIST / max_exact)
                         * (N_BUCKETS - max_exact)).astype(jnp.int32)
    large = jnp.minimum(large, N_BUCKETS - 1)
    return jnp.where(d < max_exact, d, large)

def masked_softmax(logits, mask):
    z = jnp.where(mask, logits.astype(jnp.float32), NEG)
    p = jax.nn.softmax(z, axis=-1)
    return jnp.where(mask, p, 0.0)

def moba_attention(q, k, v, tab):
    B, H, Sp, D = q.shape
    nb = Sp // BLK_A
    n_sel = max(1, min(TOPK_A, nb - 1))
    scale = D ** -0.5
    kb = k.reshape(B, H, nb, BLK_A, D)
    vb = v.reshape(B, H, nb, BLK_A, D)
    kmean = jnp.mean(kb.astype(jnp.float32), axis=3)
    bi = jnp.arange(B)[:, None, None, None]
    hi = jnp.arange(H)[None, :, None, None]
    blk_ids = jnp.arange(nb)
    offs = jnp.arange(BLK_A)
    n_chunks = Sp // QC_A
    q_chunks = q.reshape(B, H, n_chunks, QC_A, D).transpose(2, 0, 1, 3, 4)

    def chunk(args):
        ci, qc = args
        pos_q = ci * QC_A + jnp.arange(QC_A)
        own = (ci * QC_A) // BLK_A
        s = jnp.einsum('bhqd,bhnd->bhqn', qc.astype(jnp.float32), kmean)
        s = jnp.where(blk_ids < own, s, -jnp.inf)
        top_s, top_i = lax.top_k(s, n_sel)
        sel_ok = jnp.isfinite(top_s)
        kg = kb[bi, hi, top_i]
        vg = vb[bi, hi, top_i]
        key_pos = top_i[..., None] * BLK_A + offs
        l_sel = jnp.einsum('bhqd,bhqnkd->bhqnk', qc, kg).astype(jnp.float32) * scale
        l_sel = l_sel + tab[hi[..., None], t5_bucket(pos_q[:, None, None] - key_pos)]
        l_sel = l_sel.reshape(B, H, QC_A, n_sel * BLK_A)
        m_sel = jnp.broadcast_to(sel_ok[..., None], (B, H, QC_A, n_sel, BLK_A)).reshape(B, H, QC_A, n_sel * BLK_A)
        k_own = lax.dynamic_slice_in_dim(k, own * BLK_A, BLK_A, axis=2)
        v_own = lax.dynamic_slice_in_dim(v, own * BLK_A, BLK_A, axis=2)
        own_pos = own * BLK_A + offs
        l_own = jnp.einsum('bhqd,bhkd->bhqk', qc, k_own).astype(jnp.float32) * scale
        l_own = l_own + tab[:, t5_bucket(pos_q[:, None] - own_pos[None, :])]
        m_own = jnp.broadcast_to(own_pos[None, :] <= pos_q[:, None], l_own.shape)
        p = masked_softmax(jnp.concatenate([l_sel, l_own], axis=-1),
                           jnp.concatenate([m_sel, m_own], axis=-1)).astype(v.dtype)
        p_sel, p_own = p[..., :n_sel * BLK_A], p[..., n_sel * BLK_A:]
        return (jnp.einsum('bhqk,bhqkd->bhqd', p_sel, vg.reshape(B, H, QC_A, n_sel * BLK_A, D))
                + jnp.einsum('bhqk,bhkd->bhqd', p_own, v_own))

    out = lax.map(chunk, (jnp.arange(n_chunks), q_chunks))
    return out.transpose(1, 0, 3, 2, 4).reshape(B, Sp, H * D)

def compress(kv, pe, w1, w2):
    B, G, Sp, D = kv.shape
    n_cmp = (Sp - CMP_LEN) // CMP_STRIDE + 1
    idx = jnp.arange(n_cmp)[:, None] * CMP_STRIDE + jnp.arange(CMP_LEN)[None, :]
    blocks = kv[:, :, idx] + pe
    hid = jax.nn.gelu(blocks.reshape(B, G, n_cmp, CMP_LEN * D) @ w1)
    return hid @ w2

def nsa_attention(q, k_cmp, v_cmp, k_sel, v_sel, k_win, v_win, gates, tab):
    B, G, R, Sp, D = q.shape
    scale = D ** -0.5
    n_cmp = k_cmp.shape[2]
    nb = Sp // SEL_BLK
    n_sel = min(SEL_TOPK, nb)
    cmp_end = jnp.arange(n_cmp) * CMP_STRIDE + CMP_LEN - 1
    cs = jnp.arange(n_cmp)[:, None] * CMP_STRIDE
    ss = jnp.arange(nb)[None, :] * SEL_BLK
    overlap = ((cs < ss + SEL_BLK) & (cs + CMP_LEN > ss)).astype(jnp.float32)
    ksb = k_sel.reshape(B, G, nb, SEL_BLK, D)
    vsb = v_sel.reshape(B, G, nb, SEL_BLK, D)
    k_win_p = jnp.pad(k_win, ((0, 0), (0, 0), (WINDOW, 0), (0, 0)))
    v_win_p = jnp.pad(v_win, ((0, 0), (0, 0), (WINDOW, 0), (0, 0)))
    bi = jnp.arange(B)[:, None, None, None]
    gi = jnp.arange(G)[None, :, None, None]
    hb = jnp.arange(H_B).reshape(1, G, R, 1, 1)
    blk_ids = jnp.arange(nb)
    offs = jnp.arange(SEL_BLK)
    win_offs = jnp.arange(WINDOW + QC_B)
    n_chunks = Sp // QC_B
    q_chunks = q.reshape(B, G, R, n_chunks, QC_B, D).transpose(3, 0, 1, 2, 4, 5)
    g_chunks = gates.reshape(B, G, R, n_chunks, QC_B, 3).transpose(3, 0, 1, 2, 4, 5)

    def chunk(args):
        ci, qc, gc = args
        pos_q = ci * QC_B + jnp.arange(QC_B)
        l_c = jnp.einsum('bgrqd,bgnd->bgrqn', qc, k_cmp).astype(jnp.float32) * scale
        p_c = masked_softmax(l_c, cmp_end[None, :] <= pos_q[:, None])
        o_c = jnp.einsum('bgrqn,bgnd->bgrqd', p_c.astype(v_cmp.dtype), v_cmp)
        imp = jnp.einsum('bgrqn,nj->bgqj', p_c, overlap)
        cur = pos_q // SEL_BLK
        ok = blk_ids[None, :] <= cur[:, None]
        forced = (blk_ids[None, :] == 0) | (blk_ids[None, :] == cur[:, None]) | (blk_ids[None, :] == cur[:, None] - 1)
        score = jnp.where(ok, jnp.where(forced, BIG, imp), -jnp.inf)
        top_s, top_i = lax.top_k(score, n_sel)
        sel_ok = jnp.isfinite(top_s)
        kg = ksb[bi, gi, top_i]
        vg = vsb[bi, gi, top_i]
        n_keys = n_sel * SEL_BLK
        key_pos = (top_i[..., None] * SEL_BLK + offs).reshape(B, G, QC_B, n_keys)
        l_s = jnp.einsum('bgrqd,bgqnkd->bgrqnk', qc, kg).reshape(B, G, R, QC_B, n_keys).astype(jnp.float32) * scale
        l_s = l_s + tab[hb, t5_bucket(pos_q[:, None] - key_pos)[:, :, None]]
        m_s = ((key_pos <= pos_q[:, None]) & jnp.repeat(sel_ok, SEL_BLK, axis=-1))[:, :, None]
        p_s = masked_softmax(l_s, m_s).astype(v_sel.dtype)
        o_s = jnp.einsum('bgrqk,bgqkd->bgrqd', p_s, vg.reshape(B, G, QC_B, n_keys, D))
        kw = lax.dynamic_slice_in_dim(k_win_p, ci * QC_B, WINDOW + QC_B, axis=2)
        vw = lax.dynamic_slice_in_dim(v_win_p, ci * QC_B, WINDOW + QC_B, axis=2)
        w_pos = ci * QC_B - WINDOW + win_offs
        dist = pos_q[:, None] - w_pos[None, :]
        m_w = (dist >= 0) & (dist < WINDOW) & (w_pos[None, :] >= 0)
        l_w = jnp.einsum('bgrqd,bgkd->bgrqk', qc, kw).astype(jnp.float32) * scale
        l_w = l_w + tab[:, t5_bucket(dist)].reshape(G, R, QC_B, WINDOW + QC_B)
        p_w = masked_softmax(l_w, m_w).astype(v_win.dtype)
        o_w = jnp.einsum('bgrqk,bgkd->bgrqd', p_w, vw)
        return gc[..., 0:1] * o_c + gc[..., 1:2] * o_s + gc[..., 2:3] * o_w

    out = lax.map(chunk, (jnp.arange(n_chunks), q_chunks, g_chunks))
    return out.transpose(1, 0, 4, 2, 3, 5).reshape(B, Sp, G * R * D)

def setup_inputs(seed: int = 0) -> dict:
    key = jax.random.key(seed)
    ks = jax.random.split(key, 24)
    L, D, DH = DEPTH, D_MODEL, HEAD_DIM

    def nrm(k, shape, s):
        return jax.random.normal(k, shape, jnp.float32) * s

    def gain(k, shape):
        return 1.0 + 0.05 * jax.random.normal(k, shape, jnp.float32)

    return {
        'x': nrm(ks[0], (BATCH, SEQ, D), 1.0),
        'c': nrm(ks[1], (BATCH, D), 1.0),
        'rel_bias': nrm(ks[2], (N_BUCKETS, N_HEADS), 0.5),
        'w_ada': nrm(ks[3], (L, D, ADA_CHUNKS * D), 0.5 * D ** -0.5),
        'b_ada': nrm(ks[4], (L, ADA_CHUNKS * D), 0.01),
        'g_mix': gain(ks[5], (L, D)),
        'w_in': nrm(ks[6], (L, D, W_IN_COLS), D ** -0.5),
        'q_norm_a': gain(ks[7], (L, DH)),
        'k_norm_a': gain(ks[8], (L, DH)),
        'q_norm_b': gain(ks[9], (L, DH)),
        'k_norm_cmp': gain(ks[10], (L, DH)),
        'k_norm_sel': gain(ks[11], (L, DH)),
        'k_norm_win': gain(ks[12], (L, DH)),
        'cmp_pe_k': nrm(ks[13], (L, CMP_LEN, DH), 0.5),
        'cmp_w1_k': nrm(ks[14], (L, CMP_LEN * DH, CMP_HIDDEN), (CMP_LEN * DH) ** -0.5),
        'cmp_w2_k': nrm(ks[15], (L, CMP_HIDDEN, DH), CMP_HIDDEN ** -0.5),
        'cmp_pe_v': nrm(ks[16], (L, CMP_LEN, DH), 0.5),
        'cmp_w1_v': nrm(ks[17], (L, CMP_LEN * DH, CMP_HIDDEN), (CMP_LEN * DH) ** -0.5),
        'cmp_w2_v': nrm(ks[18], (L, CMP_HIDDEN, DH), CMP_HIDDEN ** -0.5),
        'w_out': nrm(ks[19], (L, D, D), D ** -0.5),
        'g_ffn': gain(ks[20], (L, D)),
        'w_gu': nrm(ks[21], (L, D, 2 * FFN_HIDDEN), D ** -0.5),
        'w_down': nrm(ks[22], (L, FFN_HIDDEN, D), FFN_HIDDEN ** -0.5),
    }

def reference(x, c, rel_bias, w_ada, b_ada, g_mix, w_in, q_norm_a, k_norm_a, q_norm_b,
              k_norm_cmp, k_norm_sel, k_norm_win, cmp_pe_k, cmp_w1_k, cmp_w2_k,
              cmp_pe_v, cmp_w1_v, cmp_w2_v, w_out, g_ffn, w_gu, w_down):
    B, S, D = x.shape
    DH = HEAD_DIM
    Sp = -(-S // PAD_MULT) * PAD_MULT
    tab = rel_bias.T
    tab_a, tab_b = tab[:H_A], tab[H_A:]
    sizes = [H_A * DH] * 3 + [H_B * DH] + [G_B * DH] * 6 + [3 * H_B]
    split_at = [int(v) for v in np.cumsum(sizes)[:-1]]

    def heads_a(t):
        return t.reshape(B, Sp, H_A, DH).transpose(0, 2, 1, 3)

    def kv_heads(t):
        return t.reshape(B, Sp, G_B, DH).transpose(0, 2, 1, 3)

    for l in range(DEPTH):
        mod = jax.nn.silu(c) @ w_ada[l] + b_ada[l]
        sh_m, sc_m, gt_m, sh_f, sc_f, gt_f = jnp.split(mod, ADA_CHUNKS, axis=-1)
        h = rmsnorm(x, g_mix[l]) * (1.0 + sc_m[:, None]) + sh_m[:, None]
        h = jnp.pad(h, ((0, 0), (0, Sp - S), (0, 0)))
        proj = h @ w_in[l]
        qa, ka, va, qb, kc, vc, ksl, vsl, kwn, vwn, gl = jnp.split(proj, split_at, axis=-1)
        qa = rmsnorm(heads_a(qa), q_norm_a[l])
        ka = rmsnorm(heads_a(ka), k_norm_a[l])
        o_a = moba_attention(qa, ka, heads_a(va), tab_a)
        qb = rmsnorm(qb.reshape(B, Sp, G_B, R_B, DH).transpose(0, 2, 3, 1, 4), q_norm_b[l])
        k_cmp = rmsnorm(compress(kv_heads(kc), cmp_pe_k[l], cmp_w1_k[l], cmp_w2_k[l]), k_norm_cmp[l])
        v_cmp = compress(kv_heads(vc), cmp_pe_v[l], cmp_w1_v[l], cmp_w2_v[l])
        k_s = rmsnorm(kv_heads(ksl), k_norm_sel[l])
        k_w = rmsnorm(kv_heads(kwn), k_norm_win[l])
        gates = jax.nn.sigmoid(gl.reshape(B, Sp, G_B, R_B, 3).transpose(0, 2, 3, 1, 4))
        o_b = nsa_attention(qb, k_cmp, v_cmp, k_s, kv_heads(vsl), k_w, kv_heads(vwn), gates, tab_b)
        mix = jnp.concatenate([o_a, o_b], axis=-1)[:, :S]
        x = x + gt_m[:, None] * (mix @ w_out[l])
        h = rmsnorm(x, g_ffn[l]) * (1.0 + sc_f[:, None]) + sh_f[:, None]
        gate, up = jnp.split(h @ w_gu[l], 2, axis=-1)
        x = x + gt_f[:, None] * ((jax.nn.silu(gate) * up) @ w_down[l])
    return x


_drawn_inputs = setup_inputs


def setup_inputs(seed=0):
    import zlib

    import numpy as np

    out = dict(_drawn_inputs(seed))
    spreads = {}
    factors = {'rel_bias': 3.057,
     'b_ada': 5.937,
     'g_mix': 8.0,
     'q_norm_a': 8.0,
     'k_norm_a': 8.0,
     'q_norm_b': 8.0,
     'k_norm_cmp': 8.0,
     'k_norm_sel': 8.0,
     'k_norm_win': 8.0,
     'cmp_pe_k': 8.0,
     'cmp_w1_k': 3.113,
     'cmp_w2_k': 2.994,
     'g_ffn': 3.941}
    for name, (base, spread) in spreads.items():
        noise = np.random.default_rng([zlib.crc32(name.encode()), seed]).standard_normal(out[name].shape)
        drawn = base * np.exp(spread * noise) if base else spread * noise
        out[name] = __import__('jax').numpy.asarray(drawn.astype(out[name].dtype))
    for name, factor in factors.items():
        out[name] = (out[name] * factor).astype(out[name].dtype)
    return out
```

```python
import math
from contextlib import ExitStack

import numpy as np
import concourse.bass as bass
from concourse import mybir

F32 = mybir.dt.float32
F32R = mybir.dt.float32r
ALU = mybir.AluOpType
ACT = mybir.ActivationFunctionType
AXX = mybir.AxisListType.X

P = 128
SEQ, D = 512, 1024
T = SEQ // P
KD = D // P
DH = 64
FFN = 2816
NF = FFN // P
NB_, MAX_DIST = 32, 128
EPS = 1e-6
NEG = -1e30
SCALE = DH ** -0.5
CL, CS = 32, 16
NCMP = (SEQ - CL) // CS + 1
NC = 32
U = 1024

W_T, W_QB, W_KV, W_QA, W_KA, W_VA = 0, 2, 6, 10, 14, 18
W_OUT, W_GU, W_DN = 22, 30, 30 + 2 * NF
N_W = W_DN + NF
N_EARLY = 16

C_C, C_BM, C_GM, C_GF, C_BF, C_GAIN, C_PE = 0, 8, 24, 32, 40, 64, 70
N_COLS = C_PE + 2 * CL // 2
G_QB, G_KSL, G_KWN, G_QA, G_KA, G_KCMP = range(6)
S_ID, S_ONE, S_MASK, S_VALID = 0, 128, 256, 384
BV = 640


def view(ap, dims, off=0):
    return bass.AP(ap.tensor, ap.offset + off, [list(ap.ap[0])] + dims)


def layer(nc, wst, ada_e, ada_l, xd, cols, shc, oneh, rel, brow, wgl, w1, w2, out):
    bvd = nc.dram_tensor("bias_by_distance", (16, BV), F32, kind="Internal").ap()
    x_v = xd.rearrange("b (t p) d -> p (b t) d", p=P)
    out_v = out.rearrange("b (t p) d -> p (b t) d", p=P)

    with ExitStack() as top:
        def sb(name, shape, dt=F32, ctx=top):
            return ctx.enter_context(nc.sbuf_tensor(name, shape, dt))

        def sem(name):
            return top.enter_context(nc.semaphore(name))

        ps = [top.enter_context(nc.psum_tensor(f"ps{i}", [P, 512], F32)) for i in range(8)]

        par = sb("par", [P, N_COLS])
        shp = sb("shp", [P, 388])
        ident, ones = shp[:, S_ID:S_ID + P], shp[:, S_ONE:S_ONE + P]
        eps = sb("eps", [P, 1])
        silc = sb("silc", [P, KD])
        xss = sb("xss", [P, 2 * T])
        xst = sb("xst", [P, T])
        xrs = sb("xrs", [P, T])
        modm = sb("modm", [P, KD, 2])
        am = sb("am", [P, KD])
        modf = sb("modf", [P, 3 * KD])
        modfb = sb("modfb", [P, 3 * KD])
        af = sb("af", [P, KD])
        gq = sb("gq", [P, 2])
        gtm = sb("gtm", [P, D])
        G = sb("G", [P, 24, T])
        raw = sb("raw", [P, 4, U])
        whi = sb("whi", [P, 4, U], F32R)
        wlo = sb("wlo", [P, 4, U], F32R)
        mhi, mlo = (sb(n, [P, KD, SEQ], F32R) for n in ("mhi", "mlo"))
        h1hi, h1lo = mhi, mlo

        ca = ExitStack()
        QT = sb("QT", [P, 8, SEQ], F32, ca)
        KT = sb("KT", [P, 6, SEQ], F32, ca)
        VA = sb("VA", [P, T, 512], F32, ca)
        VB = sb("VB", [P, T, 256], F32, ca)
        brow_s = VA[0:1, 0:2, :].rearrange("p o n -> p (o n)")
        acc = [QT[:, j, :] for j in range(4)] + [KT[:, j, :] for j in range(4)]
        with ExitStack() as c:
            x0 = sb("x0", [P, T, D], F32, c)
            xn = sb("xn", [P, T, D], F32, c)
        with ExitStack() as c:
            nat = sb("nat", [P, 2, T, 512], F32, c)
            w1s = sb("w1s", [P, CL // 2, 256], F32, c)
        mix = sb("mix", [P, T, D], F32, ca)
        L = sb("L", [P, 4, SEQ], F32, ca)
        PTs = sb("PTs", [P, 4, SEQ], F32, ca)
        with ExitStack() as c:
            ring2 = sb("ring2", [P, 4, U], F32, c)
            sq = sb("sq", [P, 2, 512], F32, c)
            R = sb("R", [P, 2, CL // 2, 2, NC], F32, c)
            ssb = sb("ssb", [P, 4, 32], F32, c)
            stb = sb("stb", [P, 4, 32], F32, c)
            rsb = sb("rsb", [P, 4, 32], F32, c)
            glr = sb("glr", [P, KD, 24], F32, c)
            glh = sb("glh", [P, KD, 24], F32R, c)
            gll = sb("gll", [P, KD, 24], F32R, c)
            w2s = sb("w2s", [P, 2, 2, DH], F32, c)
            hidk = sb("hidk", [P, 2, 2 * NC], F32, c)
            hidv = sb("hidv", [P, 2, 2, T, NC], F32, c)
            kcn = sb("kcn", [NC, 2, DH], F32, c)
            kcq = sb("kcq", [NC, 2, DH], F32, c)
            kcs = sb("kcs", [NC, 3, 2], F32, c)
            kcT = sb("kcT", [P, NC], F32, c)
            Vbd = sb("Vbd", [P, 2, T, DH], F32, c)
            gv = sb("gv", [P, 8, T], F32, c)
            cst = sb("cst", [P, 4, 32], F32, c)
            rel_s = sb("rel_s", [33, 16], F32, c)
            with ExitStack() as c2:
                oneh_s = sb("oneh_s", [33, BV], F32, c2)
                bvs = sb("bvs", [16, BV], F32, c2)
            with ExitStack() as c2:
                hf = sb("hf", [P, 2, SEQ], F32, c2)
            with ExitStack() as c2:
                kcE = sb("kcE", [P, 2, 2, 256], F32, c2)
                Kst = sb("Kst", [P, 2, 2, 256], F32, c2)
            with ExitStack() as c2:
                cm = sb("cm", [P, 32, NC], F32, c2)
                PcT = sb("PcT", [P, 8, P], F32, c2)
        with ExitStack() as c:
            qs = sb("qs", [P, SEQ], F32, c)
            ks = sb("ks", [P, SEQ], F32, c)
            bias = sb("bias", [P, 2, SEQ], F32, c)
            tmpo = sb("tmpo", [P, 2, T, DH], F32, c)
            nmx = sb("nmx", [P, 8], F32, c)
            sums = sb("sums", [P, 8], F32, c)
            rec = sb("rec", [P, 2, T], F32, c)
            recg = sb("recg", [P, 2, T], F32, c)
        ca.close()
        x1 = sb("x1", [P, T, D])
        ob = sb("ob", [P, 2, 512])
        hf2 = sb("hf2", [P, 2, SEQ])
        with ExitStack() as c:
            xn2 = sb("xn2", [P, T, D], F32, c)
        with ExitStack() as c:
            sil = sb("sil", [P, 2, SEQ], F32, c)
            actf = sb("actf", [P, 2, SEQ], F32, c)
            ahi, alo = (sb(n, [P, NF, SEQ], F32R, c) for n in ("ahi", "alo"))
        with ExitStack() as c:
            yT = sb("yT", [P, KD, SEQ], F32, c)
            yo = sb("yo", [P, T, D], F32, c)

        s_par, s_shp, s_x, s_rel, s_gl, s_w2, s_w1, s_brow = map(
            sem, "par_in shp_in x_in rel_in gl_in w2_in w1_in brow_in".split())
        s_raw = [sem(f"raw{i}_in") for i in range(4)]
        s_r2 = [sem(f"ring2_{i}_in") for i in range(4)]
        s_eps, s_silc, s_xss, s_xst, s_xrs, s_xn = map(
            sem, "eps_set silc_done xss_done xst_done xrs_done xn_done".split())
        s_bvp, s_bvs, s_bvd = map(
            sem, "bv_psum bv_sbuf bv_dram".split())
        s_adamm, s_mod, s_htp, s_hf, s_hhi, s_hlo = map(
            sem, "ada_mm mod_done hT_psum hf_done h_hi h_lo".split())
        s_hi, s_lo, s_mm = map(sem, "w_hi w_lo w_used".split())
        s_kvE, s_kst, s_Rz, s_R = map(sem, "kvT_evac kst_in R_zero R_built".split())
        s_pj, s_ev, s_ssr, s_std, s_nrm = map(
            sem, "proj_psum proj_evac ss_done std_done nat_normed".split())
        s_ach = sem("acc_added")
        s_hid, s_gelu, s_kcp, s_kce, s_kcr, s_kcst, s_kcn, s_kctp, s_kcT = map(
            sem, "hid_psum gelu_done kc_psum kc_evac kc_ss kc_std kc_normed kcT_psum kcT_evac".split())
        s_glh, s_gll, s_glp, s_sig, s_gq = map(sem, "gl_hi gl_lo gl_psum gates_done gq_done".split())
        s_csc, s_cm, s_cex, s_cpt, s_cpte, s_pvc, s_mixc = map(
            sem, "cs_psum cm_done c_exp pcT_psum pcT_evac pvc_psum mixc_done".split())
        s_tp, s_tpev, s_vz = map(sem, "tp_psum tp_evac vbd_zero".split())
        s_dch, s_begun = map(sem, "dve_chain begun".split())
        s_stg = [sem(f"staged{a}") for a in range(2)]
        s_S, s_L, s_E, s_T, s_PV, s_Ca, s_Cd, s_N, s_add, s_nch = map(
            sem, "S_psum logits exp_done PT_psum PV_psum PTa PTd normed added n_chain".split())
        s_mtp, s_mhi, s_mlo, s_op, s_ot, s_x1, s_x1in, s_x1sq, s_h2lo = map(
            sem, "mixT_psum m_hi m_lo out_psum out_gated x1_done x1_in x1_sq h2_lo".split())
        s_sil, s_prod, s_ahi, s_alo, s_dn, s_yT, s_ytp, s_yo, s_out = map(
            sem, "silu_done prod_done a_hi a_lo dn_psum yT_done y_psum yo_done out_done".split())
        s_h2tp, s_hf2, s_h2hi, s_xn2, s_x2ss, s_x2st, s_modf = map(
            sem, "h2_psum hf2_done h2_hi xn2_done x2_ss x2_std modf_done".split())

        block = top.enter_context(nc.Block())

        TP = ([("q", 4 + i) for i in range(4)] + [("gtm", 0), ("kb", 4), ("kb", 5), ("gtm", 1), ("col", 2)]
              + [("col", 3), ("col", 4)] + [("q", i) for i in range(4)] + [("vcmp", 0)]
              + [("col", 5), ("col", 6), ("col", 7)] + [("k", i) for i in range(4)])
        N_A = 4
        SLOT = [(w % 4) for w in range(N_W)]

        def raw_count(w):
            return 16 * (N_EARLY // 4 + w // 4 + 1)

        @block.sync
        def _(sp):
            sp.dma_start(par[:, :], cols).then_inc(s_par, 16)
            sp.dma_start(shp[:, :], shc).then_inc(s_shp, 16)
            sp.dma_start(x0[:, :, :], x_v).then_inc(s_x, 16)
            sp.dma_start(rel_s[0:32, :], rel).then_inc(s_rel, 16)
            sp.dma_start(rel_s[32:33, :], shc[0:1, S_ONE:S_ONE + 16]).then_inc(s_rel, 16)
            sp.dma_start(oneh_s[:, :], oneh).then_inc(s_rel, 16)
            for e in range(N_EARLY):
                if e >= 4:
                    sp.wait_ge(s_adamm, e - 3)
                sp.dma_start(raw[:, e % 4, :], ada_e[e]).then_inc(s_raw[e % 4], 16)
            sp.dma_start(brow_s, brow).then_inc(s_brow, 16)
            sp.dma_start(glr[:, :, :], wgl).then_inc(s_gl, 16)
            sp.dma_start(w2s[:, :, :, :], w2).then_inc(s_w2, 16)

            def late(k):
                if k >= 4:
                    sp.wait_ge(s_ach, 2 * (k - 3))
                sp.dma_start(ring2[:, k % 4, :], ada_l[k]).then_inc(s_r2[k % 4], 16)

            def weights(w):
                if w < 4:
                    sp.wait_ge(s_adamm, N_EARLY - 3 + w)
                else:
                    sp.wait_ge(s_lo, w - 3)
                sp.dma_start(raw[:, SLOT[w], :], wst[w]).then_inc(s_raw[SLOT[w]], 16)

            for w in range(W_OUT):
                weights(w)
                if w == 4:
                    sp.wait_ge(s_hlo, KD)
                    sp.dma_start(w1s[:, :, :], w1[0]).then_inc(s_w1, 16)
                if w == 11:
                    sp.wait_ge(s_hid, 1)
                    sp.dma_start(w1s[:, :, :], w1[1]).then_inc(s_w1, 16)
                if 4 <= w < 20:
                    late(2 * (w - 4))
                    late(2 * (w - 4) + 1)
            for w in range(W_OUT, W_OUT + 4):
                weights(w)

            def stage(u, a, qi, ki):
                if u is not None:
                    sp.wait_ge(s_L, 8 * u + 4 * a)
                h = slice(64 * a, 64 * a + 64)
                sp.dma_start(qs[h, :], QT[h, bass.ds(qi, 1), :].rearrange("p o n -> p (o n)")).then_inc(s_stg[a], 16)
                sp.dma_start(ks[h, :], KT[h, bass.ds(ki, 1), :].rearrange("p o n -> p (o n)")).then_inc(s_stg[a], 16)
                sp.dma_start(bias[:, a, :], bass.AP(bvd.tensor, qi * (2 * BV) + a * BV, [[1, P], [1, SEQ]])
                             ).then_inc(s_stg[a], 16)

            sp.wait_ge(s_tpev, len(TP))
            sp.wait_ge(s_mixc, 4)
            sp.wait_ge(s_bvd, 16)
            for a in range(2):
                stage(None, a, 0, 0)
            with sp.Fori(1, N_A) as i:
                for a in range(2):
                    stage(i, a, i, i)
            with sp.Fori(0, 4) as i:
                for br in range(2):
                    for a in range(2):
                        stage(2 * i + N_A + br, a, i + 4, 4 + br)
            sp.wait_ge(s_S, 8 * (N_A + 8))
            sp.wait_ge(s_stg[0], 48 * (N_A + 8))
            sp.wait_ge(s_stg[1], 48 * (N_A + 8))
            sp.dma_start(x1[:, :, :], x_v).then_inc(s_x1in, 16)
            for w in range(W_OUT + 4, W_GU):
                weights(w)
            with sp.Fori(0, (N_W - W_GU) // 4) as i:
                for r in range(4):
                    sp.wait_ge(s_lo, 4 * i + (W_GU + r - 3))
                    s = SLOT[W_GU + r]
                    sp.dma_start(raw[:, s, :], wst[bass.ds(4 * i + (W_GU + r), 1)].rearrange("o p n -> p (o n)")
                                 ).then_inc(s_raw[s], 16)
            for w in range(W_GU + (N_W - W_GU) // 4 * 4, N_W):
                weights(w)
            for t in range(T):
                sp.wait_ge(s_yo, 2 * (t + 1))
                sp.dma_start(out_v[:, t, :], yo[:, t, :]).then_inc(s_out, 16)
            sp.wait_ge(s_out, 16 * T)

        @block.gpsimd
        def _(pool):
            nc.gpsimd.memset(eps[:, :], EPS).then_inc(s_eps, 1)
            nc.gpsimd.memset(R[:, :, :, :, :], 0.0).then_inc(s_Rz, 1)
            nc.gpsimd.memset(Vbd[:, :, :, :], 0.0).then_inc(s_vz, 1)

            def low(w, slot):
                pool.wait_ge(s_hi, w + 1)
                nc.gpsimd.tensor_tensor(wlo[:, slot, :], raw[:, slot, :], whi[:, slot, :].bitcast(F32),
                                        ALU.subtract).then_inc(s_lo, 1)

            for w in range(W_KV):
                low(w, SLOT[w])
            pool.wait_ge(s_kst, 128)
            pool.wait_ge(s_Rz, 1)
            pool.wait_ge(s_par, 16)
            for kv in range(2):
                for g in range(2):
                    win = view(Kst[:, kv, g, :], [[1, CL // 2], [CS // 2, NCMP]])
                    pe_ = view(par[:, C_PE + 16 * kv:C_PE + 16 * kv + 16], [[1, CL // 2], [0, NCMP]])
                    nc.gpsimd.tensor_tensor(R[:, kv, :, g, 0:NCMP], win, pe_, ALU.add).then_inc(s_R, 1)
            for w in range(W_KV, W_OUT + 4):
                low(w, SLOT[w])

            def add(u, qi, a):
                pool.wait_ge(s_N, 2 * u + a + 3)
                pool.sem_inc(s_begun)
                m = mix[:, :, bass.ds(128 * qi + 64 * a, 64)]
                nc.gpsimd.tensor_tensor(m, tmpo[:, a, :, :], m, ALU.add).then_inc(s_add, 1)

            with pool.Fori(0, 4) as i:
                for br in range(2):
                    for a in range(2):
                        if br == 1:
                            pool.wait_ge(s_add, 4 * i + a + 3)
                        add(2 * i + N_A + br, i + 4, a)

            with pool.Fori(0, (N_W - W_OUT - 4) // 4) as i:
                for r in range(4):
                    low(4 * i + (W_OUT + 4 + r), SLOT[W_OUT + 4 + r])
            for w in range(W_OUT + 4 + (N_W - W_OUT - 4) // 4 * 4, N_W):
                low(w, SLOT[w])

        @block.scalar
        def _(act):
            act.wait_ge(s_par, 16)
            nc.scalar.activation(silc[:, :], par[:, C_C:C_C + KD], ACT.Silu).then_inc(s_silc, 1)
            act.wait_ge(s_x, 16)
            for t in range(T):
                nc.scalar.activation(xn[:, t, :], x0[:, t, :], ACT.Square,
                                     accum_out=xss[:, t:t + 1]).then_inc(s_xss, 1)
            act.wait_ge(s_eps, 1)
            act.wait_ge(s_xss, T)
            nc.scalar.activation(xst[:, :], xss[:, 0:T], ACT.Sqrt, bias=eps[:, :], scale=1.0 / D).then_inc(s_xst, 1)
            act.wait_ge(s_bvp, 1)
            nc.scalar.activation(bvs[:, 0:512], ps[6][0:16, 0:512], ACT.Copy).then_inc(s_bvs, 1)
            nc.scalar.activation(bvs[:, 512:BV], ps[7][0:16, 0:BV - 512], ACT.Copy).then_inc(s_bvs, 1)
            act.wait_ge(s_bvs, 2)
            act.dma_start(bvd, bvs[:, :]).then_inc(s_bvd, 16)
            act.wait_ge(s_bvd, 16)

            def h_chunk(kk, hbuf, a_col, s_col, tp, hfs, lo_s, n_lo, banks):
                act.wait_ge(tp, kk + 1)
                if kk >= 2:
                    act.wait_ge(lo_s, n_lo + kk - 1)
                nc.scalar.activation(hbuf[:, kk % 2, :], banks[kk % 2][:, :], ACT.Identity,
                                     bias=s_col, scale=a_col).then_inc(hfs, 1)

            for kk in range(KD):
                act.wait_ge(s_mod, kk + 1)
                h_chunk(kk, hf, am[:, kk:kk + 1], modm[:, kk, 1:2], s_htp, s_hf, s_hlo, 0, ps[4:6])

            def high(w, slot, landed):
                act.wait_ge(s_raw[slot], landed)
                nc.scalar.activation(whi[:, slot, :], raw[:, slot, :], ACT.Copy).then_inc(s_hi, 1)

            def high_w(w):
                if w >= 4:
                    act.wait_ge(s_mm, w - 3)
                high(w, SLOT[w], raw_count(w))

            for w in range(4):
                high_w(w)
            act.wait_ge(s_gl, 16)
            nc.scalar.activation(glh[:, :, :], glr[:, :, :], ACT.Copy).then_inc(s_glh, 1)

            high_w(4)
            act.wait_ge(s_mm, W_QB)
            act.wait_ge(s_hlo, KD)
            for kv in range(2):
                nc.scalar.activation(kcE[:, kv, :, :], ps[4 + kv][:, :].rearrange("p (m r) -> p r m", r=2),
                                     ACT.Copy).then_inc(s_kvE, 1)
            act.wait_ge(s_kvE, 2)
            for g in range(2):
                for r in range(2):
                    act.dma_start(Kst[64 * r:64 * r + 64, :, g, :], kcE[64 * g:64 * g + 64, :, r, :]
                                  ).then_inc(s_kst, 32)
            high_w(5)

            def evac(blk, t):
                if t < T - 1:
                    act.wait_ge(s_pj, 3 * blk + t + 1)
                else:
                    act.wait_ge(s_mm, W_QB + 4 * blk + 4)

            def square(q, src, width):
                if q >= 2:
                    act.wait_ge(s_ssr, q - 1)
                return nc.scalar.activation(sq[:, q % 2, 0:width], src, ACT.Square)

            def normed_block(blk, b, width, v_dst):
                if b >= 2:
                    act.wait_ge(s_tp, {2: 4, 3: 7}[b])
                for t in range(T):
                    evac(blk, t)
                    nc.scalar.activation(nat[:, b % 2, t, 0:width], ps[t][:, 0:width], ACT.Copy)
                    if v_dst is not None:
                        nc.scalar.activation(v_dst[:, t, :], ps[t][:, width:512], ACT.Copy)
                    square(4 * b + t, ps[t][:, 0:width], width).then_inc(s_ev, 1)
                h = width // DH
                act.wait_ge(s_ssr, 4 * b + 4)
                nc.scalar.activation(stb[:, b, 0:T * h], ssb[:, b, 0:T * h], ACT.Sqrt, bias=eps[:, :],
                                     scale=1.0 / DH).then_inc(s_std, 1)

            def evac_tp(n):
                kind, j = TP[n]
                bank = ps[4 + n % 2]
                act.wait_ge(s_tp, n + 1)
                if kind == "q":
                    g = gq[:, 0:1] if j >= 4 else gq[:, 1:2]
                    i = nc.scalar.activation(QT[:, j, :], bank[:, :], ACT.Copy, scale=g)
                elif kind in ("k", "kb"):
                    gi = C_GAIN + (G_KA if kind == "k" else G_KSL + j - 4)
                    i = nc.scalar.activation(KT[:, j, :], bank[:, :], ACT.Copy, scale=par[:, gi:gi + 1])
                elif kind == "gtm":
                    i = nc.scalar.activation(gtm[:, 512 * j:512 * j + 512], bank[:, :], ACT.Copy)
                elif kind == "col":
                    i = nc.scalar.activation(modf[:, 4 * (j - 2):4 * (j - 2) + 4], bank[:, 0:4], ACT.Copy)
                else:
                    act.wait_ge(s_vz, 1)
                    for t in range(T):
                        r = slice(32 * t, 32 * t + 32)
                        i = nc.scalar.activation(Vbd[r, :, t, :], bank[r, 0:128].rearrange("p (g d) -> p g d", g=2),
                                                 ACT.Copy)
                i.then_inc(s_tpev, 1)

            for w in (6, 7, 8):
                high_w(w)
            normed_block(0, 0, 512, None)
            high_w(9)
            act.wait_ge(s_hid, 1)
            nc.scalar.activation(hidk[:, :, :], ps[6][:, 0:128].rearrange("p (h n) -> p h n", h=2),
                                 ACT.Gelu_apprx_tanh).then_inc(s_gelu, 1)
            for w in (10, 11, 12):
                high_w(w)
            normed_block(1, 1, 256, VB)
            high_w(13)
            act.wait_ge(s_gq, 1)
            for n in range(5):
                evac_tp(n)
            act.wait_ge(s_kcp, 1)
            kc_ps = ps[7][0:NC, 0:128].rearrange("p (g d) -> p g d", g=2)
            nc.scalar.activation(kcn[:, :, :], kc_ps, ACT.Copy)
            nc.scalar.activation(kcq[:, :, :], kc_ps, ACT.Square).then_inc(s_kce, 1)
            act.wait_ge(s_kcr, 1)
            nc.scalar.activation(kcs[:, 1, :], kcs[:, 0, :], ACT.Sqrt, bias=eps[0:NC, :], scale=1.0 / DH
                                 ).then_inc(s_kcst, 1)
            act.wait_ge(s_glp, 1)
            nc.scalar.activation(G[:, :, :], ps[6][:, 0:96].rearrange("p (t c) -> p c t", t=T),
                                 ACT.Sigmoid).then_inc(s_sig, 1)
            for w in (14, 15, 16):
                high_w(w)
            normed_block(2, 2, 512, None)
            high_w(17)
            for n in range(5, 9):
                evac_tp(n)
            act.wait_ge(s_kctp, 1)
            nc.scalar.activation(kcT[:, :], ps[7][:, 256:288], ACT.Copy,
                                 scale=par[:, C_GAIN + G_KCMP:C_GAIN + G_KCMP + 1]).then_inc(s_kcT, 1)
            act.wait_ge(s_hid, 2)
            nc.scalar.activation(hidv[:, :, :, :, :].rearrange("p h g t n -> p (h g) t n"),
                                 view(ps[6][:, 0:128], [[NC, 4], [0, T], [1, NC]]),
                                 ACT.Gelu_apprx_tanh).then_inc(s_gelu, 1)
            for w in (18, 19, 20):
                high_w(w)
            act.wait_ge(s_cm, 1)
            nc.scalar.activation(cm[:, :, :], cm[:, :, :], ACT.Exp).then_inc(s_cex, 1)
            normed_block(3, 3, 512, None)
            high_w(21)
            for n in range(9, 16):
                evac_tp(n)
            for w in (22, 23, 24):
                high_w(w)
            for t in range(T):
                evac(4, t)
                nc.scalar.activation(VA[:, t, :], ps[t][:, :], ACT.Copy).then_inc(s_ev, 1)
            high_w(25)
            for n in range(16, len(TP)):
                evac_tp(n)

            def exp(N, n):
                act.wait_ge(s_L, N + 5)
                w = P * (n % 4 + 1)
                nc.scalar.activation(L[:, n % 4, 0:w], L[:, n % 4, 0:w], ACT.Exp, bias=nmx[:, n % 8:n % 8 + 1],
                                     scale=-1.0, accum_out=sums[:, n % 8:n % 8 + 1]).then_inc(s_E, 1)

            def copy_p(N, n):
                act.wait_ge(s_T, N + 5)
                act.wait_ge(s_PV, N + 1)
                w = P * (n % 4 + 1)
                nc.scalar.activation(PTs[:, n % 4, 0:w], ps[4 + n % 2][:, 0:w], ACT.Copy).then_inc(s_Ca, 1)

            def slot(u, n, last=False):
                if (n + 1) % 4 < 2 and not (last and n == 7):
                    copy_p(8 * u + (n + 1), (n + 1) % 8)
                if not (last and n >= 5):
                    exp(8 * u + (n + 3), (n + 3) % 8)

            for n in range(3):
                exp(n, n)
            copy_p(0, 0)
            with act.Fori(0, N_A) as i:
                for n in range(8):
                    slot(i, n)
            with act.Fori(0, 3) as i:
                for br in range(2):
                    for n in range(8):
                        slot(2 * i + N_A + br, n)
            for br in range(2):
                for n in range(8):
                    slot(N_A + 6 + br, n, last=br == 1)

            for kk in range(KD):
                act.wait_ge(s_mtp, kk + 1)
                nc.scalar.activation(mhi[:, kk, :], ps[kk % 2][:, :], ACT.Copy).then_inc(s_mhi, 1)
            for w in range(26, 34):
                high_w(w)
            for t in range(T):
                act.wait_ge(s_x1, T + t + 1)
                nc.scalar.activation(xn2[:, t, :], x1[:, t, :], ACT.Square,
                                     accum_out=xss[:, T + t:T + t + 1]).then_inc(s_x1sq, 1)
            act.wait_ge(s_x1sq, T)
            nc.scalar.activation(xst[:, :], xss[:, T:2 * T], ACT.Sqrt, bias=eps[:, :], scale=1.0 / D
                                 ).then_inc(s_x2st, 1)
            act.wait_ge(s_modf, 1)
            for kk in range(KD):
                h_chunk(kk, hf2, af[:, kk:kk + 1], modfb[:, kk:kk + 1], s_h2tp, s_hf2, s_h2lo, 0, ps[4:6])

            with act.Fori(0, NF // 2) as i:
                for jj in range(2):
                    for r in range(2):
                        w0 = W_GU + 4 + 2 * jj + r
                        act.wait_ge(s_mm, 4 * i + (w0 - 3))
                        high(None, SLOT[w0], 16 * i + raw_count(w0))
                    act.wait_ge(s_mm, 4 * i + (W_GU + 2 * jj + 2))
                    act.wait_ge(s_prod, 2 * i + (jj + 1))
                    nc.scalar.activation(sil[:, jj, :], ps[2 * jj][:, :], ACT.Silu).then_inc(s_sil, 1)
            with act.Fori(0, 4) as i:
                for r in range(4):
                    w0 = W_DN + 4 + r
                    act.wait_ge(s_mm, 4 * i + (w0 - 3))
                    high(None, SLOT[w0], 16 * i + raw_count(w0))
            for w in range(W_DN + 20, N_W):
                high_w(w)
            for dt in range(KD):
                if dt % 2:
                    act.wait_ge(s_dn, dt + 1)
                    nc.scalar.activation(yT[:, dt, :], ps[dt][:, :], ACT.Copy, scale=modfb[:, 16 + dt:17 + dt]
                                         ).then_inc(s_yT, 1)

        @block.vector
        def _(dve):
            chain = [0]

            def link(ins):
                chain[0] += 1
                ins.then_inc(s_dch, 1)
                dve.wait_ge(s_dch, chain[0])

            dve.wait_ge(s_par, 16)
            nc.vector.tensor_scalar(gq[:, 0:1], par[:, C_GAIN + G_QB:C_GAIN + G_QB + 1], SCALE, None, ALU.mult)
            nc.vector.tensor_scalar(gq[:, 1:2], par[:, C_GAIN + G_QA:C_GAIN + G_QA + 1], SCALE, None, ALU.mult
                                    ).then_inc(s_gq, 1)
            dve.wait_ge(s_xst, 1)
            link(nc.vector.reciprocal(xrs[:, :], xst[:, :]))
            for t in range(T):
                nc.vector.tensor_scalar(xn[:, t, :], x0[:, t, :], xrs[:, t:t + 1], None, ALU.mult).then_inc(s_xn, 1)

            def split(kk, hbuf, hi_t, lo_t, hfs, his, los):
                dve.wait_ge(hfs, kk + 1)
                nc.vector.tensor_copy(hi_t[:, kk, :], hbuf[:, kk % 2, :]).then_inc(his, 1)
                dve.wait_ge(his, kk + 1)
                nc.vector.tensor_tensor(lo_t[:, kk, :], hbuf[:, kk % 2, :], hi_t[:, kk, :].bitcast(F32),
                                        ALU.subtract).then_inc(los, 1)

            for kk in range(KD):
                dve.wait_ge(s_adamm, 2 * kk + 2)
                link(nc.vector.tensor_tensor(modm[:, kk, :], ps[6 + kk % 2][:, 0:2],
                                             par[:, C_BM + 2 * kk:C_BM + 2 * kk + 2], ALU.add))
                nc.vector.scalar_tensor_tensor(am[:, kk:kk + 1], modm[:, kk, 0:1], 1.0,
                                               par[:, C_GM + kk:C_GM + kk + 1], ALU.add, ALU.mult).then_inc(s_mod, 1)
                split(kk, hf, h1hi, h1lo, s_hf, s_hhi, s_hlo)
            dve.wait_ge(s_glh, 1)
            nc.vector.tensor_tensor(gll[:, :, :], glr[:, :, :], glh[:, :, :].bitcast(F32), ALU.subtract
                                    ).then_inc(s_gll, 1)

            achain = [0]

            def late(k):
                j, cp = divmod(k, 4)
                dve.wait_ge(s_r2[k % 4], 16 * (k // 4 + 1))
                a_ = acc[j]
                for c in range(2):
                    w_ = ring2[:, k % 4, 512 * c:512 * c + 512]
                    s_ = silc[:, 2 * cp + c:2 * cp + c + 1]
                    if cp == 0 and c == 0:
                        i = nc.vector.tensor_scalar(a_, w_, s_, None, ALU.mult)
                    else:
                        dve.wait_ge(s_ach, achain[0])
                        i = nc.vector.scalar_tensor_tensor(a_, w_, s_, a_, ALU.mult, ALU.add)
                    achain[0] += 1
                    i.then_inc(s_ach, 1)

            def norm_block(b, h):
                for t in range(T):
                    q = 4 * b + t
                    dve.wait_ge(s_ev, {0: 0, 1: 4, 2: 8, 3: 12}[b] + t + 1)
                    nc.vector.tensor_reduce(ssb[:, b, t * h:t * h + h],
                                            sq[:, q % 2, 0:64 * h].rearrange("p (h d) -> p h d", d=DH), AXX, ALU.add
                                            ).then_inc(s_ssr, 1)
                dve.wait_ge(s_std, b + 1)
                link(nc.vector.reciprocal(rsb[:, b, 0:T * h], stb[:, b, 0:T * h]))
                v = nat[:, b % 2, :, 0:64 * h].rearrange("p t (h d) -> p t h d", d=DH)
                nc.vector.tensor_tensor(v, v, view(rsb[:, b, 0:1], [[h, T], [1, h], [0, DH]]), ALU.mult
                                        ).then_inc(s_nrm, 1)

            def lates(a, b):
                for k in range(a, b):
                    late(k)

            lates(0, 6)
            norm_block(0, 8)
            lates(6, 14)
            norm_block(1, 4)
            dve.wait_ge(s_kce, 1)
            nc.vector.tensor_reduce(kcs[:, 0, :], kcq[:, :, :], AXX, ALU.add).then_inc(s_kcr, 1)
            dve.wait_ge(s_kcst, 1)
            link(nc.vector.reciprocal(kcs[:, 2, :], kcs[:, 1, :]))
            nc.vector.tensor_tensor(kcn[:, :, :], kcn[:, :, :], view(kcs[:, 2, 0:1], [[1, 2], [0, DH]]), ALU.mult
                                    ).then_inc(s_kcn, 1)
            dve.wait_ge(s_sig, 1)
            dve.wait_ge(s_shp, 16)
            link(nc.vector.tensor_tensor(gv[:, :, :], G[:, 0:8, :],
                                         view(shp[:, S_VALID:S_VALID + 1], [[0, 8], [1, T]]), ALU.mult))
            lates(14, 22)
            norm_block(2, 8)
            lates(22, 30)
            dve.wait_ge(s_csc, 2)
            mask = view(shp[:, S_MASK:S_MASK + 1], [[0, 4], [1, P]])
            for b in range(2):
                i = nc.vector.tensor_tensor(cm[:, 16 * b:16 * b + 16, :].rearrange("p (r t) n -> p r (t n)", t=T),
                                            ps[6 + b][:, :].rearrange("p (r m) -> p r m", r=4), mask, ALU.add)
            link(i)
            link(nc.vector.tensor_reduce(cst[:, 0, :], cm[:, :, :], AXX, ALU.max))
            nc.vector.tensor_tensor(cm[:, :, :], cm[:, :, :], view(cst[:, 0, 0:1], [[1, 32], [0, NC]]),
                                    ALU.subtract).then_inc(s_cm, 1)
            dve.wait_ge(s_cex, 1)
            link(nc.vector.tensor_reduce(cst[:, 1, :], cm[:, :, :], AXX, ALU.add))
            link(nc.vector.reciprocal(cst[:, 2, :], cst[:, 1, :]))
            link(nc.vector.tensor_tensor(cst[:, 3, :].rearrange("p (a q t) -> p a q t", a=2, t=T),
                                         cst[:, 2, :].rearrange("p (a q t) -> p a q t", a=2, t=T),
                                         view(gv[:, 0:1, 0:1], [[T, 2], [2 * T, 4], [1, T]]), ALU.mult))
            norm_block(3, 8)
            lates(30, 32)
            dve.wait_ge(s_cpt, 2)
            for b in range(2):
                nc.vector.tensor_copy(PcT[:, 4 * b:4 * b + 4, :].rearrange("p r q -> p (r q)"), ps[6 + b][:, :]
                                      ).then_inc(s_cpte, 1)
            for p in range(4):
                dve.wait_ge(s_pvc, p + 1)
                nc.vector.tensor_tensor(
                    mix[:, :, 512 + 128 * p:640 + 128 * p].rearrange("p t (a d) -> p a t d", a=2),
                    ps[p][:, :].rearrange("p (a t d) -> p a t d", a=2, t=T),
                    view(cst[:, 3, 4 * p:4 * p + 1], [[16, 2], [1, T], [0, DH]]), ALU.mult).then_inc(s_mixc, 1)

            def logits(N, n, u_stage):
                t, a = n % 4, n % 8 // 4
                w = P * (t + 1)
                dve.wait_ge(s_S, N + 1)
                dve.wait_ge(s_T, N + 1)
                if t == 0:
                    dve.wait_ge(s_stg[a], 48 * u_stage + 48)
                dve.sem_inc(s_begun)
                b_ = bias[:, a, 0:w][:, ::-1]
                nc.vector.tensor_tensor_reduce(out=L[:, t, 0:w], in0=ps[t][:, 0:w], in1=b_, scale=-1.0, scalar=3e38,
                                               op0=ALU.add, op1=ALU.min, accum_out=nmx[:, n % 8:n % 8 + 1]
                                               ).then_inc(s_L, 1)

            def copy_p(N, n):
                dve.wait_ge(s_T, N + 5)
                dve.wait_ge(s_PV, N + 1)
                w = P * (n % 4 + 1)
                nc.vector.tensor_copy(PTs[:, n % 4, 0:w], ps[4 + n % 2][:, 0:w]).then_inc(s_Cd, 1)

            def norm_half(u, a, qi, br, i_n):
                dve.wait_ge(s_PV, 8 * u + (4 * a + 8))
                nc.vector.reciprocal(rec[:, a, :], sums[:, 4 * a:4 * a + 4]).then_inc(s_nch, 1)
                dve.wait_ge(s_nch, i_n + 1)
                o_ = ps[6 + a][:, 0:T * DH].rearrange("p (t d) -> p t d", t=T)
                if br is None:
                    m = mix[:, :, bass.ds(128 * qi + 64 * a, 64)]
                    nc.vector.tensor_tensor(m, o_, view(rec[:, a, 0:1], [[1, T], [0, DH]]), ALU.mult
                                            ).then_inc(s_N, 1)
                    return
                g = G[:, bass.ds(2 * qi + (8 * br + a - 8), 1), :].rearrange("p o t -> p (o t)")
                nc.vector.tensor_tensor(recg[:, a, :], rec[:, a, :], g, ALU.mult).then_inc(s_nch, 1)
                dve.wait_ge(s_nch, i_n + 2)
                dve.wait_ge(s_add, 2 * (u - N_A) + (a + 1))
                nc.vector.tensor_tensor(tmpo[:, a, :, :], o_, view(recg[:, a, 0:1], [[1, T], [0, DH]]), ALU.mult
                                        ).then_inc(s_N, 1)

            def slot(u, n, qi, br, n0, last=False):
                if not (last and n >= 5):
                    logits(8 * u + (n + 3), n + 3, u + (n + 3) // 8)
                if (n + 1) % 4 >= 2:
                    copy_p(8 * u + (n + 1), n + 1)
                if n in (3, 7):
                    a = n // 4
                    norm_half(u, a, qi, br, n0 + a * (1 if br is None else 2))

            dve.wait_ge(s_mixc, 4)
            nc.vector.memset(nmx[:, :], 0.0).then_inc(s_L, 4)
            nc.vector.memset(rec[:, :, :], 0.0).then_inc(s_N, 2)
            nc.vector.memset(recg[:, :, :], 0.0).then_inc(s_add, 2)
            dve.wait_ge(s_L, 4)
            dve.wait_ge(s_N, 2)
            dve.wait_ge(s_add, 2)
            for n in range(3):
                logits(n, n, 0)
            with dve.Fori(0, N_A) as i:
                for n in range(8):
                    slot(i, n, i, None, 2 * i)
            with dve.Fori(0, 3) as i:
                for br in range(2):
                    for n in range(8):
                        slot(2 * i + N_A + br, n, i + 4, br + 1, 8 * i + (2 * N_A + 4 * br))
            for br in range(2):
                for n in range(8):
                    slot(N_A + 6 + br, n, 7, br + 1, 24 + 2 * N_A + 4 * br, last=br == 1)

            for kk in range(KD):
                dve.wait_ge(s_mhi, kk + 1)
                nc.vector.tensor_tensor(mlo[:, kk, :], ps[kk % 2][:, :], mhi[:, kk, :].bitcast(F32), ALU.subtract
                                        ).then_inc(s_mlo, 1)
            dve.wait_ge(s_tpev, len(TP))
            link(nc.vector.tensor_tensor(modfb[:, :], modf[:, :], par[:, C_BF:C_BF + 24], ALU.add))
            nc.vector.scalar_tensor_tensor(af[:, :], modfb[:, 8:16], 1.0, par[:, C_GF:C_GF + KD], ALU.add, ALU.mult
                                           ).then_inc(s_modf, 1)
            dve.wait_ge(s_x1in, 16)
            for h in range(2):
                for t in range(T):
                    q = T * h + t
                    c_ = slice(512 * h, 512 * h + 512)
                    if t < T - 1:
                        dve.wait_ge(s_op, 3 * h + t + 1)
                    else:
                        dve.wait_ge(s_mm, W_OUT + 4 * h + 4)
                    if q >= 2:
                        dve.wait_ge(s_x1, q - 1)
                    nc.vector.tensor_tensor(ob[:, q % 2, :], ps[4 + t][:, :], gtm[:, c_], ALU.mult
                                            ).then_inc(s_ot, 1)
                    dve.wait_ge(s_ot, q + 1)
                    nc.vector.tensor_tensor(x1[:, t, c_], x1[:, t, c_], ob[:, q % 2, :], ALU.add).then_inc(s_x1, 1)
            dve.wait_ge(s_x2st, 1)
            link(nc.vector.reciprocal(xrs[:, :], xst[:, :]))
            for t in range(T):
                nc.vector.tensor_scalar(xn2[:, t, :], x1[:, t, :], xrs[:, t:t + 1], None, ALU.mult).then_inc(s_xn2, 1)
            for kk in range(KD):
                split(kk, hf2, mhi, mlo, s_hf2, s_h2hi, s_h2lo)

            nc.vector.memset(sil[:, 0, 0:1], 0.0).then_inc(s_prod, 2)
            nc.vector.memset(actf[:, 0, 0:1], 0.0).then_inc(s_alo, 2)
            with dve.Fori(0, NF // 2) as i:
                for jj in range(2):
                    dve.wait_ge(s_sil, 2 * i + (jj + 1))
                    dve.wait_ge(s_alo, 2 * i + (jj + 1))
                    nc.vector.tensor_tensor(actf[:, jj, :], ps[2 * jj + 1][:, :], sil[:, jj, :], ALU.mult
                                            ).then_inc(s_prod, 1)
                    dve.wait_ge(s_prod, 2 * i + (jj + 3))
                    a_ = ahi[:, bass.ds(2 * i + jj, 1), :].rearrange("p o n -> p (o n)")
                    nc.vector.tensor_copy(a_, actf[:, jj, :]).then_inc(s_ahi, 1)
                    dve.wait_ge(s_ahi, 2 * i + (jj + 1))
                    nc.vector.tensor_tensor(alo[:, bass.ds(2 * i + jj, 1), :].rearrange("p o n -> p (o n)"),
                                            actf[:, jj, :], a_.bitcast(F32), ALU.subtract).then_inc(s_alo, 1)
            for dt in range(KD):
                if dt % 2 == 0:
                    dve.wait_ge(s_dn, dt + 1)
                    nc.vector.tensor_scalar(yT[:, dt, :], ps[dt][:, :], modfb[:, 16 + dt:17 + dt], None, ALU.mult
                                            ).then_inc(s_nrm, 1)
            for t in range(T):
                for h in range(2):
                    dve.wait_ge(s_ytp, 2 * t + h + 1)
                    nc.vector.tensor_tensor(yo[:, t, 512 * h:512 * h + 512], ps[2 * t + h][:, :],
                                            x1[:, t, 512 * h:512 * h + 512], ALU.add).then_inc(s_yo, 1)

        @block.tensor
        def _(pe):
            PASSES = ((0, 0), (0, 1), (1, 0))
            W2 = (whi, wlo)

            pe.wait_ge(s_rel, 48)
            nc.tensor.matmul(ps[6][0:16, 0:512], rel_s[:, :], oneh_s[:, 0:512], start=True, stop=True)
            nc.tensor.matmul(ps[7][0:16, 0:BV - 512], rel_s[:, :], oneh_s[:, 512:BV], start=True, stop=True
                             ).then_inc(s_bvp, 1)
            pe.wait_ge(s_silc, 1)
            pe.wait_ge(s_shp, 16)
            pe.wait_ge(s_bvs, 2)
            for kk in range(KD):
                if kk >= 2:
                    pe.wait_ge(s_mod, kk - 1)
                for e in (2 * kk, 2 * kk + 1):
                    pe.wait_ge(s_raw[e % 4], 16 * (e // 4 + 1))
                    for c in range(KD):
                        mm = nc.tensor.matmul(ps[6 + kk % 2][:, e % 2:e % 2 + 1], raw[:, e % 4, P * c:P * c + P], silc[:, c:c + 1],
                                              start=(c == 0), stop=(c == KD - 1))
                    mm.then_inc(s_adamm, 1)
                if kk == 0:
                    pe.wait_ge(s_xn, T)
                if kk >= 2:
                    pe.wait_ge(s_hf, kk - 1)
                for t in range(T):
                    mm = nc.tensor.transpose(ps[4 + kk % 2][:, P * t:P * t + P], xn[:, t, P * kk:P * kk + P], ident)
                mm.then_inc(s_htp, 1)

            pe.wait_ge(s_hlo, KD)
            H1 = (h1hi, h1lo)
            for w in range(W_T, W_QB):
                pe.wait_ge(s_lo, w + 1)
                for kv in range(2):
                    for k4 in range(4):
                        kk = 4 * w + k4
                        for i, (s, m) in enumerate(PASSES):
                            mm = nc.tensor.matmul(ps[4 + kv][:, :],
                                                  W2[s][:, SLOT[w], 256 * k4 + P * kv:256 * k4 + P * kv + P],
                                                  H1[m][:, kk, :], start=(kk == 0 and i == 0),
                                                  stop=(kk == KD - 1 and i == 2))
                mm.then_inc(s_mm, 1)

            def natural(w0, blk, acts, banks, out_sem, ev=None):
                for r in range(4):
                    pe.wait_ge(s_lo, w0 + r + 1)
                    for t in range(T):
                        if r == 0 and ev is not None:
                            ev(t)
                        for k2 in range(2):
                            kk = 2 * r + k2
                            for i, (s, m) in enumerate(PASSES):
                                mm = nc.tensor.matmul(banks[t][:, :], acts[s][:, kk, P * t:P * t + P],
                                                      W2[m][:, SLOT[w0 + r], 512 * k2:512 * k2 + 512],
                                                      start=(kk == 0 and i == 0), stop=(kk == KD - 1 and i == 2))
                        if r == 3 and t < T - 1:
                            mm.then_inc(out_sem, 1)
                    mm.then_inc(s_mm, 1)

            def evacuated(blk):
                def f(t):
                    if blk:
                        pe.wait_ge(s_ev, 4 * (blk - 1) + t + 1)
                return f

            def tp(n):
                kind, j = TP[n]
                bank = ps[4 + n % 2]
                if n >= 2:
                    pe.wait_ge(s_tpev, n - 1)
                else:
                    pe.wait_ge(s_kvE, 2)
                if kind in ("q", "k", "kb"):
                    half = 0 if kind == "q" else 1
                    pe.wait_ge(s_nrm, {("q", True): 1, ("kb", True): 2, ("q", False): 3, ("k", False): 4}[kind, j >= 4])
                    c = P * (j % 4)
                    for t in range(T):
                        mm = nc.tensor.transpose(bank[:, P * t:P * t + P], nat[:, half, t, c:c + P], ident)
                elif kind == "gtm":
                    pe.wait_ge(s_ach, 8 * (j + 1))
                    pe.wait_ge(s_brow, 16)
                    nc.tensor.matmul(bank[:, :], ones, acc[j], start=True, stop=False)
                    mm = nc.tensor.matmul(bank[:, :], ones[0:1, :], brow_s[0:1, 512 * j:512 * j + 512],
                                          start=False, stop=True)
                elif kind == "col":
                    pe.wait_ge(s_ach, 8 * (j + 1))
                    for q in range(4):
                        mm = nc.tensor.matmul(bank[:, q:q + 1], acc[j][:, P * q:P * q + P], ones[:, 0:1],
                                              start=True, stop=True)
                else:
                    pe.wait_ge(s_gelu, 2)
                    for g in range(2):
                        for ht in range(2):
                            mm = nc.tensor.matmul(bank[:, DH * g:DH * g + DH],
                                                  hidv[:, ht, g, :, :].rearrange("p t n -> p (t n)"),
                                                  w2s[:, 1, ht, :], start=(ht == 0), stop=(ht == 1))
                mm.then_inc(s_tp, 1)

            def hidden(kv):
                pe.wait_ge(s_w1, 16 * (kv + 1))
                pe.wait_ge(s_R, 4)
                if kv == 1:
                    pe.wait_ge(s_sig, 1)
                for ht in range(2):
                    for c in range(CL // 2):
                        mm = nc.tensor.matmul(ps[6][:, 64 * ht:64 * ht + 64], w1s[:, c, P * ht:P * ht + P],
                                              R[:, kv, c, :, :].rearrange("p g n -> p (g n)"),
                                              start=(c == 0), stop=(c == CL // 2 - 1))
                mm.then_inc(s_hid, 1)

            natural(W_QB, 0, H1, ps, s_pj, evacuated(0))
            hidden(0)
            natural(W_KV, 1, H1, ps, s_pj, evacuated(1))
            for n in range(5):
                tp(n)
            pe.wait_ge(s_gelu, 1)
            pe.wait_ge(s_w2, 16)
            for g in range(2):
                for ht in range(2):
                    mm = nc.tensor.matmul(ps[7][0:NC, DH * g:DH * g + DH], hidk[:, ht, NC * g:NC * g + NC],
                                          w2s[:, 0, ht, :], start=(ht == 0), stop=(ht == 1))
            mm.then_inc(s_kcp, 1)
            pe.wait_ge(s_gll, 1)
            for t in range(T):
                for kk in range(KD):
                    for i, (s, m) in enumerate(PASSES):
                        mm = nc.tensor.matmul(ps[6][:, 24 * t:24 * t + 24], H1[s][:, kk, P * t:P * t + P],
                                              (glh, gll)[m][:, kk, :], start=(kk == 0 and i == 0),
                                              stop=(kk == KD - 1 and i == 2))
            mm.then_inc(s_glp, 1)
            natural(W_QA, 2, H1, ps, s_pj, evacuated(2))
            for n in range(5, 9):
                tp(n)
            pe.wait_ge(s_kcn, 1)
            nc.tensor.transpose(ps[7][:, 256:288], kcn[:, :, :].rearrange("p g d -> p (g d)"), ident[0:NC, 0:NC]
                                ).then_inc(s_kctp, 1)
            hidden(1)
            pe.wait_ge(s_kcT, 1)
            pe.wait_ge(s_tpev, 4)
            pe.wait_ge(s_sig, 1)
            for a in (1, 0):
                if a == 0:
                    pe.wait_ge(s_gelu, 2)
                for p in range(4):
                    for t in range(T):
                        h = slice(64 * a, 64 * a + 64)
                        c = NC * (4 * p + t)
                        mm = nc.tensor.matmul(ps[6 + a][:, c:c + NC], QT[h, 4 + p, P * t:P * t + P], kcT[h, :],
                                              start=True, stop=True)
                mm.then_inc(s_csc, 1)
            natural(W_KA, 3, H1, ps, s_pj, evacuated(3))
            for n in range(9, 16):
                tp(n)
            pe.wait_ge(s_cex, 1)
            for b in range(2):
                for q in range(4):
                    r = 4 * b + q
                    mm = nc.tensor.transpose(ps[6 + b][:, P * q:P * q + P],
                                             cm[:, 4 * r:4 * r + 4, :].rearrange("p t n -> p (t n)"), ident)
                mm.then_inc(s_cpt, 1)
            natural(W_VA, 4, H1, ps, s_pj, evacuated(4))
            for n in range(16, len(TP)):
                tp(n)
            pe.wait_ge(s_cpte, 2)
            pe.wait_ge(s_ev, 20)
            for p in range(4):
                for a in range(2):
                    mm = nc.tensor.matmul(ps[p][:, 256 * a:256 * a + 256], PcT[:, 4 * a + p, :],
                                          Vbd[:, a, :, :].rearrange("p t d -> p (t d)"), start=True, stop=True)
                mm.then_inc(s_pvc, 1)

            def scores(N, n, u_stage):
                t, a = n % 4, n % 8 // 4
                if t == 0:
                    pe.wait_ge(s_stg[a], 48 * u_stage + 48)
                pe.wait_ge(s_L, N + 1)
                h = slice(64 * a, 64 * a + 64)
                w = P * (t + 1)
                nc.tensor.matmul(ps[t][:, 0:w], qs[h, P * t:P * t + P], ks[h, 0:w], start=True, stop=True
                                 ).then_inc(s_S, 1)

            def transposes(N, n, u, idx):
                t = n % 4
                pe.wait_ge(s_E, N + 1)
                pe.wait_ge(s_Cd if t < 2 else s_Ca, idx)
                for j in range(t + 1):
                    mm = nc.tensor.transpose(ps[4 + t % 2][:, P * j:P * j + P], L[:, t, P * j:P * j + P], ident)
                mm.then_inc(s_T, 1)

            def products(N, n, u, V, vcol, idx):
                t, a = n % 4, n % 8 // 4
                pe.wait_ge(s_Ca if t < 2 else s_Cd, idx)
                if t == 0:
                    pe.wait_ge(s_N, 2 * u + (a + 1))
                for j in range(t + 1):
                    mm = nc.tensor.matmul(ps[6 + a][:, DH * t:DH * t + DH], PTs[:, t, P * j:P * j + P],
                                          V[:, j, bass.ds(vcol + 64 * a, 64)], start=(j == 0), stop=(j == t))
                mm.then_inc(s_PV, 1)

            def t_idx(u, n):
                t, a = n % 4, n // 4
                return 4 * u + (2 * a + (t + 1 if t < 2 else t - 1)) + (0 if t < 2 else 2)

            def p_idx(u, n):
                t, a = n % 4, n // 4
                return 4 * u + (2 * a + t % 2 + 3)

            def slot(u, n, V, vcol, last=False):
                m = n + 3
                if not (last and m >= 8):
                    scores(8 * u + m, m, u + m // 8)
                m = n + 1
                if not (last and m >= 8):
                    transposes(8 * u + m, m, u, t_idx(u + 1, 0) if m == 8 else t_idx(u, m))
                products(8 * u + n, n, u, V, vcol, p_idx(u, n))

            pe.wait_ge(s_L, 4)
            pe.wait_ge(s_tpev, len(TP))
            tiny = [nc.tensor.matmul(ps[4][:, 0:1], ident, ones[:, 0:1], start=True, stop=True) for _ in range(4)]
            tiny[0].then_inc(s_T, 4)
            tiny[1].then_inc(s_PV, 4)
            tiny[2].then_inc(s_Ca, 2)
            tiny[3].then_inc(s_Cd, 2)
            for n in range(3):
                scores(n, n, 0)
            transposes(0, 0, 0, t_idx(0, 0))
            with pe.Fori(0, N_A) as i:
                for n in range(8):
                    slot(i, n, VA, 128 * i)
            with pe.Fori(0, 3) as i:
                for br in range(2):
                    for n in range(8):
                        slot(2 * i + N_A + br, n, VB, 128 * br)
            for br in range(2):
                for n in range(8):
                    slot(N_A + 6 + br, n, VB, 128 * br, last=br == 1)

            pe.wait_ge(s_add, 18)
            pe.wait_ge(s_N, 2 * (N_A + 8) + 2)
            for kk in range(KD):
                if kk >= 2:
                    pe.wait_ge(s_mlo, kk - 1)
                for t in range(T):
                    mm = nc.tensor.transpose(ps[kk % 2][:, P * t:P * t + P], mix[:, t, P * kk:P * kk + P], ident)
                mm.then_inc(s_mtp, 1)
            M1 = (mhi, mlo)
            pe.wait_ge(s_mlo, KD)
            for h in range(2):
                def ev(t, h=h):
                    if h:
                        pe.wait_ge(s_ot, t + 1)
                natural(W_OUT + 4 * h, 0, M1, ps[4:8], s_op, ev)

            pe.wait_ge(s_xn2, T)
            for kk in range(KD):
                if kk >= 2:
                    pe.wait_ge(s_hf2, kk - 1)
                for t in range(T):
                    mm = nc.tensor.transpose(ps[4 + kk % 2][:, P * t:P * t + P], xn2[:, t, P * kk:P * kk + P], ident)
                mm.then_inc(s_h2tp, 1)
            pe.wait_ge(s_h2lo, KD)

            with pe.Fori(0, NF // 2) as i:
                for jj in range(2):
                    for r in range(2):
                        w0 = W_GU + 2 * jj + r
                        pe.wait_ge(s_lo, 4 * i + (w0 + 1))
                        if r == 0:
                            pe.wait_ge(s_prod, 2 * i + (jj + 1))
                        for gu in range(2):
                            for k4 in range(4):
                                kk = 4 * r + k4
                                for q, (s, m) in enumerate(PASSES):
                                    c = 256 * k4 + P * gu
                                    mm = nc.tensor.matmul(ps[2 * jj + gu][:, :], W2[s][:, SLOT[w0], c:c + P],
                                                          M1[m][:, kk, :], start=(kk == 0 and q == 0),
                                                          stop=(kk == KD - 1 and q == 2))
                        mm.then_inc(s_mm, 1)

            def down(w, slot, k, first, last):
                pe.wait_ge(s_lo, w + 1)
                for dt in range(KD):
                    for q, (s, m) in enumerate(PASSES):
                        rhs = (ahi, alo)[m][:, bass.ds(k, 1), :].rearrange("p o n -> p (o n)")
                        mm = nc.tensor.matmul(ps[dt][:, :], W2[s][:, slot, P * dt:P * dt + P], rhs,
                                              start=(first and q == 0), stop=(last and q == 2))
                    if last:
                        mm.then_inc(s_dn, 1)
                if not last:
                    mm.then_inc(s_mm, 1)

            pe.wait_ge(s_alo, NF + 2)
            for k in range(2):
                down(W_DN + k, SLOT[W_DN + k], k, k == 0, False)
            with pe.Fori(0, (NF - 6) // 4) as i:
                for r in range(4):
                    down(4 * i + (W_DN + 2 + r), SLOT[W_DN + 2 + r], 4 * i + (2 + r), False, False)
            for k in range(2 + (NF - 6) // 4 * 4, NF):
                down(W_DN + k, SLOT[W_DN + k], k, False, k == NF - 1)

            pe.wait_ge(s_yT, KD // 2)
            pe.wait_ge(s_nrm, 4 + KD // 2)
            for t in range(T):
                for h in range(2):
                    for q in range(4):
                        dt = 4 * h + q
                        mm = nc.tensor.transpose(ps[2 * t + h][:, P * q:P * q + P], yT[:, dt, P * t:P * t + P], ident)
                    mm.then_inc(s_ytp, 1)


def shape_constants():
    shc = np.zeros((P, 388), np.float32)
    shc[:, S_ID:S_ID + P] = np.eye(P)
    shc[:, S_ONE:S_ONE + P] = 1.0
    q = np.arange(P)[:, None, None] + P * np.arange(T)[None, :, None]
    n = np.arange(NC)[None, None, :]
    hidden = (n * CS + CL - 1 > q) | (n >= NCMP)
    shc[:, S_MASK:S_MASK + P] = np.where(hidden, NEG, 0.0).reshape(P, P)
    shc[:, S_VALID:S_VALID + T] = ~hidden.all(axis=2)
    d = np.arange(BV) - (P - 1)
    half = NB_ // 2
    big = half + (np.log(np.maximum(d, 1) / half) / math.log(MAX_DIST / half) * half).astype(np.int64)
    bucket = np.where(d < half, np.maximum(d, 0), np.minimum(big, NB_ - 1))
    oneh = np.zeros((NB_ + 1, BV), np.float32)
    oneh[bucket, np.arange(BV)] = 1.0
    oneh[NB_] = np.where(d < 0, NEG, 0.0)
    return shc, oneh


def kernel(**inputs):
    import concourse.bacc as _bacc
    from concourse.bass_utils import run_bass_kernel_spmd as _run

    a = {k: np.asarray(v) for k, v in inputs.items()}
    rows = lambda w, n: w.reshape(KD, P, n).transpose(1, 0, 2)

    w_in = rows(a["w_in"][0], a["w_in"].shape[2])
    o = np.cumsum([0, 512, 512, 512, 512] + [128] * 6 + [24])
    qa, ka, va, qb, kc, vc, ksl, vsl, kwn, vwn, gl = (w_in[:, :, o[i]:o[i + 1]] for i in range(11))
    pairs = lambda w: w.reshape(P, KD, 2, 4, DH).transpose(0, 1, 3, 2, 4).reshape(P, KD, 512)
    wst = np.empty((N_W, P, U), np.float32)

    def put(w0, blk, per):
        n = blk.shape[1] // per
        wst[w0:w0 + n] = blk.reshape(P, n, U).transpose(1, 0, 2)

    put(W_T, np.concatenate([kc, vc], 2), 4)
    put(W_QB, pairs(qb), 2)
    put(W_KV, np.concatenate([ksl, kwn, vsl, vwn], 2), 2)
    put(W_QA, qa, 2)
    put(W_KA, ka, 2)
    put(W_VA, va, 2)
    wo = a["w_out"][0]
    wo = np.concatenate([wo[:512], wo[512:].reshape(2, 4, DH, D).transpose(1, 0, 2, 3).reshape(512, D)])
    wo = rows(wo, D)
    put(W_OUT, wo[:, :, :512], 2)
    put(W_OUT + 4, wo[:, :, 512:], 2)
    gu = rows(a["w_gu"][0], 2 * FFN).reshape(P, 2, 4, 2, NF, P)
    wst[W_GU:W_DN] = gu.transpose(4, 1, 0, 2, 3, 5).reshape(2 * NF, P, U)
    wst[W_DN:] = a["w_down"][0].reshape(NF, P, U)

    ada = rows(a["w_ada"][0], 6 * D).reshape(P, KD, 6, D)
    sc_sh = np.stack([ada[:, :, 1], ada[:, :, 0]], 2).reshape(P, KD, 2, KD, P)
    ada_e = sc_sh.transpose(3, 2, 0, 1, 4).reshape(N_EARLY, P, U)
    late = np.stack([ada[:, :, g] for g in (2, 3, 4, 5)], 2).reshape(P, 4, 2, 4, 2, 512)
    ada_l = late.transpose(3, 4, 1, 0, 2, 5).reshape(32, P, U)

    col = lambda v: v.reshape(KD, P).T
    b = a["b_ada"][0].reshape(6, D)
    cols = np.zeros((P, N_COLS), np.float32)
    cols[:, C_C:C_C + 8] = col(a["c"][0])
    cols[:, C_BM:C_BM + 16:2] = col(b[1])
    cols[:, C_BM + 1:C_BM + 17:2] = col(b[0])
    cols[:, C_GM:C_GM + 8] = col(a["g_mix"][0])
    cols[:, C_GF:C_GF + 8] = col(a["g_ffn"][0])
    for i, g in enumerate((3, 4, 5)):
        cols[:, C_BF + 8 * i:C_BF + 8 * i + 8] = col(b[g])
    for i, name in enumerate(("q_norm_b", "k_norm_sel", "k_norm_win", "q_norm_a", "k_norm_a", "k_norm_cmp")):
        cols[:, C_GAIN + i] = np.concatenate([a[name][0], a[name][0]])
    for i, name in enumerate(("cmp_pe_k", "cmp_pe_v")):
        cols[:, C_PE + 16 * i:C_PE + 16 * i + 16] = a[name][0].reshape(CL // 2, 2 * DH).T
    r = a["rel_bias"]
    rel = np.concatenate([r[:, :8], r[:, 8:].reshape(NB_, 2, 4).transpose(0, 2, 1).reshape(NB_, 8)], 1)
    wgl = gl.reshape(P, KD, 2, 4, 3).transpose(0, 1, 4, 3, 2).reshape(P, KD, 24)
    w1 = np.stack([a[n][0].reshape(CL // 2, P, 256).transpose(1, 0, 2) for n in ("cmp_w1_k", "cmp_w1_v")])
    w2 = np.stack([a[n][0].reshape(2, P, DH).transpose(1, 0, 2) for n in ("cmp_w2_k", "cmp_w2_v")], 1)
    shc, oneh = shape_constants()

    nc = _bacc.Bacc("TRN2", target_bir_lowering=False, num_devices=1)
    arrays, args = {}, []
    for name, v in (("wst", wst), ("ada_e", ada_e), ("ada_l", ada_l), ("x", a["x"]), ("cols", cols), ("shc", shc),
                    ("oneh", oneh), ("rel", rel), ("brow", b[2:3]), ("wgl", wgl), ("w1", w1), ("w2", w2)):
        arrays[name + "_dram"] = v = np.ascontiguousarray(v)
        args.append(nc.dram_tensor(name + "_dram", v.shape, mybir.dt.from_np(v.dtype), kind="ExternalInput").ap())
    out = nc.dram_tensor("out_dram", (1, SEQ, D), F32, kind="ExternalOutput").ap()
    layer(nc, *args, out)
    res = _run(nc, [arrays], core_ids=[0])
    return res.results[0]["out_dram"]
```

```python
import math
from contextlib import ExitStack

import numpy as np
import concourse.bass as bass
from concourse import mybir

F32 = mybir.dt.float32
F32R = mybir.dt.float32r
ALU = mybir.AluOpType
ACT = mybir.ActivationFunctionType
AXX = mybir.AxisListType.X

P = 128
SEQ, D = 512, 1024
T = SEQ // P
KD = D // P
DH = 64
FFN = 2816
NF = FFN // P
NB_, MAX_DIST = 32, 128
EPS = 1e-6
NEG = -1e30
SCALE = DH ** -0.5
CL, CS = 32, 16
NCMP = (SEQ - CL) // CS + 1
NC = 32
U = 1024

W_T, W_QB, W_KV, W_QA, W_KA, W_VA = 0, 2, 6, 10, 14, 18
W_OUT, W_GU, W_DN = 22, 30, 30 + 2 * NF
N_W = W_DN + NF
N_EARLY = 16

C_C, C_BM, C_GM, C_GF, C_BF, C_GAIN, C_PE = 0, 8, 24, 32, 40, 64, 70
N_COLS = C_PE + 2 * CL // 2
G_QB, G_KSL, G_KWN, G_QA, G_KA, G_KCMP = range(6)
S_ID, S_ONE, S_MASK, S_VALID = 0, 128, 256, 384
BV = 640
L_AT = [P * t * (t + 1) // 2 for t in range(T)]
LW = P * T * (T + 1) // 2


def view(ap, dims, off=0):
    return bass.AP(ap.tensor, ap.offset + off, [list(ap.ap[0])] + dims)


def layer(nc, wst, ada_e, ada_l, xd, cols, shc, oneh, rel, brow, wgl, w1, w2, out):
    bvd = nc.dram_tensor("bias_by_distance", (16, BV), F32, kind="Internal").ap()
    x_v = xd.rearrange("b (t p) d -> p (b t) d", p=P)
    out_v = out.rearrange("b (t p) d -> p (b t) d", p=P)

    with ExitStack() as top:
        def sb(name, shape, dt=F32, ctx=top):
            return ctx.enter_context(nc.sbuf_tensor(name, shape, dt))

        def sem(name):
            return top.enter_context(nc.semaphore(name))

        ps = [top.enter_context(nc.psum_tensor(f"ps{i}", [P, 512], F32)) for i in range(8)]

        par = sb("par", [P, N_COLS])
        shp = sb("shp", [P, 388])
        ident, ones = shp[:, S_ID:S_ID + P], shp[:, S_ONE:S_ONE + P]
        eps = sb("eps", [P, 1])
        silc = sb("silc", [P, KD])
        xss = sb("xss", [P, 2 * T])
        xst = sb("xst", [P, T])
        xrs = sb("xrs", [P, T])
        modm = sb("modm", [P, KD, 2])
        am = sb("am", [P, KD])
        modf = sb("modf", [P, 3 * KD])
        modfb = sb("modfb", [P, 3 * KD])
        af = sb("af", [P, KD])
        gq = sb("gq", [P, 2])
        gtm = sb("gtm", [P, D])
        G = sb("G", [P, 24, T])
        raw = sb("raw", [P, 4, U])
        whi = sb("whi", [P, 4, U], F32R)
        wlo = sb("wlo", [P, 4, U], F32R)
        hp = sb("hp", [P, 2 * KD, SEQ], F32R)
        mhi, mlo = hp[:, 0:KD, :], hp[:, KD:2 * KD, :]
        h1hi, h1lo = mhi, mlo
        N_QP, N_KP = 8, 12

        ca = ExitStack()
        QT = sb("QT", [P, 8, SEQ], F32, ca)
        KT = sb("KT", [P, 6, SEQ], F32, ca)
        VA = sb("VA", [P, T, 512], F32, ca)
        VB = sb("VB", [P, T, 256], F32, ca)
        brow_s = VA[0:1, 0:2, :].rearrange("p o n -> p (o n)")
        eacc = [KT[:, 4, :], KT[:, 5, :], VA[:, 2, :], VA[:, 3, :]]
        acc = [QT[:, j, :] for j in range(4)] + [KT[:, j, :] for j in range(4)]
        with ExitStack() as c:
            x0 = sb("x0", [P, T, D], F32, c)
            xn = sb("xn", [P, T, D], F32, c)
        with ExitStack() as c:
            nat = sb("nat", [P, 2, T, 512], F32, c)
            w1s = sb("w1s", [P, CL // 2, 256], F32, c)
        mf = sb("mf", [P, 8, SEQ], F32, ca)
        with ExitStack() as c:
            mixc = sb("mixc", [P, T, 512], F32, c)
        PThi, PTlo = (sb(n, [P, T, SEQ], F32R, ca) for n in ("PThi", "PTlo"))
        with ExitStack() as c:
            ring2 = sb("ring2", [P, 4, U], F32, c)
            sq = sb("sq", [P, 2, 512], F32, c)
            R = sb("R", [P, 2, CL // 2, 2, NC], F32, c)
            ssb = sb("ssb", [P, 4, 32], F32, c)
            stb = sb("stb", [P, 4, 32], F32, c)
            rsb = sb("rsb", [P, 4, 32], F32, c)
            glr = sb("glr", [P, KD, 24], F32, c)
            glh = sb("glh", [P, KD, 24], F32R, c)
            gll = sb("gll", [P, KD, 24], F32R, c)
            w2s = sb("w2s", [P, 2, 2, DH], F32, c)
            hidk = sb("hidk", [P, 2, 2 * NC], F32, c)
            hidv = sb("hidv", [P, 2, 2, T, NC], F32, c)
            kcn = sb("kcn", [NC, 2, DH], F32, c)
            kcq = sb("kcq", [NC, 2, DH], F32, c)
            kcs = sb("kcs", [NC, 3, 2], F32, c)
            kcT = sb("kcT", [P, 2, NC], F32, c)
            Vbd = sb("Vbd", [P, 2, T, DH], F32, c)
            gv = sb("gv", [P, 8, T], F32, c)
            cst = sb("cst", [P, 4, 32], F32, c)
            rel_s = sb("rel_s", [33, 16], F32, c)
            with ExitStack() as c2:
                oneh_s = sb("oneh_s", [33, BV], F32, c2)
                bvs = sb("bvs", [16, BV], F32, c2)
            with ExitStack() as c2:
                hf = sb("hf", [P, 2, SEQ], F32, c2)
            with ExitStack() as c2:
                kcE = sb("kcE", [P, 2, 2, 256], F32, c2)
                Kst = sb("Kst", [P, 2, 2, 256], F32, c2)
            with ExitStack() as c2:
                cm = sb("cm", [P, 32, NC], F32, c2)
                with ExitStack() as c3:
                    glT = sb("glT", [24, SEQ], F32, c3)
                PcT = sb("PcT", [P, 8, P], F32, c2)
        with ExitStack() as c:
            QK = sb("QK", [P, 2, 3, SEQ], F32R, c)
            L = sb("L", [P, 2, LW], F32, c)
            bias = sb("bias", [P, 2, SEQ], F32, c)
            VS = sb("VS", [P, 2, T, 2 * DH], F32R, c)
            tmp = sb("tmp", [P, SEQ], F32, c)
            nmx = sb("nmx", [P, 8], F32, c)
            sums = sb("sums", [P, 8], F32, c)
            rec = sb("rec", [P, 2, T], F32, c)
            rg = sb("rg", [P, 2, T], F32, c)
        ca.close()
        x1 = sb("x1", [P, T, D])
        ob = sb("ob", [P, 2, 512])
        hf2 = sb("hf2", [P, 2, SEQ])
        with ExitStack() as c:
            xn2 = sb("xn2", [P, T, D], F32, c)
        with ExitStack() as c:
            sil = sb("sil", [P, 2, SEQ], F32, c)
            actf = sb("actf", [P, 2, SEQ], F32, c)
            ahi, alo = (sb(n, [P, NF, SEQ], F32R, c) for n in ("ahi", "alo"))
        with ExitStack() as c:
            yT = sb("yT", [P, KD, SEQ], F32, c)
            yo = sb("yo", [P, T, D], F32, c)

        s_par, s_shp, s_x, s_rel, s_gl, s_w2, s_w1, s_brow = map(
            sem, "par_in shp_in x_in rel_in gl_in w2_in w1_in brow_in".split())
        s_raw = [sem(f"raw{i}_in") for i in range(4)]
        s_r2 = [sem(f"ring2_{i}_in") for i in range(4)]
        s_eps, s_silc, s_xss, s_xst, s_xrs, s_xn = map(
            sem, "eps_set silc_done xss_done xst_done xrs_done xn_done".split())
        s_bvp, s_bvs, s_bvd = map(
            sem, "bv_psum bv_sbuf bv_dram".split())
        s_each = sem("early_acc_added")
        s_adamm, s_mod, s_htp, s_hf, s_hhi, s_hlo = map(
            sem, "ada_mm mod_done hT_psum hf_done h_hi h_lo".split())
        s_hi, s_lo, s_mm = map(sem, "w_hi w_lo w_used".split())
        s_kvE, s_kst, s_Rz, s_R = map(sem, "kvT_evac kst_in R_zero R_built".split())
        s_pj, s_ev, s_ssr, s_std, s_nrm = map(
            sem, "proj_psum proj_evac ss_done std_done nat_normed".split())
        s_ach = sem("acc_added")
        s_hid, s_gelu, s_kcp, s_kce, s_kcr, s_kcst, s_kcn, s_kctp, s_kcT = map(
            sem, "hid_psum gelu_done kc_psum kc_evac kc_ss kc_std kc_normed kcT_psum kcT_evac".split())
        s_glT, s_gltp = map(sem, "glT_evac gates_psum".split())
        s_glh, s_gll, s_glp, s_sig, s_gq = map(sem, "gl_hi gl_lo gl_psum gates_done gq_done".split())
        s_csc, s_cm, s_cex, s_cpt, s_cpte, s_pvc, s_mixc = map(
            sem, "cs_psum cm_done c_exp pcT_psum pcT_evac pvc_psum mixc_done".split())
        s_tp, s_tpev, s_vz, s_kcz = map(sem, "tp_psum tp_evac vbd_zero kcT_zero".split())
        s_dch, s_begun = map(sem, "dve_chain begun".split())
        s_stg = [sem(f"staged{a}") for a in range(2)]
        s_S, s_L, s_E, s_rch, s_rg, s_P, s_T, s_Phi, s_Plo, s_PV = map(
            sem, "S_psum logits exp_done rec_done rg_done P_scaled PT_psum PT_hi PT_lo PV_psum".split())
        s_kn = sem("nsa_k_staged")
        s_qkh, s_qkl, s_vh, s_vl, s_tmp, s_own, s_cb, s_mct, s_mcte = map(
            sem, "qk_hi qk_lo v_hi v_lo out_moved own_added heads_done mixcT_psum mixcT_evac".split())
        s_mfz = sem("mf_zero")
        s_mhi, s_mlo, s_op, s_ot, s_x1, s_x1in, s_x1sq, s_h2lo = map(
            sem, "m_hi m_lo out_psum out_gated x1_done x1_in x1_sq h2_lo".split())
        s_sil, s_prod, s_ahi, s_alo, s_dn, s_yT, s_ytp, s_yo, s_out = map(
            sem, "silu_done prod_done a_hi a_lo dn_psum yT_done y_psum yo_done out_done".split())
        s_h2tp, s_hf2, s_h2hi, s_xn2, s_x2ss, s_x2st, s_modf = map(
            sem, "h2_psum hf2_done h2_hi xn2_done x2_ss x2_std modf_done".split())

        block = top.enter_context(nc.Block())

        TP = ([("q", 4 + i) for i in range(4)] + [("gtm", 0), ("kb", 4), ("kb", 5), ("gtm", 1), ("col", 2)]
              + [("col", 3), ("col", 4)] + [("q", i) for i in range(4)] + [("vcmp", 0)]
              + [("col", 5), ("col", 6), ("col", 7)] + [("k", i) for i in range(4)])
        STG, STGN = 64, 48
        N_A = 4
        SLOT = [(w % 4) for w in range(N_W)]

        def raw_count(w):
            return 16 * (N_EARLY // 4 + w // 4 + 1)

        @block.sync
        def _(sp):
            sp.dma_start(par[:, :], cols).then_inc(s_par, 16)
            sp.dma_start(shp[:, :], shc).then_inc(s_shp, 16)
            sp.dma_start(x0[:, :, :], x_v).then_inc(s_x, 16)
            sp.dma_start(rel_s[0:32, :], rel).then_inc(s_rel, 16)
            sp.dma_start(rel_s[32:33, :], shc[0:1, S_ONE:S_ONE + 16]).then_inc(s_rel, 16)
            sp.dma_start(oneh_s[:, :], oneh).then_inc(s_rel, 16)
            for e in range(N_EARLY):
                if e >= 4:
                    sp.wait_ge(s_each, 2 * (e - 3))
                sp.dma_start(raw[:, e % 4, :], ada_e[e]).then_inc(s_raw[e % 4], 16)
            sp.dma_start(brow_s, brow).then_inc(s_brow, 16)
            sp.dma_start(glr[:, :, :], wgl).then_inc(s_gl, 16)
            sp.dma_start(w2s[:, :, :, :], w2).then_inc(s_w2, 16)

            def late(k):
                if k >= 4:
                    sp.wait_ge(s_ach, 2 * (k - 3))
                sp.dma_start(ring2[:, k % 4, :], ada_l[k]).then_inc(s_r2[k % 4], 16)

            def weights(w):
                if w < 4:
                    sp.wait_ge(s_each, 2 * (N_EARLY - 3 + w))
                else:
                    sp.wait_ge(s_lo, w - 3)
                sp.dma_start(raw[:, SLOT[w], :], wst[w]).then_inc(s_raw[SLOT[w]], 16)

            for w in range(W_OUT):
                weights(w)
                if w == 4:
                    sp.wait_ge(s_hlo, KD)
                    sp.dma_start(w1s[:, :, :], w1[0]).then_inc(s_w1, 16)
                if w == 11:
                    sp.wait_ge(s_hid, 1)
                    sp.dma_start(w1s[:, :, :], w1[1]).then_inc(s_w1, 16)
                if 4 <= w < 20:
                    late(2 * (w - 4))
                    late(2 * (w - 4) + 1)
            for w in range(W_OUT, W_OUT + 4):
                weights(w)

            top_, low_ = slice(0, 64), slice(64, 128)

            def move(dst, src, done):
                sp.dma_start(dst.bitcast(F32), src.bitcast(F32)).then_inc(done, 16)

            def stage_bias(a, qi):
                sp.dma_start(bias[:, a, :], bass.AP(bvd.tensor, qi * (2 * BV) + a * BV, [[1, P], [1, SEQ]])
                             ).then_inc(s_stg[a], 16)

            def stage(u, a):
                h = slice(64 * a, 64 * a + 64)
                stage_bias(a, u)
                sp.wait_ge(s_qkh, 2 * u + 2)
                sp.wait_ge(s_qkl, 2 * u + 1)
                move(QK[top_, a, :, :], hp[h, 4 * u:4 * u + 3, :], s_stg[a])
                move(QK[low_, a, 1:3, :], hp[h, 4 * u + 1:4 * u + 3, :], s_stg[a])
                sp.wait_ge(s_qkl, 2 * u + 2)
                move(QK[low_, a, 0, :], hp[h, 4 * u + 3, :], s_stg[a])

            def stage_nsa(r, a):
                h = slice(64 * a, 64 * a + 64)
                stage_bias(a, r + N_A)
                sp.wait_ge(s_qkh, r + (2 * N_A + 3))
                sp.wait_ge(s_qkl, r + (2 * N_A + 3))
                move(QK[top_, a, 0, :], hp[h, N_QP, :], s_stg[a])
                move(QK[low_, a, 0, :], hp[h, N_QP + 1, :], s_stg[a])

            sp.wait_ge(s_tpev, len(TP))
            sp.wait_ge(s_bvd, 16)
            for u in range(N_A):
                for a in range(2):
                    if u:
                        sp.wait_ge(s_L, 8 * u + 4 * a - 4)
                    stage(u, a)
            for a in range(2):
                sp.wait_ge(s_stg[a], 2 * STG)
            sp.wait_ge(s_qkh, 2 * N_A + 2)
            sp.wait_ge(s_qkl, 2 * N_A + 2)
            for br in range(2):
                for a in range(2):
                    h = slice(64 * a, 64 * a + 64)
                    for rows_ in (top_, low_):
                        move(hp[rows_, 4 * br + 2 * a:4 * br + 2 * a + 2, :],
                             hp[h, N_KP + 2 * br:N_KP + 2 * br + 2, :], s_kn)
            for a in range(2):
                sp.wait_ge(s_L, 8 * N_A + 4 * a - 4)
                stage_nsa(0, a)
            with sp.Fori(0, 3) as i:
                for a in range(2):
                    sp.wait_ge(s_L, 16 * i + (8 * N_A + 12 + 4 * a))
                    stage_nsa(i + 1, a)
            sp.wait_ge(s_qkl, 2 * N_A + 6)
            sp.wait_ge(s_stg[0], STG * N_A + 4 * STGN)
            sp.wait_ge(s_stg[1], STG * N_A + 4 * STGN)
            sp.dma_start(x1[:, :, :], x_v).then_inc(s_x1in, 16)
            for w in range(W_OUT + 4, W_GU):
                weights(w)
            with sp.Fori(0, (N_W - W_GU) // 4) as i:
                for r in range(4):
                    sp.wait_ge(s_lo, 4 * i + (W_GU + r - 3))
                    s = SLOT[W_GU + r]
                    sp.dma_start(raw[:, s, :], wst[bass.ds(4 * i + (W_GU + r), 1)].rearrange("o p n -> p (o n)")
                                 ).then_inc(s_raw[s], 16)
            for w in range(W_GU + (N_W - W_GU) // 4 * 4, N_W):
                weights(w)
            for t in range(T):
                sp.wait_ge(s_yo, 2 * (t + 1))
                sp.dma_start(out_v[:, t, :], yo[:, t, :]).then_inc(s_out, 16)
            sp.wait_ge(s_out, 16 * T)

        @block.gpsimd
        def _(pool):
            nc.gpsimd.memset(eps[:, :], EPS).then_inc(s_eps, 1)
            nc.gpsimd.memset(R[:, :, :, :, :], 0.0).then_inc(s_Rz, 1)
            nc.gpsimd.memset(Vbd[:, :, :, :], 0.0).then_inc(s_vz, 1)
            nc.gpsimd.memset(kcT[:, :, :], 0.0).then_inc(s_kcz, 1)

            def low(w, slot):
                pool.wait_ge(s_hi, w + 1)
                nc.gpsimd.tensor_tensor(wlo[:, slot, :], raw[:, slot, :], whi[:, slot, :].bitcast(F32),
                                        ALU.subtract).then_inc(s_lo, 1)

            for w in range(W_KV):
                low(w, SLOT[w])
            pool.wait_ge(s_kst, 128)
            pool.wait_ge(s_Rz, 1)
            pool.wait_ge(s_par, 16)
            for kv in range(2):
                for g in range(2):
                    win = view(Kst[:, kv, g, :], [[1, CL // 2], [CS // 2, NCMP]])
                    pe_ = view(par[:, C_PE + 16 * kv:C_PE + 16 * kv + 16], [[1, CL // 2], [0, NCMP]])
                    nc.gpsimd.tensor_tensor(R[:, kv, :, g, 0:NCMP], win, pe_, ALU.add).then_inc(s_R, 1)
            for w in range(W_KV, W_OUT + 4):
                low(w, SLOT[w])

            def low_part(n, src, j, hi, lo):
                pool.wait_ge(s_qkh, n + 1)
                pool.sem_inc(s_begun)
                nc.gpsimd.tensor_tensor(hp[:, lo, :], src[:, bass.ds(j, 1), :].rearrange("p o n -> p (o n)"),
                                        hp[:, hi, :].bitcast(F32), ALU.subtract).then_inc(s_qkl, 1)

            def qk_low(u):
                low_part(2 * u, KT, u, 4 * u + 1, 4 * u + 2)
                low_part(2 * u + 1, QT, u, 4 * u, 4 * u + 3)

            def k_low_nsa():
                for br in range(2):
                    low_part(2 * N_A + br, KT, 4 + br, N_KP + 2 * br, N_KP + 2 * br + 1)

            def q_low_nsa(r):
                low_part(r + (2 * N_A + 2), QT, r + 4, N_QP, N_QP + 1)

            def scale(H, a):
                pool.wait_ge(s_rg, H + 1)
                for t in range(T):
                    l_ = L[:, a, L_AT[t]:L_AT[t] + P * (t + 1)]
                    nc.gpsimd.tensor_tensor(l_, l_, view(rg[:, a, t:t + 1], [[0, P * (t + 1)]]), ALU.mult
                                            ).then_inc(s_P, 1)

            def v_low(H, a, V, col):
                pool.wait_ge(s_vh, H + 1)
                pool.sem_inc(s_begun)
                nc.gpsimd.tensor_tensor(VS[:, a, :, DH:2 * DH], V[:, :, bass.ds(col, DH)],
                                        VS[:, a, :, 0:DH].bitcast(F32), ALU.subtract).then_inc(s_vl, 1)

            def half(H, a, v_next):
                if v_next is not None:
                    scale(H + 1, 1 - a)
                    v_low(H + 1, 1 - a, *v_next)

            qk_low(0)
            qk_low(1)
            v_low(0, 0, VA, 0)
            scale(0, 0)
            for u in range(N_A):
                half(2 * u, 0, (VA, 128 * u + 64))
                if u < 2:
                    qk_low(u + 2)
                elif u == 2:
                    k_low_nsa()
                half(2 * u + 1, 1, (VA, 128 * u + 128) if u < 3 else (VB, 0))
                if u == 2:
                    q_low_nsa(0)
            with pool.Fori(0, 3) as i:
                for br in range(2):
                    half(4 * i + (2 * N_A + 2 * br), 0, (VB, 128 * br + 64))
                    if br == 0:
                        q_low_nsa(i + 1)
                    half(4 * i + (2 * N_A + 2 * br + 1), 1, (VB, 128 - 128 * br))
            for br in range(2):
                for a in range(2):
                    half(2 * N_A + 12 + 2 * br + a, a, (VB, (128 * br + 64) if a == 0 else 128) if br + a < 2 else None)

            with pool.Fori(0, (N_W - W_OUT - 4) // 4) as i:
                for r in range(4):
                    low(4 * i + (W_OUT + 4 + r), SLOT[W_OUT + 4 + r])
            for w in range(W_OUT + 4 + (N_W - W_OUT - 4) // 4 * 4, N_W):
                low(w, SLOT[w])

        @block.scalar
        def _(act):
            act.wait_ge(s_par, 16)
            nc.scalar.activation(silc[:, :], par[:, C_C:C_C + KD], ACT.Silu).then_inc(s_silc, 1)
            act.wait_ge(s_x, 16)
            for t in range(T):
                nc.scalar.activation(xn[:, t, :], x0[:, t, :], ACT.Square,
                                     accum_out=xss[:, t:t + 1]).then_inc(s_xss, 1)
            act.wait_ge(s_eps, 1)
            act.wait_ge(s_xss, T)
            nc.scalar.activation(xst[:, :], xss[:, 0:T], ACT.Sqrt, bias=eps[:, :], scale=1.0 / D).then_inc(s_xst, 1)
            act.wait_ge(s_xrs, 1)
            for t in range(T):
                nc.scalar.activation(xn[:, t, :], x0[:, t, :], ACT.Copy, scale=xrs[:, t:t + 1]).then_inc(s_xn, 1)
            act.wait_ge(s_bvp, 1)
            nc.scalar.activation(bvs[:, 0:512], ps[6][0:16, 0:512], ACT.Copy).then_inc(s_bvs, 1)
            nc.scalar.activation(bvs[:, 512:BV], ps[7][0:16, 0:BV - 512], ACT.Copy).then_inc(s_bvs, 1)
            act.wait_ge(s_bvs, 2)
            act.dma_start(bvd, bvs[:, :]).then_inc(s_bvd, 16)
            act.wait_ge(s_bvd, 16)

            def h_chunk(kk, hbuf, a_col, s_col, tp, hfs, lo_s, n_lo, banks):
                act.wait_ge(tp, kk + 1)
                if kk >= 2:
                    act.wait_ge(lo_s, n_lo + kk - 1)
                nc.scalar.activation(hbuf[:, kk % 2, :], banks[kk % len(banks)][:, :], ACT.Identity,
                                     bias=s_col, scale=a_col).then_inc(hfs, 1)

            for kk in range(KD):
                act.wait_ge(s_mod, kk // 4 + 1)
                h_chunk(kk, hf, am[:, kk:kk + 1], modm[:, kk, 1:2], s_htp, s_hf, s_hlo, 0, ps[0:4])

            def high(w, slot, landed):
                act.wait_ge(s_raw[slot], landed)
                nc.scalar.activation(whi[:, slot, :], raw[:, slot, :], ACT.Copy).then_inc(s_hi, 1)

            def high_w(w):
                if w >= 4:
                    act.wait_ge(s_mm, w - 3)
                high(w, SLOT[w], raw_count(w))

            for w in range(4):
                high_w(w)
            act.wait_ge(s_gl, 16)
            nc.scalar.activation(glh[:, :, :], glr[:, :, :], ACT.Copy).then_inc(s_glh, 1)

            high_w(4)
            act.wait_ge(s_mm, W_QB)
            act.wait_ge(s_hlo, KD)
            for kv in range(2):
                nc.scalar.activation(kcE[:, kv, :, :], ps[4 + kv][:, :].rearrange("p (m r) -> p r m", r=2),
                                     ACT.Copy).then_inc(s_kvE, 1)
            act.wait_ge(s_kvE, 2)
            for g in range(2):
                for r in range(2):
                    act.dma_start(Kst[64 * r:64 * r + 64, :, g, :], kcE[64 * g:64 * g + 64, :, r, :]
                                  ).then_inc(s_kst, 32)
            high_w(5)

            def evac(blk, t):
                if t < T - 1:
                    act.wait_ge(s_pj, 3 * blk + t + 1)
                else:
                    act.wait_ge(s_mm, W_QB + 4 * blk + 4)

            def square(q, src, width):
                if q >= 2:
                    act.wait_ge(s_ssr, q - 1)
                return nc.scalar.activation(sq[:, q % 2, 0:width], src, ACT.Square)

            def normed_block(blk, b, width, v_dst):
                if b >= 2:
                    act.wait_ge(s_tp, {2: 4, 3: 7}[b])
                for t in range(T):
                    evac(blk, t)
                    nc.scalar.activation(nat[:, b % 2, t, 0:width], ps[t][:, 0:width], ACT.Copy)
                    if v_dst is not None:
                        nc.scalar.activation(v_dst[:, t, :], ps[t][:, width:512], ACT.Copy)
                    square(4 * b + t, ps[t][:, 0:width], width).then_inc(s_ev, 1)
                h = width // DH
                act.wait_ge(s_ssr, 4 * b + 4)
                nc.scalar.activation(stb[:, b, 0:T * h], ssb[:, b, 0:T * h], ACT.Sqrt, bias=eps[:, :],
                                     scale=1.0 / DH).then_inc(s_std, 1)

            def evac_tp(n):
                kind, j = TP[n]
                bank = ps[4 + n % 2]
                act.wait_ge(s_tp, n + 1)
                if kind == "q":
                    g = gq[:, 0:1] if j >= 4 else gq[:, 1:2]
                    i = nc.scalar.activation(QT[:, j, :], bank[:, :], ACT.Copy, scale=g)
                elif kind in ("k", "kb"):
                    gi = C_GAIN + (G_KA if kind == "k" else G_KSL + j - 4)
                    i = nc.scalar.activation(KT[:, j, :], bank[:, :], ACT.Copy, scale=par[:, gi:gi + 1])
                elif kind == "gtm":
                    i = nc.scalar.activation(gtm[:, 512 * j:512 * j + 512], bank[:, :], ACT.Copy)
                elif kind == "col":
                    i = nc.scalar.activation(modf[:, 4 * (j - 2):4 * (j - 2) + 4], bank[:, 0:4], ACT.Copy)
                else:
                    act.wait_ge(s_vz, 1)
                    for t in range(T):
                        r = slice(32 * t, 32 * t + 32)
                        i = nc.scalar.activation(Vbd[r, :, t, :], bank[r, 0:128].rearrange("p (g d) -> p g d", g=2),
                                                 ACT.Copy)
                i.then_inc(s_tpev, 1)

            for w in (6, 7, 8):
                high_w(w)
            normed_block(0, 0, 512, None)
            high_w(9)
            act.wait_ge(s_hid, 1)
            nc.scalar.activation(hidk[:, :, :], ps[6][:, 0:128].rearrange("p (h n) -> p h n", h=2),
                                 ACT.Gelu_apprx_tanh).then_inc(s_gelu, 1)
            for w in (10, 11, 12):
                high_w(w)
            normed_block(1, 1, 256, VB)
            high_w(13)
            act.wait_ge(s_gq, 1)
            for n in range(5):
                evac_tp(n)
            act.wait_ge(s_kcp, 1)
            kc_ps = ps[7][0:NC, 0:128].rearrange("p (g d) -> p g d", g=2)
            nc.scalar.activation(kcn[:, :, :], kc_ps, ACT.Copy)
            nc.scalar.activation(kcq[:, :, :], kc_ps, ACT.Square).then_inc(s_kce, 1)
            act.wait_ge(s_kcr, 1)
            nc.scalar.activation(kcs[:, 1, :], kcs[:, 0, :], ACT.Sqrt, bias=eps[0:NC, :], scale=1.0 / DH
                                 ).then_inc(s_kcst, 1)
            act.wait_ge(s_glp, 1)
            act.wait_ge(s_R, 4)
            nc.scalar.activation(glT[:, :], ps[6][0:24, :], ACT.Copy).then_inc(s_glT, 1)
            for w in (14, 15, 16):
                high_w(w)
            normed_block(2, 2, 512, None)
            high_w(17)
            act.wait_ge(s_gltp, 1)
            nc.scalar.activation(G[:, :, :], ps[6][:, 0:96].rearrange("p (t c) -> p c t", t=T),
                                 ACT.Sigmoid).then_inc(s_sig, 1)
            for n in range(5, 9):
                evac_tp(n)
            act.wait_ge(s_kctp, 1)
            act.wait_ge(s_kcz, 1)
            for g in range(2):
                h = slice(64 * g, 64 * g + 64)
                nc.scalar.activation(kcT[h, g, :], ps[7][h, 256:288], ACT.Copy,
                                     scale=par[h, C_GAIN + G_KCMP:C_GAIN + G_KCMP + 1]).then_inc(s_kcT, 1)
            act.wait_ge(s_hid, 2)
            nc.scalar.activation(hidv[:, :, :, :, :].rearrange("p h g t n -> p (h g) t n"),
                                 view(ps[6][:, 0:128], [[NC, 4], [0, T], [1, NC]]),
                                 ACT.Gelu_apprx_tanh).then_inc(s_gelu, 1)
            for w in (18, 19, 20):
                high_w(w)
            act.wait_ge(s_cm, 1)
            nc.scalar.activation(cm[:, :, :], cm[:, :, :], ACT.Exp).then_inc(s_cex, 1)
            normed_block(3, 3, 512, None)
            high_w(21)
            for n in range(9, 16):
                evac_tp(n)
            for w in (22, 23, 24):
                high_w(w)
            for t in range(T):
                evac(4, t)
                nc.scalar.activation(VA[:, t, :], ps[t][:, :], ACT.Copy).then_inc(s_ev, 1)
            high_w(25)
            for n in range(16, len(TP)):
                evac_tp(n)

            for p in range(4):
                act.wait_ge(s_mct, p + 1)
                nc.scalar.activation(mf[:, 4 + p, :], ps[4 + p][:, :], ACT.Copy).then_inc(s_mcte, 1)

            def high_part(src, j, hi):
                nc.scalar.activation(hp[:, hi, :], src[:, bass.ds(j, 1), :].rearrange("p o n -> p (o n)"), ACT.Copy
                                     ).then_inc(s_qkh, 1)

            def qk_high(u):
                high_part(KT, u, 4 * u + 1)
                high_part(QT, u, 4 * u)

            def k_high_nsa():
                for a in range(2):
                    act.wait_ge(s_stg[a], STG * N_A)
                for br in range(2):
                    high_part(KT, 4 + br, N_KP + 2 * br)

            def q_high_nsa(r, staged):
                for a in range(2):
                    act.wait_ge(s_stg[a], staged)
                act.sem_inc(s_begun)
                high_part(QT, r + 4, N_QP)

            def v_high(a, V, col):
                nc.scalar.activation(VS[:, a, :, 0:DH], V[:, :, bass.ds(col, DH)], ACT.Copy).then_inc(s_vh, 1)

            def exp(H, a, tiles):
                for t in tiles:
                    act.wait_ge(s_L, 4 * H + (t + 1))
                    l_ = L[:, a, L_AT[t]:L_AT[t] + P * (t + 1)]
                    c_ = 4 * a + t
                    nc.scalar.activation(l_, l_, ACT.Exp, bias=nmx[:, c_:c_ + 1], scale=-1.0,
                                         accum_out=sums[:, c_:c_ + 1]).then_inc(s_E, 1)

            def move(H, a, out):
                act.wait_ge(s_PV, H + 2)
                act.wait_ge(s_cb, out + 1)
                o_ = slice(64 - 64 * a, 128 - 64 * a)
                nc.scalar.activation(tmp[64 * a:64 * a + 64, :], ps[6 + a][o_, :], ACT.Copy).then_inc(s_tmp, 1)

            def half(H, a, v_next, prev=None, scores=True):
                act.wait_ge(s_PV, H + 1)
                for t in range(T):
                    act.wait_ge(s_T, 4 * H + (t + 1))
                    nc.scalar.activation(PThi[:, 0:t + 1, P * t:P * t + P],
                                         ps[4 + t % 2][:, 0:P * (t + 1)].rearrange("p (j q) -> p j q", q=P),
                                         ACT.Copy).then_inc(s_Phi, 1)
                    if t == 1 and v_next is not None:
                        exp(H + 1, 1 - a, (3,))
                if v_next is not None:
                    v_high(1 - a, *v_next)
                if prev is not None:
                    move(H - 1, 1 - a, prev)
                if scores:
                    exp(H + 2, a, (0, 1, 2))

            act.wait_ge(s_ach, 2 * 32)
            qk_high(0)
            qk_high(1)
            act.wait_ge(s_mcte, 4)
            v_high(0, VA, 0)
            exp(0, 0, range(T))
            exp(1, 1, (0, 1, 2))
            for u in range(N_A):
                half(2 * u, 0, (VA, 128 * u + 64), prev=2 * u - 1 if u else None)
                if u < 2:
                    qk_high(u + 2)
                elif u == 2:
                    k_high_nsa()
                half(2 * u + 1, 1, (VA, 128 * u + 128) if u < 3 else (VB, 0), prev=2 * u)
                if u == 2:
                    q_high_nsa(0, STG * (N_A - 1))
            with act.Fori(0, 3) as i:
                for br in range(2):
                    half(4 * i + (2 * N_A + 2 * br), 0, (VB, 128 * br + 64),
                         prev=None if br else 2 * i + (2 * N_A - 1))
                    if br == 0:
                        q_high_nsa(i + 1, STGN * i + (STG * N_A + STGN))
                    half(4 * i + (2 * N_A + 2 * br + 1), 1, (VB, 128 - 128 * br), prev=2 * i + 2 * N_A if br else None)
            for br in range(2):
                for a in range(2):
                    half(2 * N_A + 12 + 2 * br + a, a, (VB, (128 * br + 64) if a == 0 else 128) if br + a < 2 else None,
                         prev={(0, 0): 2 * N_A + 5, (1, 1): 2 * N_A + 6}.get((br, a)), scores=br == 0)
            move(2 * N_A + 15, 1, 2 * N_A + 7)

            act.wait_ge(s_cb, 4 * N_A + 2)
            for kk in range(KD):
                nc.scalar.activation(mhi[:, kk, :], mf[:, kk, :], ACT.Copy).then_inc(s_mhi, 1)
            for w in range(26, 34):
                high_w(w)
            for t in range(T):
                act.wait_ge(s_x1, T + t + 1)
                nc.scalar.activation(xn2[:, t, :], x1[:, t, :], ACT.Square,
                                     accum_out=xss[:, T + t:T + t + 1]).then_inc(s_x1sq, 1)
            act.wait_ge(s_x1sq, T)
            nc.scalar.activation(xst[:, :], xss[:, T:2 * T], ACT.Sqrt, bias=eps[:, :], scale=1.0 / D
                                 ).then_inc(s_x2st, 1)
            act.wait_ge(s_modf, 1)
            for kk in range(KD):
                h_chunk(kk, hf2, af[:, kk:kk + 1], modfb[:, kk:kk + 1], s_h2tp, s_hf2, s_h2lo, 0, ps[4:6])

            with act.Fori(0, NF // 2) as i:
                for jj in range(2):
                    for r in range(2):
                        w0 = W_GU + 4 + 2 * jj + r
                        act.wait_ge(s_mm, 4 * i + (w0 - 3))
                        high(None, SLOT[w0], 16 * i + raw_count(w0))
                    act.wait_ge(s_mm, 4 * i + (W_GU + 2 * jj + 2))
                    act.wait_ge(s_prod, 2 * i + (jj + 1))
                    nc.scalar.activation(sil[:, jj, :], ps[2 * jj][:, :], ACT.Silu).then_inc(s_sil, 1)
            with act.Fori(0, 4) as i:
                for r in range(4):
                    w0 = W_DN + 4 + r
                    act.wait_ge(s_mm, 4 * i + (w0 - 3))
                    high(None, SLOT[w0], 16 * i + raw_count(w0))
            for w in range(W_DN + 20, N_W):
                high_w(w)
            for dt in range(KD):
                if dt % 2:
                    act.wait_ge(s_dn, dt + 1)
                    nc.scalar.activation(yT[:, dt, :], ps[dt][:, :], ACT.Copy, scale=modfb[:, 16 + dt:17 + dt]
                                         ).then_inc(s_yT, 1)

        @block.vector
        def _(dve):
            chain = [0]

            def link(ins):
                chain[0] += 1
                ins.then_inc(s_dch, 1)
                dve.wait_ge(s_dch, chain[0])

            dve.wait_ge(s_par, 16)
            nc.vector.tensor_scalar(gq[:, 0:1], par[:, C_GAIN + G_QB:C_GAIN + G_QB + 1], SCALE, None, ALU.mult)
            nc.vector.tensor_scalar(gq[:, 1:2], par[:, C_GAIN + G_QA:C_GAIN + G_QA + 1], SCALE, None, ALU.mult
                                    ).then_inc(s_gq, 1)
            def split(kk, hbuf, hi_t, lo_t, hfs, his, los):
                dve.wait_ge(hfs, kk + 1)
                nc.vector.tensor_copy(hi_t[:, kk, :], hbuf[:, kk % 2, :]).then_inc(his, 1)
                dve.wait_ge(his, kk + 1)
                nc.vector.tensor_tensor(lo_t[:, kk, :], hbuf[:, kk % 2, :], hi_t[:, kk, :].bitcast(F32),
                                        ALU.subtract).then_inc(los, 1)

            echain = [0]

            def early(e):
                j, cp = divmod(e, 4)
                dve.wait_ge(s_raw[e % 4], 16 * (e // 4 + 1))
                a_ = eacc[j]
                for c in range(2):
                    w_ = raw[:, e % 4, 512 * c:512 * c + 512]
                    s_ = silc[:, 2 * cp + c:2 * cp + c + 1]
                    if cp == 0 and c == 0:
                        i = nc.vector.tensor_scalar(a_, w_, s_, None, ALU.mult)
                    else:
                        dve.wait_ge(s_each, echain[0])
                        i = nc.vector.scalar_tensor_tensor(a_, w_, s_, a_, ALU.mult, ALU.add)
                    echain[0] += 1
                    i.then_inc(s_each, 1)

            def modulation(hf_):
                dve.wait_ge(s_adamm, hf_ + 1)
                k4 = slice(4 * hf_, 4 * hf_ + 4)
                link(nc.vector.tensor_tensor(modm[:, k4, :], ps[6 + hf_][:, 0:8].rearrange("p (k g) -> p k g", g=2),
                                             par[:, C_BM + 8 * hf_:C_BM + 8 * hf_ + 8]
                                             .rearrange("p (k g) -> p k g", g=2), ALU.add))
                nc.vector.scalar_tensor_tensor(am[:, k4], modm[:, k4, 0:1].rearrange("p k o -> p (k o)"), 1.0,
                                               par[:, C_GM + 4 * hf_:C_GM + 4 * hf_ + 4], ALU.add, ALU.mult
                                               ).then_inc(s_mod, 1)

            dve.wait_ge(s_silc, 1)
            early(0)
            early(1)
            dve.wait_ge(s_xst, 1)
            nc.vector.reciprocal(xrs[:, :], xst[:, :]).then_inc(s_xrs, 1)
            for e in range(2, 9):
                early(e)
            modulation(0)
            for e in range(9, N_EARLY):
                early(e)
                if e % 2 == 0:
                    split(e // 2 - 5, hf, h1hi, h1lo, s_hf, s_hhi, s_hlo)
            modulation(1)
            for kk in range(3, KD):
                split(kk, hf, h1hi, h1lo, s_hf, s_hhi, s_hlo)
            dve.wait_ge(s_glh, 1)
            nc.vector.tensor_tensor(gll[:, :, :], glr[:, :, :], glh[:, :, :].bitcast(F32), ALU.subtract
                                    ).then_inc(s_gll, 1)

            achain = [0]

            def late(k):
                j, cp = divmod(k, 4)
                dve.wait_ge(s_r2[k % 4], 16 * (k // 4 + 1))
                a_ = acc[j]
                for c in range(2):
                    w_ = ring2[:, k % 4, 512 * c:512 * c + 512]
                    s_ = silc[:, 2 * cp + c:2 * cp + c + 1]
                    if cp == 0 and c == 0:
                        i = nc.vector.tensor_scalar(a_, w_, s_, None, ALU.mult)
                    else:
                        dve.wait_ge(s_ach, achain[0])
                        i = nc.vector.scalar_tensor_tensor(a_, w_, s_, a_, ALU.mult, ALU.add)
                    achain[0] += 1
                    i.then_inc(s_ach, 1)

            def norm_block(b, h):
                for t in range(T):
                    q = 4 * b + t
                    dve.wait_ge(s_ev, {0: 0, 1: 4, 2: 8, 3: 12}[b] + t + 1)
                    nc.vector.tensor_reduce(ssb[:, b, t * h:t * h + h],
                                            sq[:, q % 2, 0:64 * h].rearrange("p (h d) -> p h d", d=DH), AXX, ALU.add
                                            ).then_inc(s_ssr, 1)
                dve.wait_ge(s_std, b + 1)
                link(nc.vector.reciprocal(rsb[:, b, 0:T * h], stb[:, b, 0:T * h]))
                v = nat[:, b % 2, :, 0:64 * h].rearrange("p t (h d) -> p t h d", d=DH)
                nc.vector.tensor_tensor(v, v, view(rsb[:, b, 0:1], [[h, T], [1, h], [0, DH]]), ALU.mult
                                        ).then_inc(s_nrm, 1)

            def lates(a, b):
                for k in range(a, b):
                    late(k)

            lates(0, 6)
            norm_block(0, 8)
            lates(6, 14)
            norm_block(1, 4)
            dve.wait_ge(s_kce, 1)
            nc.vector.tensor_reduce(kcs[:, 0, :], kcq[:, :, :], AXX, ALU.add).then_inc(s_kcr, 1)
            dve.wait_ge(s_kcst, 1)
            link(nc.vector.reciprocal(kcs[:, 2, :], kcs[:, 1, :]))
            nc.vector.tensor_tensor(kcn[:, :, :], kcn[:, :, :], view(kcs[:, 2, 0:1], [[1, 2], [0, DH]]), ALU.mult
                                    ).then_inc(s_kcn, 1)
            lates(14, 22)
            norm_block(2, 8)
            dve.wait_ge(s_sig, 1)
            dve.wait_ge(s_shp, 16)
            link(nc.vector.tensor_tensor(gv[:, :, :], G[:, 0:8, :],
                                         view(shp[:, S_VALID:S_VALID + 1], [[0, 8], [1, T]]), ALU.mult))
            lates(22, 30)
            dve.wait_ge(s_csc, 2)
            mask = view(shp[:, S_MASK:S_MASK + 1], [[NC, T], [0, 2], [1, NC]])
            for p in range(4):
                i = nc.vector.tensor_tensor(view(cm[:, 4 * p:4 * p + 1, :], [[NC, T], [16 * NC, 2], [1, NC]]),
                                            view(ps[6 + p // 2][:, 256 * (p % 2):256 * (p % 2) + 1],
                                                 [[2 * NC, T], [NC, 2], [1, NC]]), mask, ALU.add)
            link(i)
            link(nc.vector.tensor_reduce(cst[:, 0, :], cm[:, :, :], AXX, ALU.max))
            nc.vector.tensor_tensor(cm[:, :, :], cm[:, :, :], view(cst[:, 0, 0:1], [[1, 32], [0, NC]]),
                                    ALU.subtract).then_inc(s_cm, 1)
            dve.wait_ge(s_cex, 1)
            link(nc.vector.tensor_reduce(cst[:, 1, :], cm[:, :, :], AXX, ALU.add))
            link(nc.vector.reciprocal(cst[:, 2, :], cst[:, 1, :]))
            link(nc.vector.tensor_tensor(cst[:, 3, :].rearrange("p (a q t) -> p a q t", a=2, t=T),
                                         cst[:, 2, :].rearrange("p (a q t) -> p a q t", a=2, t=T),
                                         view(gv[:, 0:1, 0:1], [[T, 2], [2 * T, 4], [1, T]]), ALU.mult))
            norm_block(3, 8)
            lates(30, 32)
            dve.wait_ge(s_cpt, 2)
            for b in range(2):
                nc.vector.tensor_copy(PcT[:, 4 * b:4 * b + 4, :].rearrange("p r q -> p (r q)"), ps[6 + b][:, :]
                                      ).then_inc(s_cpte, 1)
            for p in range(4):
                dve.wait_ge(s_pvc, p + 1)
                nc.vector.tensor_tensor(
                    mixc[:, :, 128 * p:128 * p + 128].rearrange("p t (a d) -> p a t d", a=2),
                    ps[p][:, :].rearrange("p (a t d) -> p a t d", a=2, t=T),
                    view(cst[:, 3, 4 * p:4 * p + 1], [[16, 2], [1, T], [0, DH]]), ALU.mult).then_inc(s_mixc, 1)

            def logits(H, a, staged, tiles=range(T), first=False):
                dve.wait_ge(s_stg[a], staged)
                for t in tiles:
                    w = P * (t + 1)
                    dve.wait_ge(s_S, 4 * H + (t + 1))
                    if not first:
                        dve.wait_ge(s_T, 4 * H + (t - 7))
                    dve.sem_inc(s_begun)
                    b_ = bias[:, a, 0:w][:, ::-1]
                    nc.vector.tensor_tensor_reduce(out=L[:, a, L_AT[t]:L_AT[t] + w], in0=ps[t][:, 0:w], in1=b_,
                                                   scale=-1.0, scalar=3e38, op0=ALU.add, op1=ALU.min,
                                                   accum_out=nmx[:, 4 * a + t:4 * a + t + 1]).then_inc(s_L, 1)

            def factors(H, a, gate):
                dve.wait_ge(s_E, 4 * H + 4)
                dve.sem_inc(s_begun)
                if isinstance(gate, str):
                    nc.vector.reciprocal(rg[:, a, :], sums[:, 4 * a:4 * a + 4]).then_inc(s_rg, 1)
                else:
                    nc.vector.reciprocal(rec[:, a, :], sums[:, 4 * a:4 * a + 4]).then_inc(s_rch, 1)
                    dve.wait_ge(s_rch, H - (2 * N_A - 1))
                    nc.vector.tensor_tensor(rg[:, a, :], rec[:, a, :],
                                            G[:, bass.ds(gate, 1), :].rearrange("p o t -> p (o t)"), ALU.mult
                                            ).then_inc(s_rg, 1)

            def add_up(H, a, out, pair, onto=True):
                h = slice(64 * a, 64 * a + 64)
                m = mf[h, bass.ds(pair, 1), :].rearrange("p o n -> p (o n)")
                dve.wait_ge(s_tmp, out + 1)
                dve.wait_ge(s_PV, H + 2)
                dve.sem_inc(s_begun)
                if onto:
                    nc.vector.tensor_tensor(m, ps[6 + a][h, :], m, ALU.add).then_inc(s_own, 1)
                    dve.wait_ge(s_own, out - (2 * N_A - 2))
                    nc.vector.tensor_tensor(m, tmp[h, :], m, ALU.add).then_inc(s_cb, 1)
                else:
                    nc.vector.tensor_tensor(m, ps[6 + a][h, :], tmp[h, :], ALU.add).then_inc(s_cb, 1)

            def half(H, a, gate, staged=None, prev=None):
                for t in range(T):
                    dve.wait_ge(s_Phi, 4 * H + (t + 1))
                    hi = PThi[:, 0:t + 1, P * t:P * t + P].bitcast(F32)
                    nc.vector.tensor_tensor(PTlo[:, 0:t + 1, P * t:P * t + P],
                                            ps[4 + t % 2][:, 0:P * (t + 1)].rearrange("p (j q) -> p j q", q=P),
                                            hi, ALU.subtract).then_inc(s_Plo, 1)
                    if t == 1 and staged is not None:
                        logits(H + 2, a, staged, (0, 1))
                    if t == 2 and gate is not None:
                        factors(H + 1, 1 - a, gate)
                if staged is not None:
                    logits(H + 2, a, staged, (2, 3))
                if prev is not None:
                    add_up(H - 1, 1 - a, *prev)

            dve.wait_ge(s_mcte, 4)
            nc.vector.memset(mf[64:128, N_A - 1, :], 0.0).then_inc(s_mfz, 1)
            nc.vector.memset(nmx[:, :], 0.0).then_inc(s_cb, 2)
            nc.vector.memset(rec[:, :, :], 0.0).then_inc(s_Plo, 2)
            nc.vector.memset(rg[:, :, :], 0.0).then_inc(s_PV, 1)
            dve.wait_ge(s_cb, 2)
            dve.wait_ge(s_Plo, 2)
            dve.wait_ge(s_PV, 1)
            dve.wait_ge(s_mfz, 1)
            MOBA = "no gate"
            logits(0, 0, STG, first=True)
            logits(1, 1, STG, first=True)
            factors(0, 0, MOBA)
            for u in range(N_A):
                staged = STG * (u + 2) if u < 3 else STG * N_A + STGN
                half(2 * u, 0, MOBA, staged, (2 * u - 1, u - 1, False) if u else None)
                half(2 * u + 1, 1, MOBA if u < 3 else 8, staged, (2 * u, u, False))
            with dve.Fori(0, 3) as i:
                for br in range(2):
                    staged = STGN * i + (STG * N_A + STGN * (1 + br))
                    half(4 * i + (2 * N_A + 2 * br), 0, 2 * i + (9 + 8 * br), staged,
                         None if br else (2 * i + (2 * N_A - 1), i + 3))
                    half(4 * i + (2 * N_A + 2 * br + 1), 1, 2 * i + (16 - 6 * br), staged,
                         (2 * i + 2 * N_A, i + 4) if br else None)
            for br in range(2):
                for a in range(2):
                    half(2 * N_A + 12 + 2 * br + a, a, ((15, 22), (23, None))[br][a],
                         STG * N_A + 4 * STGN if br == 0 else None,
                         {(0, 0): (2 * N_A + 5, 6), (1, 1): (2 * N_A + 6, 7)}.get((br, a)))
            add_up(2 * N_A + 15, 1, 2 * N_A + 7, 7)

            for kk in range(KD):
                dve.wait_ge(s_mhi, kk + 1)
                nc.vector.tensor_tensor(mlo[:, kk, :], mf[:, kk, :], mhi[:, kk, :].bitcast(F32), ALU.subtract
                                        ).then_inc(s_mlo, 1)
            dve.wait_ge(s_tpev, len(TP))
            link(nc.vector.tensor_tensor(modfb[:, :], modf[:, :], par[:, C_BF:C_BF + 24], ALU.add))
            nc.vector.scalar_tensor_tensor(af[:, :], modfb[:, 8:16], 1.0, par[:, C_GF:C_GF + KD], ALU.add, ALU.mult
                                           ).then_inc(s_modf, 1)
            dve.wait_ge(s_x1in, 16)
            for h in range(2):
                for t in range(T):
                    q = T * h + t
                    c_ = slice(512 * h, 512 * h + 512)
                    if t < T - 1:
                        dve.wait_ge(s_op, 3 * h + t + 1)
                    else:
                        dve.wait_ge(s_mm, W_OUT + 4 * h + 4)
                    if q >= 2:
                        dve.wait_ge(s_x1, q - 1)
                    nc.vector.tensor_tensor(ob[:, q % 2, :], ps[4 + t][:, :], gtm[:, c_], ALU.mult
                                            ).then_inc(s_ot, 1)
                    dve.wait_ge(s_ot, q + 1)
                    nc.vector.tensor_tensor(x1[:, t, c_], x1[:, t, c_], ob[:, q % 2, :], ALU.add).then_inc(s_x1, 1)
            dve.wait_ge(s_x2st, 1)
            link(nc.vector.reciprocal(xrs[:, :], xst[:, :]))
            for t in range(T):
                nc.vector.tensor_scalar(xn2[:, t, :], x1[:, t, :], xrs[:, t:t + 1], None, ALU.mult).then_inc(s_xn2, 1)
            for kk in range(KD):
                split(kk, hf2, mhi, mlo, s_hf2, s_h2hi, s_h2lo)

            nc.vector.memset(sil[:, 0, 0:1], 0.0).then_inc(s_prod, 2)
            nc.vector.memset(actf[:, 0, 0:1], 0.0).then_inc(s_alo, 2)
            with dve.Fori(0, NF // 2) as i:
                for jj in range(2):
                    dve.wait_ge(s_sil, 2 * i + (jj + 1))
                    dve.wait_ge(s_alo, 2 * i + (jj + 1))
                    nc.vector.tensor_tensor(actf[:, jj, :], ps[2 * jj + 1][:, :], sil[:, jj, :], ALU.mult
                                            ).then_inc(s_prod, 1)
                    dve.wait_ge(s_prod, 2 * i + (jj + 3))
                    a_ = ahi[:, bass.ds(2 * i + jj, 1), :].rearrange("p o n -> p (o n)")
                    nc.vector.tensor_copy(a_, actf[:, jj, :]).then_inc(s_ahi, 1)
                    dve.wait_ge(s_ahi, 2 * i + (jj + 1))
                    nc.vector.tensor_tensor(alo[:, bass.ds(2 * i + jj, 1), :].rearrange("p o n -> p (o n)"),
                                            actf[:, jj, :], a_.bitcast(F32), ALU.subtract).then_inc(s_alo, 1)
            for dt in range(KD):
                if dt % 2 == 0:
                    dve.wait_ge(s_dn, dt + 1)
                    nc.vector.tensor_scalar(yT[:, dt, :], ps[dt][:, :], modfb[:, 16 + dt:17 + dt], None, ALU.mult
                                            ).then_inc(s_nrm, 1)
            for t in range(T):
                for h in range(2):
                    dve.wait_ge(s_ytp, 2 * t + h + 1)
                    nc.vector.tensor_tensor(yo[:, t, 512 * h:512 * h + 512], ps[2 * t + h][:, :],
                                            x1[:, t, 512 * h:512 * h + 512], ALU.add).then_inc(s_yo, 1)

        @block.tensor
        def _(pe):
            PASSES = ((0, 0), (0, 1), (1, 0))
            W2 = (whi, wlo)

            pe.wait_ge(s_rel, 48)
            nc.tensor.matmul(ps[6][0:16, 0:512], rel_s[:, :], oneh_s[:, 0:512], start=True, stop=True)
            nc.tensor.matmul(ps[7][0:16, 0:BV - 512], rel_s[:, :], oneh_s[:, 512:BV], start=True, stop=True
                             ).then_inc(s_bvp, 1)
            pe.wait_ge(s_shp, 16)
            pe.wait_ge(s_xn, T)

            def x_chunk(kk):
                if kk >= 4:
                    pe.wait_ge(s_hf, kk - 3)
                for t in range(T):
                    mm = nc.tensor.transpose(ps[kk % 4][:, P * t:P * t + P], xn[:, t, P * kk:P * kk + P], ident)
                mm.then_inc(s_htp, 1)

            for kk in range(4):
                x_chunk(kk)
            pe.wait_ge(s_bvs, 2)
            for hf_ in range(2):
                pe.wait_ge(s_each, 16 * (hf_ + 1))
                for q in range(4):
                    for g in range(2):
                        mm = nc.tensor.matmul(ps[6 + hf_][:, 2 * q + g:2 * q + g + 1],
                                              eacc[2 * hf_ + g][:, P * q:P * q + P], ones[:, 0:1],
                                              start=True, stop=True)
                mm.then_inc(s_adamm, 1)
                if hf_ == 0:
                    for kk in range(4, KD):
                        x_chunk(kk)

            H1 = (h1hi, h1lo)
            for w in range(W_T, W_QB):
                pe.wait_ge(s_hlo, 4 * w + 4)
                pe.wait_ge(s_lo, w + 1)
                for kv in range(2):
                    for k4 in range(4):
                        kk = 4 * w + k4
                        for i, (s, m) in enumerate(PASSES):
                            mm = nc.tensor.matmul(ps[4 + kv][:, :],
                                                  W2[s][:, SLOT[w], 256 * k4 + P * kv:256 * k4 + P * kv + P],
                                                  H1[m][:, kk, :], start=(kk == 0 and i == 0),
                                                  stop=(kk == KD - 1 and i == 2))
                mm.then_inc(s_mm, 1)

            def natural(w0, blk, acts, banks, out_sem, ev=None, split=None):
                for r in range(4):
                    pe.wait_ge(s_lo, w0 + r + 1)
                    if split is not None:
                        pe.wait_ge(split, 2 * r + 2)
                    for t in range(T):
                        if r == 0 and ev is not None:
                            ev(t)
                        for k2 in range(2):
                            kk = 2 * r + k2
                            for i, (s, m) in enumerate(PASSES):
                                mm = nc.tensor.matmul(banks[t][:, :], acts[s][:, kk, P * t:P * t + P],
                                                      W2[m][:, SLOT[w0 + r], 512 * k2:512 * k2 + 512],
                                                      start=(kk == 0 and i == 0), stop=(kk == KD - 1 and i == 2))
                        if r == 3 and t < T - 1:
                            mm.then_inc(out_sem, 1)
                    mm.then_inc(s_mm, 1)

            def evacuated(blk):
                def f(t):
                    if blk:
                        pe.wait_ge(s_ev, 4 * (blk - 1) + t + 1)
                return f

            def tp(n):
                kind, j = TP[n]
                bank = ps[4 + n % 2]
                if n >= 2:
                    pe.wait_ge(s_tpev, n - 1)
                else:
                    pe.wait_ge(s_kvE, 2)
                if kind in ("q", "k", "kb"):
                    half = 0 if kind == "q" else 1
                    pe.wait_ge(s_nrm, {("q", True): 1, ("kb", True): 2, ("q", False): 3, ("k", False): 4}[kind, j >= 4])
                    c = P * (j % 4)
                    for t in range(T):
                        mm = nc.tensor.transpose(bank[:, P * t:P * t + P], nat[:, half, t, c:c + P], ident)
                elif kind == "gtm":
                    pe.wait_ge(s_ach, 8 * (j + 1))
                    pe.wait_ge(s_brow, 16)
                    nc.tensor.matmul(bank[:, :], ones, acc[j], start=True, stop=False)
                    mm = nc.tensor.matmul(bank[:, :], ones[0:1, :], brow_s[0:1, 512 * j:512 * j + 512],
                                          start=False, stop=True)
                elif kind == "col":
                    pe.wait_ge(s_ach, 8 * (j + 1))
                    for q in range(4):
                        mm = nc.tensor.matmul(bank[:, q:q + 1], acc[j][:, P * q:P * q + P], ones[:, 0:1],
                                              start=True, stop=True)
                else:
                    pe.wait_ge(s_gelu, 2)
                    for g in range(2):
                        for ht in range(2):
                            mm = nc.tensor.matmul(bank[:, DH * g:DH * g + DH],
                                                  hidv[:, ht, g, :, :].rearrange("p t n -> p (t n)"),
                                                  w2s[:, 1, ht, :], start=(ht == 0), stop=(ht == 1))
                mm.then_inc(s_tp, 1)

            def hidden(kv):
                pe.wait_ge(s_w1, 16 * (kv + 1))
                pe.wait_ge(s_R, 4)
                if kv == 1:
                    pe.wait_ge(s_sig, 1)
                for ht in range(2):
                    for c in range(CL // 2):
                        mm = nc.tensor.matmul(ps[6][:, 64 * ht:64 * ht + 64], w1s[:, c, P * ht:P * ht + P],
                                              R[:, kv, c, :, :].rearrange("p g n -> p (g n)"),
                                              start=(c == 0), stop=(c == CL // 2 - 1))
                mm.then_inc(s_hid, 1)

            natural(W_QB, 0, H1, ps, s_pj, evacuated(0))
            hidden(0)
            natural(W_KV, 1, H1, ps, s_pj, evacuated(1))
            for n in range(5):
                tp(n)
            pe.wait_ge(s_gelu, 1)
            pe.wait_ge(s_w2, 16)
            for g in range(2):
                for ht in range(2):
                    mm = nc.tensor.matmul(ps[7][0:NC, DH * g:DH * g + DH], hidk[:, ht, NC * g:NC * g + NC],
                                          w2s[:, 0, ht, :], start=(ht == 0), stop=(ht == 1))
            mm.then_inc(s_kcp, 1)
            pe.wait_ge(s_gll, 1)
            for kk in range(KD):
                for i, (s, m) in enumerate(PASSES):
                    mm = nc.tensor.matmul(ps[6][0:24, :], (glh, gll)[s][:, kk, :], H1[m][:, kk, :],
                                          start=(kk == 0 and i == 0), stop=(kk == KD - 1 and i == 2))
            mm.then_inc(s_glp, 1)
            natural(W_QA, 2, H1, ps, s_pj, evacuated(2))
            pe.wait_ge(s_glT, 1)
            for t in range(T):
                mm = nc.tensor.transpose(ps[6][:, 24 * t:24 * t + 24], glT[:, P * t:P * t + P], ident[0:24, 0:24])
            mm.then_inc(s_gltp, 1)
            for n in range(5, 9):
                tp(n)
            pe.wait_ge(s_kcn, 1)
            nc.tensor.transpose(ps[7][:, 256:288], kcn[:, :, :].rearrange("p g d -> p (g d)"), ident[0:NC, 0:NC]
                                ).then_inc(s_kctp, 1)
            hidden(1)
            pe.wait_ge(s_kcT, 2)
            pe.wait_ge(s_tpev, 4)
            pe.wait_ge(s_sig, 1)
            pe.wait_ge(s_gelu, 2)
            for p in range(4):
                for t in range(T):
                    c = 2 * NC * (4 * (p % 2) + t)
                    mm = nc.tensor.matmul(ps[6 + p // 2][:, c:c + 2 * NC], QT[:, 4 + p, P * t:P * t + P],
                                          kcT[:, :, :].rearrange("p g n -> p (g n)"), start=True, stop=True)
                if p % 2:
                    mm.then_inc(s_csc, 1)
            natural(W_KA, 3, H1, ps, s_pj, evacuated(3))
            for n in range(9, 16):
                tp(n)
            pe.wait_ge(s_cex, 1)
            for b in range(2):
                for q in range(4):
                    r = 4 * b + q
                    mm = nc.tensor.transpose(ps[6 + b][:, P * q:P * q + P],
                                             cm[:, 4 * r:4 * r + 4, :].rearrange("p t n -> p (t n)"), ident)
                mm.then_inc(s_cpt, 1)
            natural(W_VA, 4, H1, ps, s_pj, evacuated(4))
            for n in range(16, len(TP)):
                tp(n)
            pe.wait_ge(s_cpte, 2)
            pe.wait_ge(s_ev, 20)
            for p in range(4):
                for a in range(2):
                    mm = nc.tensor.matmul(ps[p][:, 256 * a:256 * a + 256], PcT[:, 4 * a + p, :],
                                          Vbd[:, a, :, :].rearrange("p t d -> p (t d)"), start=True, stop=True)
                mm.then_inc(s_pvc, 1)

            pe.wait_ge(s_tpev, len(TP))
            pe.wait_ge(s_mixc, 4)
            for p in range(4):
                for t in range(T):
                    mm = nc.tensor.transpose(ps[4 + p][:, P * t:P * t + P], mixc[:, t, P * p:P * p + P], ident)
                mm.then_inc(s_mct, 1)

            def scores(H, a, staged, tiles=range(T), first=False, br=None):
                pe.wait_ge(s_stg[a], staged)
                for t in tiles:
                    if not first:
                        pe.wait_ge(s_L, 4 * H + (t - 3))
                    w = P * (t + 1)
                    q_ = QK[:, a, 0, P * t:P * t + P]
                    k_ = [QK[:, a, 1 + i, 0:w] if br is None else hp[:, 4 * br + 2 * a + i, 0:w] for i in range(2)]
                    nc.tensor.matmul(ps[t][:, 0:w], q_, k_[0], start=True, stop=False)
                    nc.tensor.matmul(ps[t][:, 0:w], q_, k_[1], start=False, stop=True).then_inc(s_S, 1)

            def half(H, a, staged=None, br=None, start=True, stop=True, done=0):
                for t in range(T):
                    pe.wait_ge(s_P, 4 * H + (t + 1))
                    pe.wait_ge(s_Plo, 4 * H + (t + 1))
                    for j in range(t + 1):
                        mm = nc.tensor.transpose(ps[4 + t % 2][:, P * j:P * j + P],
                                                 L[:, a, L_AT[t] + P * j:L_AT[t] + P * j + P], ident)
                    mm.then_inc(s_T, 1)
                    if t % 2 and staged is not None:
                        scores(H + 2, a, staged, (t - 1, t), br=br)
                pe.wait_ge(s_Plo, 4 * H + 6)
                pe.wait_ge(s_vl, H + 1)
                if start:
                    pe.wait_ge(s_cb, done + 1)
                for j in range(T):
                    for i, part in enumerate((PThi, PTlo)):
                        mm = nc.tensor.matmul(ps[6 + a][:, P * j:SEQ], VS[:, a, j, :], part[:, j, P * j:SEQ],
                                              start=start and j == 0 and i == 0,
                                              stop=stop and j == T - 1 and i == 1)
                mm.then_inc(s_PV, 1)

            pe.wait_ge(s_mcte, 4)
            scores(0, 0, STG, first=True)
            scores(1, 1, STG)
            for u in range(N_A):
                if u == 3:
                    pe.wait_ge(s_kn, 128)
                for a in range(2):
                    half(2 * u + a, a, STG * (u + 2) if u < 3 else STG * N_A + STGN, br=0 if u == 3 else None,
                         done=2 * u + a)
            with pe.Fori(0, 3) as i:
                for br in range(2):
                    for a in range(2):
                        half(4 * i + (2 * N_A + 2 * br + a), a, STGN * i + (STG * N_A + STGN * (1 + br)), br=1 - br,
                             start=br == 0, stop=br == 1, done=2 * i + (2 * N_A + a))
            for br in range(2):
                for a in range(2):
                    half(2 * N_A + 12 + 2 * br + a, a, STG * N_A + 4 * STGN if br == 0 else None, br=1,
                         start=br == 0, stop=br == 1, done=2 * N_A + 6 + a)

            M1 = (mhi, mlo)
            for h in range(2):
                def ev(t, h=h):
                    if h:
                        pe.wait_ge(s_ot, t + 1)
                natural(W_OUT + 4 * h, 0, M1, ps[4:8], s_op, ev, s_mlo)

            pe.wait_ge(s_xn2, T)
            for kk in range(KD):
                if kk >= 2:
                    pe.wait_ge(s_hf2, kk - 1)
                for t in range(T):
                    mm = nc.tensor.transpose(ps[4 + kk % 2][:, P * t:P * t + P], xn2[:, t, P * kk:P * kk + P], ident)
                mm.then_inc(s_h2tp, 1)
            pe.wait_ge(s_h2lo, KD)

            with pe.Fori(0, NF // 2) as i:
                for jj in range(2):
                    for r in range(2):
                        w0 = W_GU + 2 * jj + r
                        pe.wait_ge(s_lo, 4 * i + (w0 + 1))
                        if r == 0:
                            pe.wait_ge(s_prod, 2 * i + (jj + 1))
                        for gu in range(2):
                            for k4 in range(4):
                                kk = 4 * r + k4
                                for q, (s, m) in enumerate(PASSES):
                                    c = 256 * k4 + P * gu
                                    mm = nc.tensor.matmul(ps[2 * jj + gu][:, :], W2[s][:, SLOT[w0], c:c + P],
                                                          M1[m][:, kk, :], start=(kk == 0 and q == 0),
                                                          stop=(kk == KD - 1 and q == 2))
                        mm.then_inc(s_mm, 1)

            def down(w, slot, k, first, last):
                pe.wait_ge(s_lo, w + 1)
                for dt in range(KD):
                    for q, (s, m) in enumerate(PASSES):
                        rhs = (ahi, alo)[m][:, bass.ds(k, 1), :].rearrange("p o n -> p (o n)")
                        mm = nc.tensor.matmul(ps[dt][:, :], W2[s][:, slot, P * dt:P * dt + P], rhs,
                                              start=(first and q == 0), stop=(last and q == 2))
                    if last:
                        mm.then_inc(s_dn, 1)
                if not last:
                    mm.then_inc(s_mm, 1)

            pe.wait_ge(s_alo, NF + 2)
            for k in range(2):
                down(W_DN + k, SLOT[W_DN + k], k, k == 0, False)
            with pe.Fori(0, (NF - 6) // 4) as i:
                for r in range(4):
                    down(4 * i + (W_DN + 2 + r), SLOT[W_DN + 2 + r], 4 * i + (2 + r), False, False)
            for k in range(2 + (NF - 6) // 4 * 4, NF):
                down(W_DN + k, SLOT[W_DN + k], k, False, k == NF - 1)

            pe.wait_ge(s_yT, KD // 2)
            pe.wait_ge(s_nrm, 4 + KD // 2)
            for t in range(T):
                for h in range(2):
                    for q in range(4):
                        dt = 4 * h + q
                        mm = nc.tensor.transpose(ps[2 * t + h][:, P * q:P * q + P], yT[:, dt, P * t:P * t + P], ident)
                    mm.then_inc(s_ytp, 1)


def shape_constants():
    shc = np.zeros((P, 388), np.float32)
    shc[:, S_ID:S_ID + P] = np.eye(P)
    shc[:, S_ONE:S_ONE + P] = 1.0
    q = np.arange(P)[:, None, None] + P * np.arange(T)[None, :, None]
    n = np.arange(NC)[None, None, :]
    hidden = (n * CS + CL - 1 > q) | (n >= NCMP)
    shc[:, S_MASK:S_MASK + P] = np.where(hidden, NEG, 0.0).reshape(P, P)
    shc[:, S_VALID:S_VALID + T] = ~hidden.all(axis=2)
    d = np.arange(BV) - (P - 1)
    half = NB_ // 2
    big = half + (np.log(np.maximum(d, 1) / half) / math.log(MAX_DIST / half) * half).astype(np.int64)
    bucket = np.where(d < half, np.maximum(d, 0), np.minimum(big, NB_ - 1))
    oneh = np.zeros((NB_ + 1, BV), np.float32)
    oneh[bucket, np.arange(BV)] = 1.0
    oneh[NB_] = np.where(d < 0, NEG, 0.0)
    return shc, oneh


def kernel(**inputs):
    import concourse.bacc as _bacc
    from concourse.bass_utils import run_bass_kernel_spmd as _run

    a = {k: np.asarray(v) for k, v in inputs.items()}
    rows = lambda w, n: w.reshape(KD, P, n).transpose(1, 0, 2)

    w_in = rows(a["w_in"][0], a["w_in"].shape[2])
    o = np.cumsum([0, 512, 512, 512, 512] + [128] * 6 + [24])
    qa, ka, va, qb, kc, vc, ksl, vsl, kwn, vwn, gl = (w_in[:, :, o[i]:o[i + 1]] for i in range(11))
    pairs = lambda w: w.reshape(P, KD, 2, 4, DH).transpose(0, 1, 3, 2, 4).reshape(P, KD, 512)
    wst = np.empty((N_W, P, U), np.float32)

    def put(w0, blk, per):
        n = blk.shape[1] // per
        wst[w0:w0 + n] = blk.reshape(P, n, U).transpose(1, 0, 2)

    put(W_T, np.concatenate([kc, vc], 2), 4)
    put(W_QB, pairs(qb), 2)
    put(W_KV, np.concatenate([ksl, kwn, vsl, vwn], 2), 2)
    put(W_QA, qa, 2)
    put(W_KA, ka, 2)
    put(W_VA, va, 2)
    wo = a["w_out"][0]
    wo = np.concatenate([wo[:512], wo[512:].reshape(2, 4, DH, D).transpose(1, 0, 2, 3).reshape(512, D)])
    wo = rows(wo, D)
    put(W_OUT, wo[:, :, :512], 2)
    put(W_OUT + 4, wo[:, :, 512:], 2)
    gu = rows(a["w_gu"][0], 2 * FFN).reshape(P, 2, 4, 2, NF, P)
    wst[W_GU:W_DN] = gu.transpose(4, 1, 0, 2, 3, 5).reshape(2 * NF, P, U)
    wst[W_DN:] = a["w_down"][0].reshape(NF, P, U)

    ada = rows(a["w_ada"][0], 6 * D).reshape(P, KD, 6, D)
    sc_sh = np.stack([ada[:, :, 1], ada[:, :, 0]], 2).reshape(P, 4, 2, 2, 2, 512)
    ada_e = sc_sh.transpose(4, 3, 1, 0, 2, 5).reshape(N_EARLY, P, U)
    late = np.stack([ada[:, :, g] for g in (2, 3, 4, 5)], 2).reshape(P, 4, 2, 4, 2, 512)
    ada_l = late.transpose(3, 4, 1, 0, 2, 5).reshape(32, P, U)

    col = lambda v: v.reshape(KD, P).T
    b = a["b_ada"][0].reshape(6, D)
    cols = np.zeros((P, N_COLS), np.float32)
    cols[:, C_C:C_C + 8] = col(a["c"][0])
    cols[:, C_BM:C_BM + 16:2] = col(b[1])
    cols[:, C_BM + 1:C_BM + 17:2] = col(b[0])
    cols[:, C_GM:C_GM + 8] = col(a["g_mix"][0])
    cols[:, C_GF:C_GF + 8] = col(a["g_ffn"][0])
    for i, g in enumerate((3, 4, 5)):
        cols[:, C_BF + 8 * i:C_BF + 8 * i + 8] = col(b[g])
    for i, name in enumerate(("q_norm_b", "k_norm_sel", "k_norm_win", "q_norm_a", "k_norm_a", "k_norm_cmp")):
        cols[:, C_GAIN + i] = np.concatenate([a[name][0], a[name][0]])
    for i, name in enumerate(("cmp_pe_k", "cmp_pe_v")):
        cols[:, C_PE + 16 * i:C_PE + 16 * i + 16] = a[name][0].reshape(CL // 2, 2 * DH).T
    r = a["rel_bias"]
    rel = np.concatenate([r[:, :8], r[:, 8:].reshape(NB_, 2, 4).transpose(0, 2, 1).reshape(NB_, 8)], 1)
    wgl = gl.reshape(P, KD, 2, 4, 3).transpose(0, 1, 4, 3, 2).reshape(P, KD, 24)
    w1 = np.stack([a[n][0].reshape(CL // 2, P, 256).transpose(1, 0, 2) for n in ("cmp_w1_k", "cmp_w1_v")])
    w2 = np.stack([a[n][0].reshape(2, P, DH).transpose(1, 0, 2) for n in ("cmp_w2_k", "cmp_w2_v")], 1)
    shc, oneh = shape_constants()

    nc = _bacc.Bacc("TRN2", target_bir_lowering=False, num_devices=1)
    arrays, args = {}, []
    for name, v in (("wst", wst), ("ada_e", ada_e), ("ada_l", ada_l), ("x", a["x"]), ("cols", cols), ("shc", shc),
                    ("oneh", oneh), ("rel", rel), ("brow", b[2:3]), ("wgl", wgl), ("w1", w1), ("w2", w2)):
        arrays[name + "_dram"] = v = np.ascontiguousarray(v)
        args.append(nc.dram_tensor(name + "_dram", v.shape, mybir.dt.from_np(v.dtype), kind="ExternalInput").ap())
    out = nc.dram_tensor("out_dram", (1, SEQ, D), F32, kind="ExternalOutput").ap()
    layer(nc, *args, out)
    res = _run(nc, [arrays], core_ids=[0])
    return res.results[0]["out_dram"]
```

```python
import math
from contextlib import ExitStack

import numpy as np
import concourse.bass as bass
from concourse import mybir

F32 = mybir.dt.float32
F32R = mybir.dt.float32r
ALU = mybir.AluOpType
ACT = mybir.ActivationFunctionType
AXX = mybir.AxisListType.X

P = 128
SEQ, D = 512, 1024
T = SEQ // P
KD = D // P
DH = 64
FFN = 2816
NF = FFN // P
NB_, MAX_DIST = 32, 128
EPS = 1e-6
NEG = -1e30
SCALE = DH ** -0.5
CL, CS = 32, 16
NCMP = (SEQ - CL) // CS + 1
NC = 32
U = 1024

W_T, W_QB, W_KV, W_QA, W_KA, W_VA = 0, 2, 6, 10, 14, 18
W_OUT, W_GU, W_DN = 22, 30, 30 + 2 * NF
N_W = W_DN + NF
N_EARLY = 16

C_C, C_BM, C_GM, C_GF, C_BF, C_GAIN, C_PE = 0, 8, 24, 32, 40, 64, 70
N_COLS = C_PE + 2 * CL // 2
G_QB, G_KSL, G_KWN, G_QA, G_KA, G_KCMP = range(6)
S_ID, S_ONE, S_MASK, S_VALID = 0, 128, 256, 384
BV = 640
L_AT = [P * t * (t + 1) // 2 for t in range(T)]
LW = P * T * (T + 1) // 2


def view(ap, dims, off=0):
    return bass.AP(ap.tensor, ap.offset + off, [list(ap.ap[0])] + dims)


def layer(nc, wst, ada_e, ada_l, xd, cols, shc, oneh, rel, brow, wgl, w1, w2, out):
    bvd = nc.dram_tensor("bias_by_distance", (16, BV), F32, kind="Internal").ap()
    x_v = xd.rearrange("b (t p) d -> p (b t) d", p=P)
    out_v = out.rearrange("b (t p) d -> p (b t) d", p=P)

    with ExitStack() as top:
        def sb(name, shape, dt=F32, ctx=top):
            return ctx.enter_context(nc.sbuf_tensor(name, shape, dt))

        def sem(name):
            return top.enter_context(nc.semaphore(name))

        ps = [top.enter_context(nc.psum_tensor(f"ps{i}", [P, 512], F32)) for i in range(8)]

        par = sb("par", [P, N_COLS])
        shp = sb("shp", [P, 388])
        ident, ones = shp[:, S_ID:S_ID + P], shp[:, S_ONE:S_ONE + P]
        eps = sb("eps", [P, 1])
        silc = sb("silc", [P, KD])
        xss = sb("xss", [P, T])
        xss2 = sb("xss2", [P, 3 * T])
        xst = sb("xst", [P, T])
        xrs = sb("xrs", [P, T])
        modm = sb("modm", [P, KD, 2])
        am = sb("am", [P, KD])
        modf = sb("modf", [P, 3 * KD])
        modfb = sb("modfb", [P, 3 * KD])
        af = sb("af", [P, KD])
        gq = sb("gq", [P, 2])
        gtm = sb("gtm", [P, D])
        G = sb("G", [P, 24, T])
        raw = sb("raw", [P, 4, U])
        whi = sb("whi", [P, 4, U], F32R)
        wlo = sb("wlo", [P, 4, U], F32R)
        hp = sb("hp", [P, 2 * KD, SEQ], F32R)
        mhi, mlo = hp[:, 0:KD, :], hp[:, KD:2 * KD, :]
        h1hi, h1lo = mhi, mlo
        PARTS = (0, 4, 8, 0)
        N_QP, N_KP, N_KS = 8, 12, (4, 0)

        ca = ExitStack()
        QT = sb("QT", [P, 8, SEQ], F32, ca)
        KT = sb("KT", [P, 6, SEQ], F32, ca)
        VA = sb("VA", [P, T, 512], F32, ca)
        VB = sb("VB", [P, T, 256], F32, ca)
        brow_s = VA[0:1, 0:2, :].rearrange("p o n -> p (o n)")
        eacc = [KT[:, 4, :], KT[:, 5, :], VA[:, 2, :], VA[:, 3, :]]
        acc = [QT[:, j, :] for j in range(4)] + [KT[:, j, :] for j in range(4)]
        with ExitStack() as c:
            x0 = sb("x0", [P, T, D], F32, c)
            xn = sb("xn", [P, T, D], F32, c)
        with ExitStack() as c:
            nat = sb("nat", [P, 2, T, 512], F32, c)
            w1s = sb("w1s", [P, CL // 2, 256], F32, c)
        mf = sb("mf", [P, 8, SEQ], F32, ca)
        with ExitStack() as c:
            mixc = sb("mixc", [P, T, 512], F32, c)
        PThi, PTlo = (sb(n, [P, T, SEQ], F32R, ca) for n in ("PThi", "PTlo"))
        with ExitStack() as c:
            ring2 = sb("ring2", [P, 4, U], F32, c)
            sq = sb("sq", [P, 2, 512], F32, c)
            R = sb("R", [P, 2, CL // 2, 2, NC], F32, c)
            ssb = sb("ssb", [P, 4, 32], F32, c)
            stb = sb("stb", [P, 4, 32], F32, c)
            rsb = sb("rsb", [P, 4, 32], F32, c)
            glr = sb("glr", [P, KD, 24], F32, c)
            glh = sb("glh", [P, KD, 24], F32R, c)
            gll = sb("gll", [P, KD, 24], F32R, c)
            w2s = sb("w2s", [P, 2, 2, DH], F32, c)
            hidk = sb("hidk", [P, 2, 2 * NC], F32, c)
            hidv = sb("hidv", [P, 2, 2, T, NC], F32, c)
            kcn = sb("kcn", [NC, 2, DH], F32, c)
            kcq = sb("kcq", [NC, 2, DH], F32, c)
            kcs = sb("kcs", [NC, 3, 2], F32, c)
            kcT = sb("kcT", [P, 2, NC], F32, c)
            Vbd = sb("Vbd", [P, 2, T, DH], F32, c)
            gv = sb("gv", [P, 8, T], F32, c)
            cst = sb("cst", [P, 4, 32], F32, c)
            rel_s = sb("rel_s", [33, 16], F32, c)
            with ExitStack() as c2:
                oneh_s = sb("oneh_s", [33, BV], F32, c2)
                bvs = sb("bvs", [16, BV], F32, c2)
            with ExitStack() as c2:
                hf = sb("hf", [P, 2, SEQ], F32, c2)
            with ExitStack() as c2:
                kcE = sb("kcE", [P, 2, 2, 256], F32, c2)
                Kst = sb("Kst", [P, 2, 2, 256], F32, c2)
            with ExitStack() as c2:
                cm = sb("cm", [P, 32, NC], F32, c2)
                with ExitStack() as c3:
                    glT = sb("glT", [24, SEQ], F32, c3)
                PcT = sb("PcT", [P, 8, P], F32, c2)
        with ExitStack() as c:
            QK = sb("QK", [P, 2, 3, SEQ], F32R, c)
            L = sb("L", [P, 2, LW], F32, c)
            bias = sb("bias", [P, 2, SEQ], F32, c)
            VS = sb("VS", [P, 2, T, 2 * DH], F32R, c)
            tmp = sb("tmp", [P, SEQ], F32, c)
            nmx = sb("nmx", [P, 8], F32, c)
            sums = sb("sums", [P, 8], F32, c)
            rec = sb("rec", [P, 2, T], F32, c)
            rg = sb("rg", [P, 2, T], F32, c)
        ca.close()
        x1 = sb("x1", [P, T, D])
        ob = sb("ob", [P, 2, 512])
        hf2 = sb("hf2", [P, 2, SEQ])
        with ExitStack() as c:
            xn2 = sb("xn2", [P, T, D], F32, c)
        with ExitStack() as c:
            sil = sb("sil", [P, 2, SEQ], F32, c)
            actf = sb("actf", [P, 2, SEQ], F32, c)
            ahi, alo = (sb(n, [P, NF, SEQ], F32R, c) for n in ("ahi", "alo"))
        with ExitStack() as c:
            yT = sb("yT", [P, KD, SEQ], F32, c)
            yo = sb("yo", [P, T, D], F32, c)

        s_par, s_shp, s_x, s_rel, s_gl, s_w2, s_w1, s_brow = map(
            sem, "par_in shp_in x_in rel_in gl_in w2_in w1_in brow_in".split())
        s_raw = [sem(f"raw{i}_in") for i in range(4)]
        s_r2 = [sem(f"ring2_{i}_in") for i in range(4)]
        s_eps, s_silc, s_xss, s_xst, s_xrs, s_xn = map(
            sem, "eps_set silc_done xss_done xst_done xrs_done xn_done".split())
        s_bvp, s_bvs, s_bvd = map(
            sem, "bv_psum bv_sbuf bv_dram".split())
        s_each = sem("early_acc_added")
        s_hlo2 = sem("h_lo_4_to_7")
        s_adamm, s_mod, s_htp, s_hf, s_hhi, s_hlo = map(
            sem, "ada_mm mod_done hT_psum hf_done h_hi h_lo".split())
        s_hi, s_lo, s_mm = map(sem, "w_hi w_lo w_used".split())
        s_kvE, s_kst, s_Rz, s_R = map(sem, "kvT_evac kst_in R_zero R_built".split())
        s_pj, s_ev, s_ssr, s_std, s_nrm = map(
            sem, "proj_psum proj_evac ss_done std_done nat_normed".split())
        s_ach, s_offs = map(sem, "acc_added offsets_added".split())
        s_hid, s_gelu, s_kcp, s_kce, s_kcr, s_kcst, s_kcn, s_kctp, s_kcT = map(
            sem, "hid_psum gelu_done kc_psum kc_evac kc_ss kc_std kc_normed kcT_psum kcT_evac".split())
        s_glT, s_gltp = map(sem, "glT_evac gates_psum".split())
        s_glh, s_gll, s_glp, s_sig, s_gq = map(sem, "gl_hi gl_lo gl_psum gates_done gq_done".split())
        s_csc, s_cm, s_cex, s_cpt, s_cpte, s_pvc, s_mixc = map(
            sem, "cs_psum cm_done c_exp pcT_psum pcT_evac pvc_psum mixc_done".split())
        s_tp, s_tpev, s_vz, s_kcz = map(sem, "tp_psum tp_evac vbd_zero kcT_zero".split())
        s_dch, s_begun = map(sem, "dve_chain begun".split())
        s_stg = [sem(f"staged{a}") for a in range(2)]
        s_S, s_L, s_E, s_rch, s_rg, s_P, s_T, s_Phi, s_Plo, s_PV = map(
            sem, "S_psum logits exp_done rec_done rg_done P_scaled PT_psum PT_hi PT_lo PV_psum".split())
        s_kn = [sem(f"nsa_k{br}_staged") for br in range(2)]
        s_qkh, s_qkl, s_vh, s_vl, s_tmp, s_own, s_cb, s_mct, s_mcte = map(
            sem, "qk_hi qk_lo v_hi v_lo out_moved own_added heads_done mixcT_psum mixcT_evac".split())
        s_mfz = sem("mf_zero")
        s_x2s, s_yT0 = map(sem, "x2_sums yT_first_done".split())
        s_mhi, s_mlo, s_op, s_ot, s_x1, s_x1in, s_x1sq, s_h2lo = map(
            sem, "m_hi m_lo out_psum out_gated x1_done x1_in x1_sq h2_lo".split())
        s_sil, s_prod, s_ahi, s_alo, s_dn, s_yT, s_ytp, s_yo, s_out = map(
            sem, "silu_done prod_done a_hi a_lo dn_psum yT_done y_psum yo_done out_done".split())
        s_h2tp, s_hf2, s_h2hi, s_xn2, s_x2ss, s_x2st, s_modf = map(
            sem, "h2_psum hf2_done h2_hi xn2_done x2_ss x2_std modf_done".split())

        block = top.enter_context(nc.Block())

        TP = ([("q", 4 + i) for i in range(4)] + [("gtm", 0), ("kb", 4), ("kb", 5), ("gtm", 1), ("col", 2)]
              + [("col", 3), ("col", 4)] + [("q", i) for i in range(4)] + [("vcmp", 0)]
              + [("col", 5), ("col", 6), ("col", 7)] + [("k", i) for i in range(4)])
        STG, STGN = 64, 48
        N_A = 4
        SLOT = [(w % 4) for w in range(N_W)]

        def raw_count(w):
            return 16 * (N_EARLY // 4 + w // 4 + 1)

        @block.sync
        def _(sp):
            sp.dma_start(par[:, :], cols).then_inc(s_par, 16)
            sp.dma_start(shp[:, :], shc).then_inc(s_shp, 16)
            sp.dma_start(rel_s[0:32, :], rel).then_inc(s_rel, 16)
            sp.dma_start(rel_s[32:33, :], shc[0:1, S_ONE:S_ONE + 16]).then_inc(s_rel, 16)
            sp.dma_start(oneh_s[:, :], oneh).then_inc(s_rel, 16)
            for e in range(N_EARLY):
                if e == 2:
                    sp.dma_start(x0[:, :, :], x_v).then_inc(s_x, 16)
                if e >= 4:
                    sp.wait_ge(s_each, 2 * (e - 3))
                sp.dma_start(raw[:, e % 4, :], ada_e[e]).then_inc(s_raw[e % 4], 16)
            sp.dma_start(brow_s, brow).then_inc(s_brow, 16)
            sp.dma_start(glr[:, :, :], wgl).then_inc(s_gl, 16)
            sp.dma_start(w2s[:, :, :, :], w2).then_inc(s_w2, 16)

            def late(k):
                if k >= 4:
                    sp.wait_ge(s_ach, 2 * (k - 3))
                sp.dma_start(ring2[:, k % 4, :], ada_l[k]).then_inc(s_r2[k % 4], 16)

            def weights(w):
                if w < 4:
                    sp.wait_ge(s_each, 2 * (N_EARLY - 3 + w))
                else:
                    sp.wait_ge(s_lo, w - 3)
                sp.dma_start(raw[:, SLOT[w], :], wst[w]).then_inc(s_raw[SLOT[w]], 16)

            for w in range(W_OUT):
                weights(w)
                if w == 4:
                    sp.wait_ge(s_hlo2, KD - 4)
                    sp.dma_start(w1s[:, :, :], w1[0]).then_inc(s_w1, 16)
                if w == 11:
                    sp.wait_ge(s_hid, 1)
                    sp.dma_start(w1s[:, :, :], w1[1]).then_inc(s_w1, 16)
                if 4 <= w < 20:
                    late(2 * (w - 4))
                    late(2 * (w - 4) + 1)
            for w in range(W_OUT, W_OUT + 4):
                weights(w)

            top_, low_ = slice(0, 64), slice(64, 128)

            def move(dst, src, done):
                sp.dma_start(dst.bitcast(F32), src.bitcast(F32)).then_inc(done, 16)

            def stage_bias(a, qi):
                sp.dma_start(bias[:, a, :], bass.AP(bvd.tensor, qi * (2 * BV) + a * BV, [[1, P], [1, SEQ]])
                             ).then_inc(s_stg[a], 16)

            def stage(u, a):
                h = slice(64 * a, 64 * a + 64)
                p = PARTS[u]
                if u:
                    stage_bias(a, u)
                sp.wait_ge(s_qkh, 2 * u + 2)
                sp.wait_ge(s_qkl, 2 * u + 1)
                move(QK[top_, a, :, :], hp[h, p:p + 3, :], s_stg[a])
                move(QK[low_, a, 1:3, :], hp[h, p + 1:p + 3, :], s_stg[a])
                sp.wait_ge(s_qkl, 2 * u + 2)
                move(QK[low_, a, 0, :], hp[h, p + 3, :], s_stg[a])

            def stage_nsa(r, a):
                h = slice(64 * a, 64 * a + 64)
                stage_bias(a, r + N_A)
                sp.wait_ge(s_qkh, r + (2 * N_A + 3))
                sp.wait_ge(s_qkl, r + (2 * N_A + 3))
                move(QK[top_, a, 0, :], hp[h, N_QP, :], s_stg[a])
                move(QK[low_, a, 0, :], hp[h, N_QP + 1, :], s_stg[a])

            sp.wait_ge(s_tpev, 22)
            sp.wait_ge(s_ach, 2 * 32)
            sp.wait_ge(s_bvd, 16)
            stage_bias(0, 0)
            stage_bias(1, 0)
            for u in range(N_A):
                for a in range(2):
                    if u:
                        sp.wait_ge(s_L, 8 * u + 4 * a - 4)
                    stage(u, a)
            for a in range(2):
                sp.wait_ge(s_stg[a], N_A * STG)
            sp.wait_ge(s_qkh, 2 * N_A + 2)
            sp.wait_ge(s_qkl, 2 * N_A + 2)

            def stage_k(br):
                for a in range(2):
                    h = slice(64 * a, 64 * a + 64)
                    for rows_ in (top_, low_):
                        move(hp[rows_, N_KS[br] + 2 * a:N_KS[br] + 2 * a + 2, :],
                             hp[h, N_KP + 2 * br:N_KP + 2 * br + 2, :], s_kn[br])

            stage_k(0)
            for a in range(2):
                sp.wait_ge(s_L, 8 * N_A + 4 * a - 4)
                stage_nsa(0, a)
            stage_k(1)
            with sp.Fori(0, 3) as i:
                for a in range(2):
                    sp.wait_ge(s_L, 16 * i + (8 * N_A + 12 + 4 * a))
                    stage_nsa(i + 1, a)
            sp.wait_ge(s_qkl, 2 * N_A + 6)
            sp.wait_ge(s_stg[0], STG * N_A + 4 * STGN)
            sp.wait_ge(s_stg[1], STG * N_A + 4 * STGN)
            sp.dma_start(x1[:, :, :], x_v).then_inc(s_x1in, 16)
            for w in range(W_OUT + 4, W_GU):
                weights(w)
            with sp.Fori(0, (N_W - W_GU) // 4) as i:
                for r in range(4):
                    sp.wait_ge(s_lo, 4 * i + (W_GU + r - 3))
                    s = SLOT[W_GU + r]
                    sp.dma_start(raw[:, s, :], wst[bass.ds(4 * i + (W_GU + r), 1)].rearrange("o p n -> p (o n)")
                                 ).then_inc(s_raw[s], 16)
            for w in range(W_GU + (N_W - W_GU) // 4 * 4, N_W):
                weights(w)
            for h in range(2):
                for t in range(T):
                    sp.wait_ge(s_yo, 4 * h + t + 1)
                    c_ = slice(512 * h, 512 * h + 512)
                    sp.dma_start(out_v[:, t, c_], yo[:, t, c_]).then_inc(s_out, 16)
            sp.wait_ge(s_out, 32 * T)

        @block.gpsimd
        def _(pool):
            nc.gpsimd.memset(eps[:, :], EPS).then_inc(s_eps, 1)
            nc.gpsimd.memset(R[:, :, :, :, :], 0.0).then_inc(s_Rz, 1)
            nc.gpsimd.memset(Vbd[:, :, :, :], 0.0).then_inc(s_vz, 1)
            nc.gpsimd.memset(kcT[:, :, :], 0.0).then_inc(s_kcz, 1)

            def low(w, slot):
                pool.wait_ge(s_hi, w + 1)
                nc.gpsimd.tensor_tensor(wlo[:, slot, :], raw[:, slot, :], whi[:, slot, :].bitcast(F32),
                                        ALU.subtract).then_inc(s_lo, 1)

            for kk in range(4):
                pool.wait_ge(s_hhi, kk + 1)
                nc.gpsimd.tensor_tensor(h1lo[:, kk, :], hf[:, kk % 2, :], h1hi[:, kk, :].bitcast(F32),
                                        ALU.subtract).then_inc(s_hlo, 1)
            for w in range(W_KV):
                low(w, SLOT[w])
            pool.wait_ge(s_kst, 128)
            pool.wait_ge(s_Rz, 1)
            pool.wait_ge(s_par, 16)
            for kv in range(2):
                for g in range(2):
                    win = view(Kst[:, kv, g, :], [[1, CL // 2], [CS // 2, NCMP]])
                    pe_ = view(par[:, C_PE + 16 * kv:C_PE + 16 * kv + 16], [[1, CL // 2], [0, NCMP]])
                    nc.gpsimd.tensor_tensor(R[:, kv, :, g, 0:NCMP], win, pe_, ALU.add).then_inc(s_R, 1)
            for w in range(W_KV, W_OUT + 3):
                low(w, SLOT[w])

            def low_part(n, src, j, hi, lo):
                pool.wait_ge(s_qkh, n + 1)
                pool.sem_inc(s_begun)
                nc.gpsimd.tensor_tensor(hp[:, lo, :], src[:, bass.ds(j, 1), :].rearrange("p o n -> p (o n)"),
                                        hp[:, hi, :].bitcast(F32), ALU.subtract).then_inc(s_qkl, 1)

            def qk_low(u):
                low_part(2 * u, KT, u, PARTS[u] + 1, PARTS[u] + 2)
                low_part(2 * u + 1, QT, u, PARTS[u], PARTS[u] + 3)

            def k_low_nsa():
                for br in range(2):
                    low_part(2 * N_A + br, KT, 4 + br, N_KP + 2 * br, N_KP + 2 * br + 1)

            def q_low_nsa(r):
                low_part(r + (2 * N_A + 2), QT, r + 4, N_QP, N_QP + 1)

            def scale(H, a):
                pool.wait_ge(s_rg, H + 1)
                for t in range(T):
                    l_ = L[:, a, L_AT[t]:L_AT[t] + P * (t + 1)]
                    nc.gpsimd.tensor_tensor(l_, l_, view(rg[:, a, t:t + 1], [[0, P * (t + 1)]]), ALU.mult
                                            ).then_inc(s_P, 1)

            def v_low(H, a, V, col):
                pool.wait_ge(s_vh, H + 1)
                pool.sem_inc(s_begun)
                nc.gpsimd.tensor_tensor(VS[:, a, :, DH:2 * DH], V[:, :, bass.ds(col, DH)],
                                        VS[:, a, :, 0:DH].bitcast(F32), ALU.subtract).then_inc(s_vl, 1)

            def half(H, a, v_next):
                if v_next is not None:
                    scale(H + 1, 1 - a)
                    v_low(H + 1, 1 - a, *v_next)

            qk_low(0)
            qk_low(1)
            v_low(0, 0, VA, 0)
            scale(0, 0)
            low(W_OUT + 3, SLOT[W_OUT + 3])
            for u in range(N_A):
                half(2 * u, 0, (VA, 128 * u + 64))
                if u < 2:
                    qk_low(u + 2)
                elif u == 2:
                    q_low_nsa(0)
                half(2 * u + 1, 1, (VA, 128 * u + 128) if u < 3 else (VB, 0))
                if u == 1:
                    k_low_nsa()
            with pool.Fori(0, 3) as i:
                for br in range(2):
                    half(4 * i + (2 * N_A + 2 * br), 0, (VB, 128 * br + 64))
                    if br == 0:
                        q_low_nsa(i + 1)
                    half(4 * i + (2 * N_A + 2 * br + 1), 1, (VB, 128 - 128 * br))
            for br in range(2):
                for a in range(2):
                    half(2 * N_A + 12 + 2 * br + a, a, (VB, (128 * br + 64) if a == 0 else 128) if br + a < 2 else None)

            with pool.Fori(0, (N_W - W_OUT - 4) // 4) as i:
                for r in range(4):
                    low(4 * i + (W_OUT + 4 + r), SLOT[W_OUT + 4 + r])
            for w in range(W_OUT + 4 + (N_W - W_OUT - 4) // 4 * 4, N_W):
                low(w, SLOT[w])

        @block.scalar
        def _(act):
            act.wait_ge(s_par, 16)
            nc.scalar.activation(silc[:, :], par[:, C_C:C_C + KD], ACT.Silu).then_inc(s_silc, 1)
            act.wait_ge(s_bvp, 1)
            nc.scalar.activation(bvs[:, 0:512], ps[6][0:16, 0:512], ACT.Copy).then_inc(s_bvs, 1)
            nc.scalar.activation(bvs[:, 512:BV], ps[7][0:16, 0:BV - 512], ACT.Copy).then_inc(s_bvs, 1)
            act.wait_ge(s_x, 16)
            for t in range(T):
                nc.scalar.activation(xn[:, t, :], x0[:, t, :], ACT.Square,
                                     accum_out=xss[:, t:t + 1]).then_inc(s_xss, 1)
            act.wait_ge(s_eps, 1)
            act.wait_ge(s_xss, T)
            nc.scalar.activation(xst[:, :], xss[:, 0:T], ACT.Sqrt, bias=eps[:, :], scale=1.0 / D).then_inc(s_xst, 1)
            act.wait_ge(s_xrs, 1)
            for t in range(T):
                nc.scalar.activation(xn[:, t, :], x0[:, t, :], ACT.Copy, scale=xrs[:, t:t + 1]).then_inc(s_xn, 1)
            act.wait_ge(s_bvs, 2)
            act.dma_start(bvd, bvs[:, :]).then_inc(s_bvd, 16)
            act.wait_ge(s_bvd, 16)

            def h_chunk(kk, hbuf, a_col, s_col, tp, hfs, lo_s, n_lo, banks):
                act.wait_ge(tp, kk + 1)
                if kk >= 2:
                    act.wait_ge(lo_s, n_lo + kk - 1)
                nc.scalar.activation(hbuf[:, kk % 2, :], banks[kk % len(banks)][:, :], ACT.Identity,
                                     bias=s_col, scale=a_col).then_inc(hfs, 1)

            def high(w, slot, landed):
                act.wait_ge(s_raw[slot], landed)
                nc.scalar.activation(whi[:, slot, :], raw[:, slot, :], ACT.Copy).then_inc(s_hi, 1)

            def high_w(w):
                if w >= 4:
                    act.wait_ge(s_mm, w - 3)
                high(w, SLOT[w], raw_count(w))

            for kk in range(KD):
                act.wait_ge(s_mod, kk // 4 + 1)
                h_chunk(kk, hf, am[:, kk:kk + 1], modm[:, kk, 1:2], s_htp, s_hf,
                        s_hlo if kk < 6 else s_hlo2, 0 if kk < 6 else -4, ps[0:4])
                act.wait_ge(s_hf, kk + 1)
                nc.scalar.activation(h1hi[:, kk, :], hf[:, kk % 2, :], ACT.Copy).then_inc(s_hhi, 1)
                if kk in (3, 4):
                    high_w(kk - 3)
            high_w(2)
            high_w(3)
            act.wait_ge(s_gl, 16)
            nc.scalar.activation(glh[:, :, :], glr[:, :, :], ACT.Copy).then_inc(s_glh, 1)

            high_w(4)
            act.wait_ge(s_mm, W_QB)
            act.wait_ge(s_hlo2, KD - 4)
            for kv in range(2):
                nc.scalar.activation(kcE[:, kv, :, :], ps[4 + kv][:, :].rearrange("p (m r) -> p r m", r=2),
                                     ACT.Copy).then_inc(s_kvE, 1)
            act.wait_ge(s_kvE, 2)
            for g in range(2):
                for r in range(2):
                    act.dma_start(Kst[64 * r:64 * r + 64, :, g, :], kcE[64 * g:64 * g + 64, :, r, :]
                                  ).then_inc(s_kst, 32)
            high_w(5)

            def high_part(src, j, hi):
                nc.scalar.activation(hp[:, hi, :], src[:, bass.ds(j, 1), :].rearrange("p o n -> p (o n)"), ACT.Copy
                                     ).then_inc(s_qkh, 1)

            def qk_high(u):
                if u == 3:
                    for a in range(2):
                        act.wait_ge(s_stg[a], STG)
                high_part(KT, u, PARTS[u] + 1)
                high_part(QT, u, PARTS[u])

            def evac(blk, t):
                if t < T - 1:
                    act.wait_ge(s_pj, 3 * blk + t + 1)
                else:
                    act.wait_ge(s_mm, W_QB + 4 * blk + 4)

            def square(q, src, width):
                if q >= 2:
                    act.wait_ge(s_ssr, q - 1)
                return nc.scalar.activation(sq[:, q % 2, 0:width], src, ACT.Square)

            def normed_block(blk, b, width, v_dst):
                if b >= 2:
                    act.wait_ge(s_tp, {2: 4, 3: 7}[b])
                for t in range(T):
                    evac(blk, t)
                    nc.scalar.activation(nat[:, b % 2, t, 0:width], ps[t][:, 0:width], ACT.Copy)
                    if v_dst is not None:
                        nc.scalar.activation(v_dst[:, t, :], ps[t][:, width:512], ACT.Copy)
                    square(4 * b + t, ps[t][:, 0:width], width).then_inc(s_ev, 1)
                h = width // DH
                act.wait_ge(s_ssr, 4 * b + 4)
                nc.scalar.activation(stb[:, b, 0:T * h], ssb[:, b, 0:T * h], ACT.Sqrt, bias=eps[:, :],
                                     scale=1.0 / DH).then_inc(s_std, 1)

            def evac_tp(n):
                kind, j = TP[n]
                bank = ps[4 + n % 2]
                act.wait_ge(s_tp, n + 1)
                if kind == "q":
                    g = gq[:, 0:1] if j >= 4 else gq[:, 1:2]
                    i = nc.scalar.activation(QT[:, j, :], bank[:, :], ACT.Copy, scale=g)
                elif kind in ("k", "kb"):
                    gi = C_GAIN + (G_KA if kind == "k" else G_KSL + j - 4)
                    i = nc.scalar.activation(KT[:, j, :], bank[:, :], ACT.Copy, scale=par[:, gi:gi + 1])
                elif kind == "gtm":
                    i = nc.scalar.activation(gtm[:, 512 * j:512 * j + 512], bank[:, :], ACT.Copy)
                elif kind == "col":
                    i = nc.scalar.activation(modf[:, 4 * (j - 2):4 * (j - 2) + 4], bank[:, 0:4], ACT.Copy)
                else:
                    act.wait_ge(s_vz, 1)
                    for t in range(T):
                        r = slice(32 * t, 32 * t + 32)
                        i = nc.scalar.activation(Vbd[r, :, t, :], bank[r, 0:128].rearrange("p (g d) -> p g d", g=2),
                                                 ACT.Copy)
                i.then_inc(s_tpev, 1)

            for w in (6, 7, 8):
                high_w(w)
            normed_block(0, 0, 512, None)
            high_w(9)
            act.wait_ge(s_hid, 1)
            nc.scalar.activation(hidk[:, :, :], ps[6][:, 0:128].rearrange("p (h n) -> p h n", h=2),
                                 ACT.Gelu_apprx_tanh).then_inc(s_gelu, 1)
            high_w(10)
            high_w(11)
            act.wait_ge(s_gq, 1)
            for n in range(4):
                evac_tp(n)
            high_w(12)
            normed_block(1, 1, 256, VB)
            high_w(13)
            evac_tp(4)
            act.wait_ge(s_kcp, 1)
            kc_ps = ps[7][0:NC, 0:128].rearrange("p (g d) -> p g d", g=2)
            nc.scalar.activation(kcn[:, :, :], kc_ps, ACT.Copy)
            nc.scalar.activation(kcq[:, :, :], kc_ps, ACT.Square).then_inc(s_kce, 1)
            act.wait_ge(s_kcr, 1)
            nc.scalar.activation(kcs[:, 1, :], kcs[:, 0, :], ACT.Sqrt, bias=eps[0:NC, :], scale=1.0 / DH
                                 ).then_inc(s_kcst, 1)
            act.wait_ge(s_glp, 1)
            act.wait_ge(s_R, 4)
            nc.scalar.activation(glT[:, :], ps[6][0:24, :], ACT.Copy).then_inc(s_glT, 1)
            high_w(14)
            act.wait_ge(s_gltp, 1)
            nc.scalar.activation(G[:, :, :], ps[6][:, 0:96].rearrange("p (t c) -> p c t", t=T),
                                 ACT.Sigmoid).then_inc(s_sig, 1)
            for w in (15, 16):
                high_w(w)
                evac_tp(2 * w - 25)
                evac_tp(2 * w - 24)
            normed_block(2, 2, 512, None)
            high_w(17)
            act.wait_ge(s_kctp, 1)
            act.wait_ge(s_kcz, 1)
            for g in range(2):
                h = slice(64 * g, 64 * g + 64)
                nc.scalar.activation(kcT[h, g, :], ps[7][h, 256:288], ACT.Copy,
                                     scale=par[h, C_GAIN + G_KCMP:C_GAIN + G_KCMP + 1]).then_inc(s_kcT, 1)
            act.wait_ge(s_hid, 2)
            nc.scalar.activation(hidv[:, :, :, :, :].rearrange("p h g t n -> p (h g) t n"),
                                 view(ps[6][:, 0:128], [[NC, 4], [0, T], [1, NC]]),
                                 ACT.Gelu_apprx_tanh).then_inc(s_gelu, 1)
            for w in (18, 19, 20):
                high_w(w)
                evac_tp(2 * w - 27)
                evac_tp(2 * w - 26)
            act.wait_ge(s_cm, 1)
            nc.scalar.activation(cm[:, :, :], cm[:, :, :], ACT.Exp).then_inc(s_cex, 1)
            normed_block(3, 3, 512, None)
            high_w(21)
            evac_tp(15)
            for w in (22, 23, 24):
                high_w(w)
                evac_tp(2 * w - 28)
                evac_tp(2 * w - 27)
            for t in range(T):
                evac(4, t)
                nc.scalar.activation(VA[:, t, :], ps[t][:, :], ACT.Copy).then_inc(s_ev, 1)
            act.wait_ge(s_ach, 2 * 32)
            qk_high(0)
            evac_tp(22)
            qk_high(1)

            for p in range(4):
                act.wait_ge(s_mct, p + 1)
                nc.scalar.activation(mf[:, 4 + p, :], ps[4 + p][:, :], ACT.Copy).then_inc(s_mcte, 1)

            def k_high_nsa():
                for br in range(2):
                    high_part(KT, 4 + br, N_KP + 2 * br)

            def q_high_nsa(r, staged):
                for a in range(2):
                    act.wait_ge(s_stg[a], staged)
                act.sem_inc(s_begun)
                high_part(QT, r + 4, N_QP)

            def v_high(a, V, col):
                nc.scalar.activation(VS[:, a, :, 0:DH], V[:, :, bass.ds(col, DH)], ACT.Copy).then_inc(s_vh, 1)

            def exp(H, a, tiles):
                for t in tiles:
                    act.wait_ge(s_L, 4 * H + (t + 1))
                    l_ = L[:, a, L_AT[t]:L_AT[t] + P * (t + 1)]
                    c_ = 4 * a + t
                    nc.scalar.activation(l_, l_, ACT.Exp, bias=nmx[:, c_:c_ + 1], scale=-1.0,
                                         accum_out=sums[:, c_:c_ + 1]).then_inc(s_E, 1)

            def mix_high(kk):
                nc.scalar.activation(mhi[:, kk, :], mf[:, kk, :], ACT.Copy).then_inc(s_mhi, 1)

            def move(H, a, out):
                act.wait_ge(s_PV, H + 2)
                act.wait_ge(s_cb, out + 1)
                o_ = slice(64 - 64 * a, 128 - 64 * a)
                nc.scalar.activation(tmp[64 * a:64 * a + 64, :], ps[6 + a][o_, :], ACT.Copy).then_inc(s_tmp, 1)

            def half(H, a, v_next, prev=None, scores=True):
                act.wait_ge(s_PV, H + 1)
                for t in range(T):
                    act.wait_ge(s_T, 4 * H + (t + 1))
                    nc.scalar.activation(PThi[:, 0:t + 1, P * t:P * t + P],
                                         ps[4 + t % 2][:, 0:P * (t + 1)].rearrange("p (j q) -> p j q", q=P),
                                         ACT.Copy).then_inc(s_Phi, 1)
                    if t == 1 and v_next is not None:
                        exp(H + 1, 1 - a, (3,))
                if v_next is not None:
                    v_high(1 - a, *v_next)
                if prev is not None:
                    move(H - 1, 1 - a, prev)
                if scores:
                    exp(H + 2, a, (0, 1, 2))

            act.wait_ge(s_mcte, 4)
            v_high(0, VA, 0)
            exp(0, 0, range(T))
            exp(1, 1, (0, 1, 2))
            high_w(25)
            for u in range(N_A):
                half(2 * u, 0, (VA, 128 * u + 64), prev=2 * u - 1 if u else None)
                if u < 2:
                    qk_high(u + 2)
                elif u == 2:
                    q_high_nsa(0, STG * (N_A - 1))
                half(2 * u + 1, 1, (VA, 128 * u + 128) if u < 3 else (VB, 0), prev=2 * u)
                if u == 1:
                    k_high_nsa()
            with act.Fori(0, 3) as i:
                for br in range(2):
                    half(4 * i + (2 * N_A + 2 * br), 0, (VB, 128 * br + 64),
                         prev=None if br else 2 * i + (2 * N_A - 1))
                    if br == 0:
                        q_high_nsa(i + 1, STGN * i + (STG * N_A + STGN))
                    half(4 * i + (2 * N_A + 2 * br + 1), 1, (VB, 128 - 128 * br), prev=2 * i + 2 * N_A if br else None)
            for br in range(2):
                for a in range(2):
                    half(2 * N_A + 12 + 2 * br + a, a, (VB, (128 * br + 64) if a == 0 else 128) if br + a < 2 else None,
                         prev={(0, 0): 2 * N_A + 5, (1, 1): 2 * N_A + 6}.get((br, a)), scores=br == 0)
                    if br == 1 and a == 0:
                        act.wait_ge(s_S, 8 * (N_A + 8))
                        act.wait_ge(s_cb, 2 * N_A + 2)
                        mix_high(0)
                        mix_high(1)
            move(2 * N_A + 15, 1, 2 * N_A + 7)

            for kk in range(2, KD):
                act.wait_ge(s_cb, 2 * kk + 4)
                mix_high(kk)
            def x1_square(q):
                c_ = slice(512 * (q // T), 512 * (q // T) + 512)
                act.wait_ge(s_x1, q + 1)
                nc.scalar.activation(xn2[:, q % T, c_], x1[:, q % T, c_], ACT.Square,
                                     accum_out=xss2[:, q:q + 1]).then_inc(s_x1sq, 1)

            for w in range(26, 33):
                high_w(w)
                if w >= 30:
                    for q in ((0, 1), (2,), (3,))[w - 30]:
                        x1_square(q)
            act.wait_ge(s_x2s, 1)
            for t in range(T):
                x1_square(T + t)
                act.wait_ge(s_x1sq, T + t + 1)
                nc.scalar.activation(xst[:, t:t + 1], xss2[:, T + t:T + t + 1], ACT.Sqrt,
                                     bias=xss2[:, 2 * T + t:2 * T + t + 1], scale=1.0 / D).then_inc(s_x2st, 1)
            high_w(33)
            act.wait_ge(s_modf, 1)
            for kk in range(KD):
                h_chunk(kk, hf2, af[:, kk:kk + 1], modfb[:, kk:kk + 1], s_h2tp, s_hf2, s_h2lo, 0, ps[4:8])

            with act.Fori(0, NF // 2) as i:
                for jj in range(2):
                    for r in range(2):
                        w0 = W_GU + 4 + 2 * jj + r
                        act.wait_ge(s_mm, 4 * i + (w0 - 3))
                        high(None, SLOT[w0], 16 * i + raw_count(w0))
                    act.wait_ge(s_mm, 4 * i + (W_GU + 2 * jj + 2))
                    act.wait_ge(s_prod, 2 * i + (jj + 1))
                    nc.scalar.activation(sil[:, jj, :], ps[2 * jj][:, :], ACT.Silu).then_inc(s_sil, 1)
            with act.Fori(0, 4) as i:
                for r in range(4):
                    w0 = W_DN + 4 + r
                    act.wait_ge(s_mm, 4 * i + (w0 - 3))
                    high(None, SLOT[w0], 16 * i + raw_count(w0))
            for w in range(W_DN + 20, N_W):
                high_w(w)
            for dt in range(4, KD):
                act.wait_ge(s_dn, dt + 1)
                nc.scalar.activation(yT[:, dt, :], ps[dt][:, :], ACT.Copy, scale=modfb[:, 16 + dt:17 + dt]
                                     ).then_inc(s_yT, 1)

        @block.vector
        def _(dve):
            chain = [0]

            def link(ins):
                chain[0] += 1
                ins.then_inc(s_dch, 1)
                dve.wait_ge(s_dch, chain[0])

            dve.wait_ge(s_par, 16)
            nc.vector.tensor_scalar(gq[:, 0:1], par[:, C_GAIN + G_QB:C_GAIN + G_QB + 1], SCALE, None, ALU.mult)
            nc.vector.tensor_scalar(gq[:, 1:2], par[:, C_GAIN + G_QA:C_GAIN + G_QA + 1], SCALE, None, ALU.mult
                                    ).then_inc(s_gq, 1)
            def split(kk, hbuf, hi_t, lo_t, hfs, his, los):
                dve.wait_ge(hfs, kk + 1)
                nc.vector.tensor_copy(hi_t[:, kk, :], hbuf[:, kk % 2, :]).then_inc(his, 1)
                dve.wait_ge(his, kk + 1)
                nc.vector.tensor_tensor(lo_t[:, kk, :], hbuf[:, kk % 2, :], hi_t[:, kk, :].bitcast(F32),
                                        ALU.subtract).then_inc(los, 1)

            echain = [0]

            def early(e):
                j, cp = divmod(e, 4)
                dve.wait_ge(s_raw[e % 4], 16 * (e // 4 + 1))
                a_ = eacc[j]
                for c in range(2):
                    w_ = raw[:, e % 4, 512 * c:512 * c + 512]
                    s_ = silc[:, 2 * cp + c:2 * cp + c + 1]
                    if cp == 0 and c == 0:
                        i = nc.vector.tensor_scalar(a_, w_, s_, None, ALU.mult)
                    else:
                        dve.wait_ge(s_each, echain[0])
                        i = nc.vector.scalar_tensor_tensor(a_, w_, s_, a_, ALU.mult, ALU.add)
                    echain[0] += 1
                    i.then_inc(s_each, 1)

            def modulation(hf_):
                dve.wait_ge(s_adamm, hf_ + 1)
                k4 = slice(4 * hf_, 4 * hf_ + 4)
                link(nc.vector.tensor_tensor(modm[:, k4, :], ps[6 + hf_][:, 0:8].rearrange("p (k g) -> p k g", g=2),
                                             par[:, C_BM + 8 * hf_:C_BM + 8 * hf_ + 8]
                                             .rearrange("p (k g) -> p k g", g=2), ALU.add))
                nc.vector.scalar_tensor_tensor(am[:, k4], modm[:, k4, 0:1].rearrange("p k o -> p (k o)"), 1.0,
                                               par[:, C_GM + 4 * hf_:C_GM + 4 * hf_ + 4], ALU.add, ALU.mult
                                               ).then_inc(s_mod, 1)

            dve.wait_ge(s_silc, 1)
            for e in range(11):
                early(e)
                if e == 6:
                    dve.wait_ge(s_xst, 1)
                    nc.vector.reciprocal(xrs[:, :], xst[:, :]).then_inc(s_xrs, 1)
            modulation(0)
            for e in range(11, N_EARLY):
                early(e)
            modulation(1)
            for kk in range(4, KD):
                dve.wait_ge(s_hhi, kk + 1)
                nc.vector.tensor_tensor(h1lo[:, kk, :], hf[:, kk % 2, :], h1hi[:, kk, :].bitcast(F32),
                                        ALU.subtract).then_inc(s_hlo2, 1)
            dve.wait_ge(s_glh, 1)
            nc.vector.tensor_tensor(gll[:, :, :], glr[:, :, :], glh[:, :, :].bitcast(F32), ALU.subtract
                                    ).then_inc(s_gll, 1)

            achain = [0]

            def late(k):
                j, cp = divmod(k, 4)
                dve.wait_ge(s_r2[k % 4], 16 * (k // 4 + 1))
                a_ = acc[j]
                for c in range(2):
                    w_ = ring2[:, k % 4, 512 * c:512 * c + 512]
                    s_ = silc[:, 2 * cp + c:2 * cp + c + 1]
                    if cp == 0 and c == 0:
                        i = nc.vector.tensor_scalar(a_, w_, s_, None, ALU.mult)
                    else:
                        dve.wait_ge(s_ach, achain[0])
                        i = nc.vector.scalar_tensor_tensor(a_, w_, s_, a_, ALU.mult, ALU.add)
                    achain[0] += 1
                    i.then_inc(s_ach, 1)
                if cp == 3 and j < 2:
                    dve.wait_ge(s_ach, achain[0])
                    dve.wait_ge(s_brow, 16)
                    nc.vector.tensor_tensor(a_[0:1, :], a_[0:1, :], brow_s[0:1, 512 * j:512 * j + 512], ALU.add
                                            ).then_inc(s_offs, 1)

            def norm_block(b, h):
                for t in range(T):
                    q = 4 * b + t
                    dve.wait_ge(s_ev, {0: 0, 1: 4, 2: 8, 3: 12}[b] + t + 1)
                    nc.vector.tensor_reduce(ssb[:, b, t * h:t * h + h],
                                            sq[:, q % 2, 0:64 * h].rearrange("p (h d) -> p h d", d=DH), AXX, ALU.add
                                            ).then_inc(s_ssr, 1)
                dve.wait_ge(s_std, b + 1)
                link(nc.vector.reciprocal(rsb[:, b, 0:T * h], stb[:, b, 0:T * h]))
                v = nat[:, b % 2, :, 0:64 * h].rearrange("p t (h d) -> p t h d", d=DH)
                nc.vector.tensor_tensor(v, v, view(rsb[:, b, 0:1], [[h, T], [1, h], [0, DH]]), ALU.mult
                                        ).then_inc(s_nrm, 1)

            def lates(a, b):
                for k in range(a, b):
                    late(k)

            lates(0, 6)
            norm_block(0, 8)
            lates(6, 14)
            norm_block(1, 4)
            dve.wait_ge(s_kce, 1)
            nc.vector.tensor_reduce(kcs[:, 0, :], kcq[:, :, :], AXX, ALU.add).then_inc(s_kcr, 1)
            dve.wait_ge(s_kcst, 1)
            link(nc.vector.reciprocal(kcs[:, 2, :], kcs[:, 1, :]))
            nc.vector.tensor_tensor(kcn[:, :, :], kcn[:, :, :], view(kcs[:, 2, 0:1], [[1, 2], [0, DH]]), ALU.mult
                                    ).then_inc(s_kcn, 1)
            lates(14, 22)
            norm_block(2, 8)
            dve.wait_ge(s_sig, 1)
            dve.wait_ge(s_shp, 16)
            link(nc.vector.tensor_tensor(gv[:, :, :], G[:, 0:8, :],
                                         view(shp[:, S_VALID:S_VALID + 1], [[0, 8], [1, T]]), ALU.mult))
            lates(22, 30)
            dve.wait_ge(s_csc, 2)
            mask = view(shp[:, S_MASK:S_MASK + 1], [[NC, T], [0, 2], [1, NC]])
            for p in range(4):
                i = nc.vector.tensor_tensor(view(cm[:, 4 * p:4 * p + 1, :], [[NC, T], [16 * NC, 2], [1, NC]]),
                                            view(ps[6 + p // 2][:, 256 * (p % 2):256 * (p % 2) + 1],
                                                 [[2 * NC, T], [NC, 2], [1, NC]]), mask, ALU.add)
            link(i)
            link(nc.vector.tensor_reduce(cst[:, 0, :], cm[:, :, :], AXX, ALU.max))
            nc.vector.tensor_tensor(cm[:, :, :], cm[:, :, :], view(cst[:, 0, 0:1], [[1, 32], [0, NC]]),
                                    ALU.subtract).then_inc(s_cm, 1)
            dve.wait_ge(s_cex, 1)
            link(nc.vector.tensor_reduce(cst[:, 1, :], cm[:, :, :], AXX, ALU.add))
            link(nc.vector.reciprocal(cst[:, 2, :], cst[:, 1, :]))
            link(nc.vector.tensor_tensor(cst[:, 3, :].rearrange("p (a q t) -> p a q t", a=2, t=T),
                                         cst[:, 2, :].rearrange("p (a q t) -> p a q t", a=2, t=T),
                                         view(gv[:, 0:1, 0:1], [[T, 2], [2 * T, 4], [1, T]]), ALU.mult))
            dve.wait_ge(s_cpt, 2)
            for b in range(2):
                nc.vector.tensor_copy(PcT[:, 4 * b:4 * b + 4, :].rearrange("p r q -> p (r q)"), ps[6 + b][:, :]
                                      ).then_inc(s_cpte, 1)
            norm_block(3, 8)
            lates(30, 32)
            for p in range(4):
                dve.wait_ge(s_pvc, p + 1)
                nc.vector.tensor_tensor(
                    mixc[:, :, 128 * p:128 * p + 128].rearrange("p t (a d) -> p a t d", a=2),
                    ps[6 + p % 2][:, :].rearrange("p (a t d) -> p a t d", a=2, t=T),
                    view(cst[:, 3, 4 * p:4 * p + 1], [[16, 2], [1, T], [0, DH]]), ALU.mult).then_inc(s_mixc, 1)

            def logits(H, a, staged, tiles=range(T), first=False):
                dve.wait_ge(s_stg[a], staged)
                for t in tiles:
                    w = P * (t + 1)
                    dve.wait_ge(s_S, 4 * H + (t + 1))
                    if not first:
                        dve.wait_ge(s_T, 4 * H + (t - 7))
                    dve.sem_inc(s_begun)
                    b_ = bias[:, a, 0:w][:, ::-1]
                    nc.vector.tensor_tensor_reduce(out=L[:, a, L_AT[t]:L_AT[t] + w], in0=ps[t][:, 0:w], in1=b_,
                                                   scale=-1.0, scalar=3e38, op0=ALU.add, op1=ALU.min,
                                                   accum_out=nmx[:, 4 * a + t:4 * a + t + 1]).then_inc(s_L, 1)

            def factors(H, a, gate):
                dve.wait_ge(s_E, 4 * H + 4)
                dve.sem_inc(s_begun)
                if isinstance(gate, str):
                    nc.vector.reciprocal(rg[:, a, :], sums[:, 4 * a:4 * a + 4]).then_inc(s_rg, 1)
                else:
                    nc.vector.reciprocal(rec[:, a, :], sums[:, 4 * a:4 * a + 4]).then_inc(s_rch, 1)
                    dve.wait_ge(s_rch, H - (2 * N_A - 1))
                    nc.vector.tensor_tensor(rg[:, a, :], rec[:, a, :],
                                            G[:, bass.ds(gate, 1), :].rearrange("p o t -> p (o t)"), ALU.mult
                                            ).then_inc(s_rg, 1)

            def mix_low(kk):
                dve.wait_ge(s_mhi, kk + 1)
                nc.vector.tensor_tensor(mlo[:, kk, :], mf[:, kk, :], mhi[:, kk, :].bitcast(F32), ALU.subtract
                                        ).then_inc(s_mlo, 1)

            def add_up(H, a, out, pair, onto=True):
                h = slice(64 * a, 64 * a + 64)
                m = mf[h, bass.ds(pair, 1), :].rearrange("p o n -> p (o n)")
                dve.wait_ge(s_tmp, out + 1)
                dve.wait_ge(s_PV, H + 2)
                dve.sem_inc(s_begun)
                if onto:
                    nc.vector.tensor_tensor(m, ps[6 + a][h, :], m, ALU.add).then_inc(s_own, 1)
                    dve.wait_ge(s_own, out - (2 * N_A - 2))
                    nc.vector.tensor_tensor(m, tmp[h, :], m, ALU.add).then_inc(s_cb, 1)
                else:
                    nc.vector.tensor_tensor(m, ps[6 + a][h, :], tmp[h, :], ALU.add).then_inc(s_cb, 1)

            def half(H, a, gate, staged=None, prev=None):
                for t in range(T):
                    dve.wait_ge(s_Phi, 4 * H + (t + 1))
                    hi = PThi[:, 0:t + 1, P * t:P * t + P].bitcast(F32)
                    nc.vector.tensor_tensor(PTlo[:, 0:t + 1, P * t:P * t + P],
                                            ps[4 + t % 2][:, 0:P * (t + 1)].rearrange("p (j q) -> p j q", q=P),
                                            hi, ALU.subtract).then_inc(s_Plo, 1)
                    if t == 1 and staged is not None:
                        logits(H + 2, a, staged, (0, 1))
                    if t == 1 and gate is not None:
                        factors(H + 1, 1 - a, gate)
                if staged is not None:
                    logits(H + 2, a, staged, (2, 3))
                if prev is not None:
                    add_up(H - 1, 1 - a, *prev)

            MOBA = "no gate"
            dve.wait_ge(s_mixc, 4)
            nc.vector.memset(nmx[:, :], 0.0).then_inc(s_cb, 2)
            nc.vector.memset(rec[:, :, :], 0.0).then_inc(s_Plo, 2)
            nc.vector.memset(rg[:, :, :], 0.0).then_inc(s_PV, 1)
            dve.wait_ge(s_cb, 2)
            dve.wait_ge(s_Plo, 2)
            dve.wait_ge(s_PV, 1)
            logits(0, 0, STG, first=True)
            factors(0, 0, MOBA)
            logits(1, 1, STG, first=True)
            dve.wait_ge(s_mcte, 4)
            nc.vector.memset(mf[64:128, N_A - 1, :], 0.0).then_inc(s_mfz, 1)
            dve.wait_ge(s_mfz, 1)
            for u in range(N_A):
                staged = STG * (u + 2) if u < 3 else STG * N_A + STGN
                half(2 * u, 0, MOBA, staged, (2 * u - 1, u - 1, False) if u else None)
                half(2 * u + 1, 1, MOBA if u < 3 else 8, staged, (2 * u, u, False))
            with dve.Fori(0, 3) as i:
                for br in range(2):
                    staged = STGN * i + (STG * N_A + STGN * (1 + br))
                    half(4 * i + (2 * N_A + 2 * br), 0, 2 * i + (9 + 8 * br), staged,
                         None if br else (2 * i + (2 * N_A - 1), i + 3))
                    half(4 * i + (2 * N_A + 2 * br + 1), 1, 2 * i + (16 - 6 * br), staged,
                         (2 * i + 2 * N_A, i + 4) if br else None)
            for br in range(2):
                for a in range(2):
                    half(2 * N_A + 12 + 2 * br + a, a, ((15, 22), (23, None))[br][a],
                         STG * N_A + 4 * STGN if br == 0 else None,
                         {(0, 0): (2 * N_A + 5, 6), (1, 1): (2 * N_A + 6, 7)}.get((br, a)))
                    if br == 1 and a == 0:
                        mix_low(0)
                        mix_low(1)
            add_up(2 * N_A + 15, 1, 2 * N_A + 7, 7)

            for kk in range(2, KD):
                mix_low(kk)
            dve.wait_ge(s_tpev, len(TP))
            link(nc.vector.tensor_tensor(modfb[:, :], modf[:, :], par[:, C_BF:C_BF + 24], ALU.add))
            nc.vector.scalar_tensor_tensor(af[:, :], modfb[:, 8:16], 1.0, par[:, C_GF:C_GF + KD], ALU.add, ALU.mult
                                           ).then_inc(s_modf, 1)
            nc.vector.memset(xss[:, 0:1], 0.0).then_inc(s_prod, 2)
            nc.vector.memset(xss[:, 1:2], 0.0).then_inc(s_alo, 2)
            dve.wait_ge(s_x1in, 16)

            def normed_x1(t):
                dve.wait_ge(s_x2st, t + 1)
                link(nc.vector.reciprocal(xrs[:, t:t + 1], xst[:, t:t + 1]))
                nc.vector.tensor_scalar(xn2[:, t, :], x1[:, t, :], xrs[:, t:t + 1], None, ALU.mult).then_inc(s_xn2, 1)

            for h in range(2):
                for t in range(T):
                    q = T * h + t
                    c_ = slice(512 * h, 512 * h + 512)
                    if t < T - 1:
                        dve.wait_ge(s_op, 3 * h + t + 1)
                    else:
                        dve.wait_ge(s_mm, W_OUT + 4 * h + 4)
                    if q >= 2:
                        dve.wait_ge(s_x1, q - 1)
                    nc.vector.tensor_tensor(ob[:, q % 2, :], ps[t][:, :], gtm[:, c_], ALU.mult
                                            ).then_inc(s_ot, 1)
                    dve.wait_ge(s_ot, q + 1)
                    nc.vector.tensor_tensor(x1[:, t, c_], x1[:, t, c_], ob[:, q % 2, :], ALU.add).then_inc(s_x1, 1)
                    if h == 1 and t >= 2:
                        normed_x1(t - 2)
                if h == 0:
                    dve.wait_ge(s_x1sq, T)
                    nc.vector.tensor_scalar(xss2[:, 2 * T:3 * T], xss2[:, 0:T], 1.0 / D, EPS, ALU.mult, ALU.add
                                            ).then_inc(s_x2s, 1)
            normed_x1(T - 2)
            normed_x1(T - 1)
            for kk in range(KD):
                split(kk, hf2, mhi, mlo, s_hf2, s_h2hi, s_h2lo)

            with dve.Fori(0, NF // 2) as i:
                for jj in range(2):
                    dve.wait_ge(s_sil, 2 * i + (jj + 1))
                    dve.wait_ge(s_alo, 2 * i + (jj + 1))
                    nc.vector.tensor_tensor(actf[:, jj, :], ps[2 * jj + 1][:, :], sil[:, jj, :], ALU.mult
                                            ).then_inc(s_prod, 1)
                    dve.wait_ge(s_prod, 2 * i + (jj + 3))
                    a_ = ahi[:, bass.ds(2 * i + jj, 1), :].rearrange("p o n -> p (o n)")
                    nc.vector.tensor_copy(a_, actf[:, jj, :]).then_inc(s_ahi, 1)
                    dve.wait_ge(s_ahi, 2 * i + (jj + 1))
                    nc.vector.tensor_tensor(alo[:, bass.ds(2 * i + jj, 1), :].rearrange("p o n -> p (o n)"),
                                            actf[:, jj, :], a_.bitcast(F32), ALU.subtract).then_inc(s_alo, 1)
            for dt in range(4):
                dve.wait_ge(s_dn, dt + 1)
                nc.vector.tensor_scalar(yT[:, dt, :], ps[dt][:, :], modfb[:, 16 + dt:17 + dt], None, ALU.mult
                                        ).then_inc(s_yT0, 1)
            for h in range(2):
                for t in range(T):
                    dve.wait_ge(s_ytp, 4 * h + t + 1)
                    nc.vector.tensor_tensor(yo[:, t, 512 * h:512 * h + 512], ps[4 * h + t][:, :],
                                            x1[:, t, 512 * h:512 * h + 512], ALU.add).then_inc(s_yo, 1)

        @block.tensor
        def _(pe):
            PASSES = ((0, 0), (0, 1), (1, 0))
            W2 = (whi, wlo)

            pe.wait_ge(s_rel, 48)
            nc.tensor.matmul(ps[6][0:16, 0:512], rel_s[:, :], oneh_s[:, 0:512], start=True, stop=True)
            nc.tensor.matmul(ps[7][0:16, 0:BV - 512], rel_s[:, :], oneh_s[:, 512:BV], start=True, stop=True
                             ).then_inc(s_bvp, 1)
            pe.wait_ge(s_shp, 16)
            pe.wait_ge(s_bvs, 2)

            def columns(hf_):
                pe.wait_ge(s_each, 16 * (hf_ + 1))
                for q in range(4):
                    for g in range(2):
                        mm = nc.tensor.matmul(ps[6 + hf_][:, 2 * q + g:2 * q + g + 1],
                                              eacc[2 * hf_ + g][:, P * q:P * q + P], ones[:, 0:1],
                                              start=True, stop=True)
                mm.then_inc(s_adamm, 1)

            columns(0)
            pe.wait_ge(s_xn, T)
            for kk in range(KD):
                if kk >= 4:
                    pe.wait_ge(s_hf, kk - 3)
                for t in range(T):
                    mm = nc.tensor.transpose(ps[kk % 4][:, P * t:P * t + P], xn[:, t, P * kk:P * kk + P], ident)
                mm.then_inc(s_htp, 1)
            columns(1)

            H1 = (h1hi, h1lo)
            for w in range(W_T, W_QB):
                pe.wait_ge((s_hlo, s_hlo2)[w], 4)
                pe.wait_ge(s_lo, w + 1)
                for kv in range(2):
                    for k4 in range(4):
                        kk = 4 * w + k4
                        for i, (s, m) in enumerate(PASSES):
                            mm = nc.tensor.matmul(ps[4 + kv][:, :],
                                                  W2[s][:, SLOT[w], 256 * k4 + P * kv:256 * k4 + P * kv + P],
                                                  H1[m][:, kk, :], start=(kk == 0 and i == 0),
                                                  stop=(kk == KD - 1 and i == 2))
                mm.then_inc(s_mm, 1)

            def natural(w0, blk, acts, banks, out_sem, ev=None, split=None, between={}, also={}, do=None):
                for r in range(4):
                    for n in between.get(r, ()):
                        tp(n)
                    for n in also.get(r, ()):
                        do(n)
                    pe.wait_ge(s_lo, w0 + r + 1)
                    if split is not None:
                        pe.wait_ge(split, 2 * r + 2)
                    for t in range(T):
                        if r == 0 and ev is not None:
                            ev(t)
                        for k2 in range(2):
                            kk = 2 * r + k2
                            for i, (s, m) in enumerate(PASSES):
                                mm = nc.tensor.matmul(banks[t][:, :], acts[s][:, kk, P * t:P * t + P],
                                                      W2[m][:, SLOT[w0 + r], 512 * k2:512 * k2 + 512],
                                                      start=(kk == 0 and i == 0), stop=(kk == KD - 1 and i == 2))
                        if r == 3 and t < T - 1:
                            mm.then_inc(out_sem, 1)
                    mm.then_inc(s_mm, 1)

            def evacuated(blk):
                def f(t):
                    if blk:
                        pe.wait_ge(s_ev, 4 * (blk - 1) + t + 1)
                return f

            def tp(n):
                kind, j = TP[n]
                bank = ps[4 + n % 2]
                if n >= 2:
                    pe.wait_ge(s_tpev, n - 1)
                else:
                    pe.wait_ge(s_kvE, 2)
                if kind in ("q", "k", "kb"):
                    half = 0 if kind == "q" else 1
                    pe.wait_ge(s_nrm, {("q", True): 1, ("kb", True): 2, ("q", False): 3, ("k", False): 4}[kind, j >= 4])
                    c = P * (j % 4)
                    for t in range(T):
                        mm = nc.tensor.transpose(bank[:, P * t:P * t + P], nat[:, half, t, c:c + P], ident)
                elif kind == "gtm":
                    pe.wait_ge(s_offs, j + 1)
                    mm = nc.tensor.matmul(bank[:, :], ones, acc[j], start=True, stop=True)
                elif kind == "col":
                    pe.wait_ge(s_ach, 8 * (j + 1))
                    for q in range(4):
                        mm = nc.tensor.matmul(bank[:, q:q + 1], acc[j][:, P * q:P * q + P], ones[:, 0:1],
                                              start=True, stop=True)
                else:
                    pe.wait_ge(s_gelu, 2)
                    for g in range(2):
                        for ht in range(2):
                            mm = nc.tensor.matmul(bank[:, DH * g:DH * g + DH],
                                                  hidv[:, ht, g, :, :].rearrange("p t n -> p (t n)"),
                                                  w2s[:, 1, ht, :], start=(ht == 0), stop=(ht == 1))
                mm.then_inc(s_tp, 1)

            def hidden(kv):
                pe.wait_ge(s_w1, 16 * (kv + 1))
                pe.wait_ge(s_R, 4)
                if kv == 1:
                    pe.wait_ge(s_sig, 1)
                for ht in range(2):
                    for c in range(CL // 2):
                        mm = nc.tensor.matmul(ps[6][:, 64 * ht:64 * ht + 64], w1s[:, c, P * ht:P * ht + P],
                                              R[:, kv, c, :, :].rearrange("p g n -> p (g n)"),
                                              start=(c == 0), stop=(c == CL // 2 - 1))
                mm.then_inc(s_hid, 1)

            natural(W_QB, 0, H1, ps, s_pj, evacuated(0))
            hidden(0)
            natural(W_KV, 1, H1, ps, s_pj, evacuated(1), between={2: (0, 1), 3: (2, 3)})
            tp(4)
            pe.wait_ge(s_gelu, 1)
            pe.wait_ge(s_w2, 16)
            for g in range(2):
                for ht in range(2):
                    mm = nc.tensor.matmul(ps[7][0:NC, DH * g:DH * g + DH], hidk[:, ht, NC * g:NC * g + NC],
                                          w2s[:, 0, ht, :], start=(ht == 0), stop=(ht == 1))
            mm.then_inc(s_kcp, 1)
            pe.wait_ge(s_gll, 1)
            for kk in range(KD):
                for i, (s, m) in enumerate(PASSES):
                    mm = nc.tensor.matmul(ps[6][0:24, :], (glh, gll)[s][:, kk, :], H1[m][:, kk, :],
                                          start=(kk == 0 and i == 0), stop=(kk == KD - 1 and i == 2))
            mm.then_inc(s_glp, 1)
            def gates(_):
                pe.wait_ge(s_glT, 1)
                for t in range(T):
                    mm = nc.tensor.transpose(ps[6][:, 24 * t:24 * t + 24], glT[:, P * t:P * t + P], ident[0:24, 0:24])
                mm.then_inc(s_gltp, 1)

            natural(W_QA, 2, H1, ps, s_pj, evacuated(2), between={2: (5, 6), 3: (7, 8)},
                    also={1: (0,)}, do=gates)
            pe.wait_ge(s_kcn, 1)
            nc.tensor.transpose(ps[7][:, 256:288], kcn[:, :, :].rearrange("p g d -> p (g d)"), ident[0:NC, 0:NC]
                                ).then_inc(s_kctp, 1)
            hidden(1)
            pe.wait_ge(s_kcT, 2)
            pe.wait_ge(s_tpev, 4)
            pe.wait_ge(s_sig, 1)
            pe.wait_ge(s_gelu, 2)
            for p in range(4):
                for t in range(T):
                    c = 2 * NC * (4 * (p % 2) + t)
                    mm = nc.tensor.matmul(ps[6 + p // 2][:, c:c + 2 * NC], QT[:, 4 + p, P * t:P * t + P],
                                          kcT[:, :, :].rearrange("p g n -> p (g n)"), start=True, stop=True)
                if p % 2:
                    mm.then_inc(s_csc, 1)
            natural(W_KA, 3, H1, ps, s_pj, evacuated(3), between={1: (9, 10), 2: (11, 12), 3: (13, 14)})
            tp(15)
            pe.wait_ge(s_cex, 1)
            for b in range(2):
                for q in range(4):
                    r = 4 * b + q
                    mm = nc.tensor.transpose(ps[6 + b][:, P * q:P * q + P],
                                             cm[:, 4 * r:4 * r + 4, :].rearrange("p t n -> p (t n)"), ident)
                mm.then_inc(s_cpt, 1)
            def compressed(p):
                pe.wait_ge(s_cpte, 2)
                if p >= 2:
                    pe.wait_ge(s_mixc, p - 1)
                for a in range(2):
                    mm = nc.tensor.matmul(ps[6 + p % 2][:, 256 * a:256 * a + 256], PcT[:, 4 * a + p, :],
                                          Vbd[:, a, :, :].rearrange("p t d -> p (t d)"), start=True, stop=True)
                mm.then_inc(s_pvc, 1)

            natural(W_VA, 4, H1, ps, s_pj, evacuated(4), between={1: (16, 17), 2: (18, 19), 3: (20, 21)},
                    also={2: (0, 1)}, do=compressed)
            tp(22)
            compressed(2)
            compressed(3)
            pe.wait_ge(s_ev, 20)
            pe.wait_ge(s_tpev, len(TP))
            pe.wait_ge(s_mixc, 4)
            for p in range(4):
                for t in range(T):
                    mm = nc.tensor.transpose(ps[4 + p][:, P * t:P * t + P], mixc[:, t, P * p:P * p + P], ident)
                mm.then_inc(s_mct, 1)

            def scores(H, a, staged, tiles=range(T), first=False, br=None):
                pe.wait_ge(s_stg[a], staged)
                for t in tiles:
                    if not first:
                        pe.wait_ge(s_L, 4 * H + (t - 3))
                    w = P * (t + 1)
                    q_ = QK[:, a, 0, P * t:P * t + P]
                    k_ = [QK[:, a, 1 + i, 0:w] if br is None else hp[:, N_KS[br] + 2 * a + i, 0:w] for i in range(2)]
                    nc.tensor.matmul(ps[t][:, 0:w], q_, k_[0], start=True, stop=False)
                    nc.tensor.matmul(ps[t][:, 0:w], q_, k_[1], start=False, stop=True).then_inc(s_S, 1)

            def half(H, a, staged=None, br=None, start=True, stop=True, done=0):
                for t in range(T):
                    pe.wait_ge(s_P, 4 * H + (t + 1))
                    pe.wait_ge(s_Plo, 4 * H + (t + 1))
                    for j in range(t + 1):
                        mm = nc.tensor.transpose(ps[4 + t % 2][:, P * j:P * j + P],
                                                 L[:, a, L_AT[t] + P * j:L_AT[t] + P * j + P], ident)
                    mm.then_inc(s_T, 1)
                    if t % 2 and staged is not None:
                        scores(H + 2, a, staged, (t - 1, t), br=br)
                pe.wait_ge(s_Plo, 4 * H + 6)
                pe.wait_ge(s_vl, H + 1)
                if start:
                    pe.wait_ge(s_cb, done + 1)
                for j in range(T):
                    for i, part in enumerate((PThi, PTlo)):
                        mm = nc.tensor.matmul(ps[6 + a][:, P * j:SEQ], VS[:, a, j, :], part[:, j, P * j:SEQ],
                                              start=start and j == 0 and i == 0,
                                              stop=stop and j == T - 1 and i == 1)
                mm.then_inc(s_PV, 1)

            scores(0, 0, STG, first=True)
            scores(1, 1, STG)
            pe.wait_ge(s_mcte, 4)
            for u in range(N_A):
                if u == 3:
                    pe.wait_ge(s_kn[0], 64)
                for a in range(2):
                    half(2 * u + a, a, STG * (u + 2) if u < 3 else STG * N_A + STGN, br=0 if u == 3 else None,
                         done=2 * u + a)
            pe.wait_ge(s_kn[1], 64)
            with pe.Fori(0, 3) as i:
                for br in range(2):
                    for a in range(2):
                        half(4 * i + (2 * N_A + 2 * br + a), a, STGN * i + (STG * N_A + STGN * (1 + br)), br=1 - br,
                             start=br == 0, stop=br == 1, done=2 * i + (2 * N_A + a))
            for br in range(2):
                for a in range(2):
                    half(2 * N_A + 12 + 2 * br + a, a, STG * N_A + 4 * STGN if br == 0 else None, br=1,
                         start=br == 0, stop=br == 1, done=2 * N_A + 6 + a)

            M1 = (mhi, mlo)
            for h in range(2):
                def ev(t, h=h):
                    if h:
                        pe.wait_ge(s_ot, t + 1)
                natural(W_OUT + 4 * h, 0, M1, ps[0:4], s_op, ev, s_mlo)

            for t in range(T):
                pe.wait_ge(s_xn2, t + 1)
                for kk in range(4):
                    mm = nc.tensor.transpose(ps[4 + kk][:, P * t:P * t + P], xn2[:, t, P * kk:P * kk + P], ident)
                    if t == T - 1:
                        mm.then_inc(s_h2tp, 1)
            for kk in range(4, KD):
                pe.wait_ge(s_hf2, kk - 3)
                for t in range(T):
                    mm = nc.tensor.transpose(ps[kk][:, P * t:P * t + P], xn2[:, t, P * kk:P * kk + P], ident)
                mm.then_inc(s_h2tp, 1)

            with pe.Fori(0, NF // 2) as i:
                for jj in range(2):
                    for r in range(2):
                        w0 = W_GU + 2 * jj + r
                        pe.wait_ge(s_lo, 4 * i + (w0 + 1))
                        pe.wait_ge(s_h2lo, 4 * r + 4)
                        if r == 0:
                            pe.wait_ge(s_prod, 2 * i + (jj + 1))
                        for gu in range(2):
                            for k4 in range(4):
                                kk = 4 * r + k4
                                for q, (s, m) in enumerate(PASSES):
                                    c = 256 * k4 + P * gu
                                    mm = nc.tensor.matmul(ps[2 * jj + gu][:, :], W2[s][:, SLOT[w0], c:c + P],
                                                          M1[m][:, kk, :], start=(kk == 0 and q == 0),
                                                          stop=(kk == KD - 1 and q == 2))
                        mm.then_inc(s_mm, 1)

            def back(h):
                pe.wait_ge((s_yT0, s_yT)[h], 4)
                for t in range(T):
                    for q in range(4):
                        dt = 4 * h + q
                        mm = nc.tensor.transpose(ps[4 * h + t][:, P * q:P * q + P], yT[:, dt, P * t:P * t + P], ident)
                    mm.then_inc(s_ytp, 1)

            def down(w, slot, k, first, last):
                pe.wait_ge(s_lo, w + 1)
                for dt in (4, 5, 6, 7, 0, 1, 2, 3) if first else range(KD):
                    if first and dt == 0:
                        pe.wait_ge(s_prod, NF + 2)
                    for q, (s, m) in enumerate(PASSES):
                        rhs = (ahi, alo)[m][:, bass.ds(k, 1), :].rearrange("p o n -> p (o n)")
                        mm = nc.tensor.matmul(ps[dt][:, :], W2[s][:, slot, P * dt:P * dt + P], rhs,
                                              start=(first and q == 0), stop=(last and q == 2))
                    if last:
                        mm.then_inc(s_dn, 1)
                        if dt == 5:
                            back(0)
                if not last:
                    mm.then_inc(s_mm, 1)

            for k in range(2):
                pe.wait_ge(s_alo, (3, NF + 2)[k])
                down(W_DN + k, SLOT[W_DN + k], k, k == 0, False)
            with pe.Fori(0, (NF - 6) // 4) as i:
                for r in range(4):
                    down(4 * i + (W_DN + 2 + r), SLOT[W_DN + 2 + r], 4 * i + (2 + r), False, False)
            for k in range(2 + (NF - 6) // 4 * 4, NF):
                down(W_DN + k, SLOT[W_DN + k], k, False, k == NF - 1)
            back(1)


def shape_constants():
    shc = np.zeros((P, 388), np.float32)
    shc[:, S_ID:S_ID + P] = np.eye(P)
    shc[:, S_ONE:S_ONE + P] = 1.0
    q = np.arange(P)[:, None, None] + P * np.arange(T)[None, :, None]
    n = np.arange(NC)[None, None, :]
    hidden = (n * CS + CL - 1 > q) | (n >= NCMP)
    shc[:, S_MASK:S_MASK + P] = np.where(hidden, NEG, 0.0).reshape(P, P)
    shc[:, S_VALID:S_VALID + T] = ~hidden.all(axis=2)
    d = np.arange(BV) - (P - 1)
    half = NB_ // 2
    big = half + (np.log(np.maximum(d, 1) / half) / math.log(MAX_DIST / half) * half).astype(np.int64)
    bucket = np.where(d < half, np.maximum(d, 0), np.minimum(big, NB_ - 1))
    oneh = np.zeros((NB_ + 1, BV), np.float32)
    oneh[bucket, np.arange(BV)] = 1.0
    oneh[NB_] = np.where(d < 0, NEG, 0.0)
    return shc, oneh


def kernel(**inputs):
    import concourse.bacc as _bacc
    from concourse.bass_utils import run_bass_kernel_spmd as _run

    a = {k: np.asarray(v) for k, v in inputs.items()}
    rows = lambda w, n: w.reshape(KD, P, n).transpose(1, 0, 2)

    w_in = rows(a["w_in"][0], a["w_in"].shape[2])
    o = np.cumsum([0, 512, 512, 512, 512] + [128] * 6 + [24])
    qa, ka, va, qb, kc, vc, ksl, vsl, kwn, vwn, gl = (w_in[:, :, o[i]:o[i + 1]] for i in range(11))
    pairs = lambda w: w.reshape(P, KD, 2, 4, DH).transpose(0, 1, 3, 2, 4).reshape(P, KD, 512)
    wst = np.empty((N_W, P, U), np.float32)

    def put(w0, blk, per):
        n = blk.shape[1] // per
        wst[w0:w0 + n] = blk.reshape(P, n, U).transpose(1, 0, 2)

    put(W_T, np.concatenate([kc, vc], 2), 4)
    put(W_QB, pairs(qb), 2)
    put(W_KV, np.concatenate([ksl, kwn, vsl, vwn], 2), 2)
    put(W_QA, qa, 2)
    put(W_KA, ka, 2)
    put(W_VA, va, 2)
    wo = a["w_out"][0]
    wo = np.concatenate([wo[:512], wo[512:].reshape(2, 4, DH, D).transpose(1, 0, 2, 3).reshape(512, D)])
    wo = rows(wo, D)
    put(W_OUT, wo[:, :, :512], 2)
    put(W_OUT + 4, wo[:, :, 512:], 2)
    gu = rows(a["w_gu"][0], 2 * FFN).reshape(P, 2, 4, 2, NF, P)
    wst[W_GU:W_DN] = gu.transpose(4, 1, 0, 2, 3, 5).reshape(2 * NF, P, U)
    wst[W_DN:] = a["w_down"][0].reshape(NF, P, U)

    ada = rows(a["w_ada"][0], 6 * D).reshape(P, KD, 6, D)
    sc_sh = np.stack([ada[:, :, 1], ada[:, :, 0]], 2).reshape(P, 4, 2, 2, 2, 512)
    ada_e = sc_sh.transpose(4, 3, 1, 0, 2, 5).reshape(N_EARLY, P, U)
    late = np.stack([ada[:, :, g] for g in (2, 3, 4, 5)], 2).reshape(P, 4, 2, 4, 2, 512)
    ada_l = late.transpose(3, 4, 1, 0, 2, 5).reshape(32, P, U)

    col = lambda v: v.reshape(KD, P).T
    b = a["b_ada"][0].reshape(6, D)
    cols = np.zeros((P, N_COLS), np.float32)
    cols[:, C_C:C_C + 8] = col(a["c"][0])
    cols[:, C_BM:C_BM + 16:2] = col(b[1])
    cols[:, C_BM + 1:C_BM + 17:2] = col(b[0])
    cols[:, C_GM:C_GM + 8] = col(a["g_mix"][0])
    cols[:, C_GF:C_GF + 8] = col(a["g_ffn"][0])
    for i, g in enumerate((3, 4, 5)):
        cols[:, C_BF + 8 * i:C_BF + 8 * i + 8] = col(b[g])
    for i, name in enumerate(("q_norm_b", "k_norm_sel", "k_norm_win", "q_norm_a", "k_norm_a", "k_norm_cmp")):
        cols[:, C_GAIN + i] = np.concatenate([a[name][0], a[name][0]])
    for i, name in enumerate(("cmp_pe_k", "cmp_pe_v")):
        cols[:, C_PE + 16 * i:C_PE + 16 * i + 16] = a[name][0].reshape(CL // 2, 2 * DH).T
    r = a["rel_bias"]
    rel = np.concatenate([r[:, :8], r[:, 8:].reshape(NB_, 2, 4).transpose(0, 2, 1).reshape(NB_, 8)], 1)
    wgl = gl.reshape(P, KD, 2, 4, 3).transpose(0, 1, 4, 3, 2).reshape(P, KD, 24)
    w1 = np.stack([a[n][0].reshape(CL // 2, P, 256).transpose(1, 0, 2) for n in ("cmp_w1_k", "cmp_w1_v")])
    w2 = np.stack([a[n][0].reshape(2, P, DH).transpose(1, 0, 2) for n in ("cmp_w2_k", "cmp_w2_v")], 1)
    shc, oneh = shape_constants()

    nc = _bacc.Bacc("TRN2", target_bir_lowering=False, num_devices=1)
    arrays, args = {}, []
    for name, v in (("wst", wst), ("ada_e", ada_e), ("ada_l", ada_l), ("x", a["x"]), ("cols", cols), ("shc", shc),
                    ("oneh", oneh), ("rel", rel), ("brow", b[2:3]), ("wgl", wgl), ("w1", w1), ("w2", w2)):
        arrays[name + "_dram"] = v = np.ascontiguousarray(v)
        args.append(nc.dram_tensor(name + "_dram", v.shape, mybir.dt.from_np(v.dtype), kind="ExternalInput").ap())
    out = nc.dram_tensor("out_dram", (1, SEQ, D), F32, kind="ExternalOutput").ap()
    layer(nc, *args, out)
    res = _run(nc, [arrays], core_ids=[0])
    return res.results[0]["out_dram"]
```
